# Optimizing a Trainium2 kernel written in Bass

```python
import math
import jax, jax.numpy as jnp
from jax import lax
import numpy as np

D_MODEL = 1024
BATCH = 1
SEQ = 512
DEPTH = 2

GRID_W = 64
CTX_LEN = 256

BRANCH_W = D_MODEL // 2
N_BRANCH = 3
M_HEADS = 4
M_DV = BRANCH_W // M_HEADS
M_DQK = M_DV // 2
M_CHUNK = 128
M_INIT = -1e30
POOL_GROUPS = 4
POOL_GC = BRANCH_W // POOL_GROUPS
POOL_WINDOWS = (2, 4, 8, 16)
NA_HEADS = 8
NA_DH = BRANCH_W // NA_HEADS
NA_KH = 8
NA_KW = 16
N_EXPERTS = 16
EXPERT_FF = D_MODEL
EC_FACTOR = 2
ROPE_BASE = 10000.0
RMS_EPS = 1e-6
N_MOD = 6
SPLIT_SIZES = (M_HEADS * M_DQK, M_HEADS * M_DQK, M_HEADS * M_DV, M_HEADS * M_DV, 4 * M_HEADS,
               POOL_GROUPS * POOL_GC, NA_HEADS * NA_DH, NA_HEADS * NA_DH, NA_HEADS * NA_DH,
               N_BRANCH * D_MODEL)
PROJ_W = sum(SPLIT_SIZES)

kernel_name = 'hybrid_mlstm_pool_natten_ecmoe_dit'

def rmsnorm(x, g):
    xf = x.astype(jnp.float32)
    y = xf * lax.rsqrt(jnp.mean(xf * xf, axis=-1, keepdims=True) + RMS_EPS)
    return (y * g.astype(jnp.float32)).astype(x.dtype)

def modulate(h, shift, scale):
    return h * (1 + scale) + shift

def rope_tables(n_tokens, dtype):
    t = jnp.arange(n_tokens)
    row = (t // GRID_W).astype(jnp.float32)
    col = (t % GRID_W).astype(jnp.float32)
    half = M_DQK // 2
    inv = ROPE_BASE ** (-jnp.arange(0, half, 2, dtype=jnp.float32) / half)
    ar = row[:, None] * inv[None, :]
    ac = col[:, None] * inv[None, :]
    return tuple(a.astype(dtype) for a in (jnp.cos(ar), jnp.sin(ar), jnp.cos(ac), jnp.sin(ac)))

def _rotate(x, cos, sin):
    x1, x2 = jnp.split(x, 2, axis=-1)
    cos = cos[:, None, :]
    sin = sin[:, None, :]
    return jnp.concatenate([x1 * cos - x2 * sin, x2 * cos + x1 * sin], axis=-1)

def rope_2d(x, tabs):
    cr, sr, cc, sc = tabs
    xr, xc = jnp.split(x, 2, axis=-1)
    return jnp.concatenate([_rotate(xr, cr, sr), _rotate(xc, cc, sc)], axis=-1)

def mlstm_scan(q, k, v, li, lf, state):
    B, T, H, _ = q.shape
    dv = v.shape[-1]
    L = M_CHUNK
    N = T // L

    def chunks(a):
        a = a.reshape((B, N, L, H) + a.shape[3:])
        return jnp.moveaxis(a, (1, 3), (0, 2))

    tril = jnp.tril(jnp.ones((L, L), dtype=bool))

    def step(carry, inp):
        C, n, m = carry
        qc, kc, vc, ic, fc = inp
        b = jnp.cumsum(fc, axis=-1)
        dmat = jnp.where(tril, b[..., :, None] - b[..., None, :] + ic[..., None, :], -jnp.inf)
        g = b + m[..., None]
        mt = jnp.maximum(g, dmat.max(-1))
        sc = jnp.einsum('bhtd,bhsd->bhts', qc, kc) * jnp.exp(dmat - mt[..., None])
        inter = jnp.exp(g - mt)
        num = inter[..., None] * jnp.einsum('bhvd,bhtd->bhtv', C, qc) + jnp.einsum('bhts,bhsv->bhtv', sc, vc)
        den = inter * jnp.einsum('bhd,bhtd->bht', n, qc) + sc.sum(-1)
        h = num / jnp.maximum(jnp.abs(den), jnp.exp(-mt))[..., None]
        bl = b[..., -1]
        w = bl[..., None] - b + ic
        m_new = jnp.maximum(bl + m, w.max(-1))
        decay = jnp.exp(bl + m - m_new)
        ws = jnp.exp(w - m_new[..., None])
        C_new = decay[..., None, None] * C + jnp.einsum('bhs,bhsv,bhsd->bhvd', ws, vc, kc)
        n_new = decay[..., None] * n + jnp.einsum('bhs,bhsd->bhd', ws, kc)
        return (C_new, n_new, m_new), h

    xs = (chunks(q), chunks(k), chunks(v), chunks(li), chunks(lf))
    state, h = lax.scan(step, state, xs)
    h = jnp.moveaxis(h, (0, 2), (1, 3)).reshape(B, T, H, dv)
    return state, h

def head_rms(h):
    return h * lax.rsqrt(jnp.mean(h * h, axis=-1, keepdims=True) + RMS_EPS)

def mlstm_branch(ctx_parts, lat_parts, gate_bias, need_ctx):
    f32 = jnp.float32
    qscale = M_DQK ** -0.5

    def prep(parts):
        q, k, v, o, gt = parts
        q = q.astype(f32) * qscale
        k = k.astype(f32)
        v = v.astype(f32)
        gt = gt.astype(f32) + gate_bias.astype(f32)
        fwd = (q, k, v, gt[..., 0, :], jax.nn.log_sigmoid(gt[..., 1, :]))
        bwd = tuple(jnp.flip(a, axis=1) for a in (q, k, v, gt[..., 2, :], jax.nn.log_sigmoid(gt[..., 3, :])))
        return fwd, bwd

    c_f, c_b = prep(ctx_parts)
    l_f, l_b = prep(lat_parts)
    B = l_f[0].shape[0]
    st0 = (jnp.zeros((B, M_HEADS, M_DV, M_DQK), f32), jnp.zeros((B, M_HEADS, M_DQK), f32),
           jnp.full((B, M_HEADS), M_INIT, f32))
    st_f, hc_f = mlstm_scan(*c_f, st0)
    _, hl_f = mlstm_scan(*l_f, st_f)
    st_b, hc_b = mlstm_scan(*c_b, st0)
    _, hl_b = mlstm_scan(*l_b, st_b)

    def finish(h_f, h_b_rev, o):
        h = head_rms(h_f + jnp.flip(h_b_rev, axis=1))
        return jax.nn.sigmoid(o) * h.reshape(o.shape).astype(o.dtype)

    out_l = finish(hl_f, hl_b, lat_parts[3])
    out_c = finish(hc_f, hc_b, ctx_parts[3]) if need_ctx else None
    return out_l, out_c

def pool_branch(u, pool_w, pool_scale):
    B, T, _ = u.shape
    uf = u.astype(jnp.float32).reshape(B, T, POOL_GROUPS, POOL_GC)
    csum = jnp.concatenate([jnp.zeros((B, 1, POOL_GROUPS, POOL_GC), jnp.float32),
                            jnp.cumsum(uf, axis=1)], axis=1)
    t = jnp.arange(T)
    outs = []
    for gi, w in enumerate(POOL_WINDOWS):
        lo = jnp.clip(t - w // 2, 0, T - 1)
        hi = jnp.clip(t - w // 2 + w - 1, 0, T - 1)
        cnt = (hi - lo + 1).astype(jnp.float32)[:, None]
        cg = csum[:, :, gi]
        mean = (cg[:, hi + 1] - cg[:, lo]) / cnt
        outs.append(jnp.einsum('btc,cd->btd', (mean - uf[:, :, gi]).astype(u.dtype), pool_w[gi]))
    return jnp.concatenate(outs, axis=-1) * pool_scale

def na_latent(q, k, v, k_ctx, v_ctx, rpb):
    B, S, H, dh = q.shape
    rows = S // GRID_W
    kh = min(NA_KH, rows)
    f32 = jnp.float32
    scale = dh ** -0.5

    def grid(a):
        return a.reshape(B, rows, GRID_W, H, dh).transpose(1, 0, 3, 2, 4)

    qg, kg, vg = grid(q), grid(k), grid(v)
    kc = k_ctx.transpose(0, 2, 1, 3)
    vc = v_ctx.transpose(0, 2, 1, 3)
    cols = jnp.arange(GRID_W)
    cs = jnp.clip(cols - NA_KW // 2, 0, GRID_W - NA_KW)
    colmask = (cols[None, :] >= cs[:, None]) & (cols[None, :] < cs[:, None] + NA_KW)
    mask = jnp.tile(colmask, (1, kh))
    dc_idx = jnp.clip(cols[None, :] - cols[:, None] + NA_KW - 1, 0, 2 * NA_KW - 2)
    n_loc = kh * GRID_W

    def row_fn(r):
        rs = jnp.clip(r - kh // 2, 0, rows - kh)
        qr = qg[r]
        kr = jnp.moveaxis(lax.dynamic_slice_in_dim(kg, rs, kh, axis=0), 0, 2).reshape(B, H, n_loc, dh)
        vr = jnp.moveaxis(lax.dynamic_slice_in_dim(vg, rs, kh, axis=0), 0, 2).reshape(B, H, n_loc, dh)
        dr_idx = rs + jnp.arange(kh) - r + NA_KH - 1
        bias = rpb[:, dr_idx][:, :, dc_idx]
        bias = bias.transpose(0, 2, 1, 3).reshape(H, GRID_W, n_loc).astype(f32)
        s_loc = jnp.einsum('bhqd,bhkd->bhqk', qr, kr, preferred_element_type=f32) * scale + bias
        s_loc = jnp.where(mask, s_loc, -jnp.inf)
        s_ctx = jnp.einsum('bhqd,bhkd->bhqk', qr, kc, preferred_element_type=f32) * scale
        p = jax.nn.softmax(jnp.concatenate([s_loc, s_ctx], axis=-1), axis=-1).astype(v.dtype)
        return (jnp.einsum('bhqk,bhkd->bhqd', p[..., :n_loc], vr)
                + jnp.einsum('bhqk,bhkd->bhqd', p[..., n_loc:], vc))

    out = lax.map(row_fn, jnp.arange(rows))
    return out.transpose(1, 0, 3, 2, 4).reshape(B, S, H * dh)

def na_context(q, k, v):
    B, T, H, dh = q.shape
    s = jnp.einsum('bqhd,bkhd->bhqk', q, k, preferred_element_type=jnp.float32) * dh ** -0.5
    p = jax.nn.softmax(s, axis=-1).astype(v.dtype)
    return jnp.einsum('bhqk,bkhd->bqhd', p, v).reshape(B, T, H * dh)

def merge_branches(branches, bg, w_branch, w_out):
    D = w_out.shape[0]
    acc = None
    for bi, br in enumerate(branches):
        term = jax.nn.sigmoid(bg[..., bi * D:(bi + 1) * D]) * (br @ w_branch[bi])
        acc = term if acc is None else acc + term
    return acc @ w_out

def mixer(h_lat, h_ctx, w_in, gate_bias, pool_w, pool_scale, rpb, w_branch, w_out, tabs, need_ctx):
    split_at = [int(s) for s in np.cumsum(SPLIT_SIZES)[:-1]]

    def project(h):
        B, T, _ = h.shape
        qm, km, vm, om, gm, pu, qn, kn, vn, bg = jnp.split(h @ w_in, split_at, axis=-1)
        return (qm.reshape(B, T, M_HEADS, M_DQK), km.reshape(B, T, M_HEADS, M_DQK),
                vm.reshape(B, T, M_HEADS, M_DV), om, gm.reshape(B, T, 4, M_HEADS), pu,
                qn.reshape(B, T, NA_HEADS, NA_DH), kn.reshape(B, T, NA_HEADS, NA_DH),
                vn.reshape(B, T, NA_HEADS, NA_DH), bg)

    qm_l, km_l, vm_l, om_l, gm_l, pu_l, qn_l, kn_l, vn_l, bg_l = project(h_lat)
    qm_c, km_c, vm_c, om_c, gm_c, pu_c, qn_c, kn_c, vn_c, bg_c = project(h_ctx)
    qm_l = rope_2d(qm_l, tabs)
    km_l = rope_2d(km_l, tabs)
    m_l, m_c = mlstm_branch((qm_c, km_c, vm_c, om_c, gm_c), (qm_l, km_l, vm_l, om_l, gm_l),
                            gate_bias, need_ctx)
    p_l = pool_branch(pu_l, pool_w, pool_scale)
    n_l = na_latent(qn_l, kn_l, vn_l, kn_c, vn_c, rpb)
    y_l = merge_branches((m_l, p_l, n_l), bg_l, w_branch, w_out)
    y_c = None
    if need_ctx:
        p_c = pool_branch(pu_c, pool_w, pool_scale)
        n_c = na_context(qn_c, kn_c, vn_c)
        y_c = merge_branches((m_c, p_c, n_c), bg_c, w_branch, w_out)
    return y_l, y_c

def ec_moe(h, w_router, w_gate, w_up, w_down):
    B, T, D = h.shape
    cap = EC_FACTOR * T // N_EXPERTS
    aff = jax.nn.softmax(jnp.einsum('btd,de->bte', h, w_router, preferred_element_type=jnp.float32), axis=-1)
    gate, idx = lax.top_k(jnp.swapaxes(aff, 1, 2), cap)
    xe = jax.vmap(lambda hb, ib: hb[ib])(h, idx)
    hid = jax.nn.silu(jnp.einsum('becd,edf->becf', xe, w_gate)) * jnp.einsum('becd,edf->becf', xe, w_up)
    ye = jnp.einsum('becf,efd->becd', hid, w_down) * gate[..., None].astype(h.dtype)
    return jax.vmap(lambda ib, yb: jnp.zeros((T, D), yb.dtype).at[ib.reshape(-1)].add(yb.reshape(-1, D)))(idx, ye)

def setup_inputs(seed: int = 0) -> dict:
    key = jax.random.key(seed)
    ks = jax.random.split(key, 20)
    f32 = jnp.float32

    def nrm(k, shape, scale):
        return jax.random.normal(k, shape, f32) * scale

    D = D_MODEL
    lin = jnp.linspace(3.0, 6.0, M_HEADS, dtype=f32)
    gb_base = jnp.zeros((4, M_HEADS), f32).at[1].set(lin).at[3].set(lin)
    return {
        'x': nrm(ks[0], (BATCH, SEQ, D), 1.0),
        'c': nrm(ks[1], (BATCH, D), 1.0),
        'ctx': nrm(ks[2], (BATCH, CTX_LEN, D), 1.0),
        'c_ctx': nrm(ks[3], (D,), 1.0),
        'norm_gain': 1.0 + nrm(ks[4], (DEPTH, 4, D), 0.05),
        'ada_w': nrm(ks[5], (DEPTH, D, N_MOD * D), 0.5 * D ** -0.5),
        'ada_b': nrm(ks[6], (DEPTH, N_MOD * D), 0.02),
        'w_in': nrm(ks[7], (DEPTH, D, PROJ_W), D ** -0.5),
        'mlstm_gate_bias': gb_base[None] + nrm(ks[8], (DEPTH, 4, M_HEADS), 0.1),
        'pool_w': nrm(ks[9], (DEPTH, POOL_GROUPS, POOL_GC, POOL_GC), POOL_GC ** -0.5),
        'pool_scale': 1.0 + nrm(ks[10], (DEPTH, BRANCH_W), 0.1),
        'na_rpb': nrm(ks[11], (DEPTH, NA_HEADS, 2 * NA_KH - 1, 2 * NA_KW - 1), 0.1),
        'w_branch': nrm(ks[12], (DEPTH, N_BRANCH, BRANCH_W, D), BRANCH_W ** -0.5),
        'w_out': nrm(ks[13], (DEPTH, D, D), D ** -0.5),
        'router_w': nrm(ks[14], (DEPTH, D, N_EXPERTS), D ** -0.5),
        'w_gate': nrm(ks[15], (DEPTH, N_EXPERTS, D, EXPERT_FF), D ** -0.5),
        'w_up': nrm(ks[16], (DEPTH, N_EXPERTS, D, EXPERT_FF), D ** -0.5),
        'w_down': nrm(ks[17], (DEPTH, N_EXPERTS, EXPERT_FF, D), EXPERT_FF ** -0.5),
    }

def reference(x, c, ctx, c_ctx, norm_gain, ada_w, ada_b, w_in, mlstm_gate_bias, pool_w, pool_scale,
              na_rpb, w_branch, w_out, router_w, w_gate, w_up, w_down):
    S = x.shape[1]
    tabs = rope_tables(S, x.dtype)
    for l in range(DEPTH):
        need_ctx = l < DEPTH - 1
        g = norm_gain[l]
        mod_l = jnp.split((jax.nn.silu(c) @ ada_w[l] + ada_b[l])[:, None, :], N_MOD, axis=-1)
        mod_c = jnp.split(jax.nn.silu(c_ctx) @ ada_w[l] + ada_b[l], N_MOD, axis=-1)
        h_l = modulate(rmsnorm(x, g[0]), mod_l[0], mod_l[1])
        h_c = modulate(rmsnorm(ctx, g[0]), mod_c[0], mod_c[1])
        y_l, y_c = mixer(h_l, h_c, w_in[l], mlstm_gate_bias[l], pool_w[l], pool_scale[l], na_rpb[l],
                         w_branch[l], w_out[l], tabs, need_ctx)
        x = x + mod_l[2] * rmsnorm(y_l, g[1])
        h2 = modulate(rmsnorm(x, g[2]), mod_l[3], mod_l[4])
        x = x + mod_l[5] * rmsnorm(ec_moe(h2, router_w[l], w_gate[l], w_up[l], w_down[l]), g[3])
        if need_ctx:
            ctx = ctx + mod_c[2] * rmsnorm(y_c, g[1])
            h2c = modulate(rmsnorm(ctx, g[2]), mod_c[3], mod_c[4])
            ctx = ctx + mod_c[5] * rmsnorm(ec_moe(h2c, router_w[l], w_gate[l], w_up[l], w_down[l]), g[3])
    return x


_drawn_inputs = setup_inputs


def setup_inputs(seed=0):
    import zlib

    import numpy as np

    out = dict(_drawn_inputs(seed))
    spreads = {}
    factors = {'na_rpb': 3.789}
    for name, (base, spread) in spreads.items():
        noise = np.random.default_rng([zlib.crc32(name.encode()), seed]).standard_normal(out[name].shape)
        drawn = base * np.exp(spread * noise) if base else spread * noise
        out[name] = __import__('jax').numpy.asarray(drawn.astype(out[name].dtype))
    for name, factor in factors.items():
        out[name] = (out[name] * factor).astype(out[name].dtype)
    return out
```

```python
import concourse.bass as bass
from concourse import mybir
from contextlib import ExitStack

F32 = mybir.dt.float32
U32 = mybir.dt.uint32
ALU = mybir.AluOpType
ACT = mybir.ActivationFunctionType
AX = mybir.AxisListType

D, S, CTX, DEPTH = 1024, 512, 256, 2
TOK = S + CTX
P = 128
KD = D // P
LT, CT = S // P, CTX // P
NT = LT + CT
BW = D // 2
KB = BW // P
MH, DV, DK = 4, 128, 64
NH, DH = 8, 64
GW, ROWS = 64, 8
NB, QC, KC = 4, 16, 32
KSTART = [0, 8, 24, 32]
WINDOWS = (2, 4, 8, 16)
NE, FF = 16, 1024
EPS = 1e-6
C_QK, C_V, C_O, C_G, C_PU, C_QN, C_KN, C_VN, C_BG = 0, 512, 1024, 1536, 1552, 2064, 2576, 3088, 3600
NEG = -1.0e30
PADW = 8 + S + 8 + CTX + 8
RPW = 64
LCOL, CCOL = 8, 8 + S + 8

CI, CU, CL, CMF, CMB, CNM, CED, CCOS, CSIN = 0, 128, 256, 384, 512, 640, 768, 832, 1088
CW = 1344


def constants():
    import numpy as np
    t = np.zeros((P, CW), np.float32)
    i = np.arange(P)
    t[:, CI:CI + P] = np.eye(P)
    t[:, CU:CU + P] = i[:, None] <= i[None, :]
    t[:, CL:CL + P] = i[:, None] >= i[None, :]
    t[:, CMF:CMF + P] = np.where(i[None, :] <= i[:, None], 0, NEG)
    t[:, CMB:CMB + P] = np.where(i[None, :] >= i[:, None], 0, NEG)
    for b in range(NB):
        qc = QC * b + QC - 1 - i % QC
        cs = np.clip(qc - 8, 0, GW - 16)
        kc = KSTART[b] + np.arange(KC)
        ok = (kc[None] >= cs[:, None]) & (kc[None] < cs[:, None] + 16)
        t[:, CNM + b * KC:CNM + (b + 1) * KC] = np.where(ok, 0, NEG)
    for g, w in enumerate(WINDOWS):
        for side, tt in enumerate((np.arange(8), np.arange(CTX - 8, CTX))):
            lo = np.clip(tt - w // 2, 0, CTX - 1)
            hi = np.clip(tt - w // 2 + w - 1, 0, CTX - 1)
            t[:, CED + g * 16 + side * 8:CED + g * 16 + side * 8 + 8] = w / (hi - lo + 1).astype(np.float32)
    half = DK // 2
    inv = (10000.0 ** (-np.arange(0, half, 2, dtype=np.float32) / half)).astype(np.float32)
    for lt in range(LT):
        tk = lt * P + i
        for part, pos in enumerate((tk // GW, tk % GW)):
            a = pos[:, None].astype(np.float32) * inv[None]
            c, s = np.cos(a), np.sin(a)
            o = lt * DK + part * 32
            t[:, CCOS + o:CCOS + o + 32] = np.concatenate([c, c], 1)
            t[:, CSIN + o:CSIN + o + 32] = np.concatenate([-s, s], 1)
    return t


def build(nc, A, out):
    ctx = ExitStack()
    with ctx:
        def sb(name, width, dt=F32, parts=P):
            return ctx.enter_context(nc.sbuf_tensor(name, [parts, width], dt))

        made = {}

        def sem(name):
            if name not in made:
                made[name] = ctx.enter_context(nc.semaphore(name))
            return made[name]

        def dram(name, shape):
            return nc.dram_tensor(name, shape, F32, kind="Internal").ap()

        SLOT = KD * 512
        x_sb = sb("x_sb", NT * D)[:, :].rearrange("p (t d) -> p t d", t=NT)
        ring_lo = sb("ring_lo", 3 * SLOT)
        ZW = 29000
        zone = sb("zone", ZW)
        cst = sb("cst", CW)
        ones = sb("ones", P)
        small = sb("small", 2600)

        def slot_ap(s):
            return ring_lo[:, s * SLOT:(s + 1) * SLOT] if s < 3 else zone[:, (s - 3) * SLOT:(s - 2) * SLOT]

        def cut(area, off, pattern=None, width=None, parts=P, **k):
            ap = area[0:parts, off:off + width]
            return ap.rearrange(pattern, **k) if pattern else ap

        ident = cst[:, CI:CI + P]
        tri_f, tri_b = cst[:, CU:CU + P], cst[:, CL:CL + P]
        mask_d = [cst[:, CMF:CMF + P], cst[:, CMB:CMB + P]]

        at = [0]

        def sm(width, pattern=None, **k):
            o = at[0]
            at[0] += width
            assert at[0] <= 2600
            return cut(small, o, pattern, width, **k)

        NP_ROWS = 100
        stage = [sm(P) for _ in range(DEPTH)]
        pcol = [sm(NP_ROWS) for _ in range(DEPTH)]
        csil = sm(16)
        modc = sm(96, "p (m s) -> p m s", m=48)
        cA = [sm(16, "p (k s) -> p k s", k=KD) for _ in range(2)]
        cS = [sm(16, "p (k s) -> p k s", k=KD) for _ in range(2)]
        cG = [sm(16, "p (k s) -> p k s", k=KD) for _ in range(2)]
        ss, rstd, = sm(NT), sm(NT)
        gw = sm(KD * 16, "p (k n) -> p k n", k=KD)
        rw = sm(KD * NE, "p (k n) -> p k n", k=KD)
        gbias = sm(16)
        gates = sm(NT * 16, "p (c g) -> p c g", c=NT)

        def g48(n=1):
            return [sm(48, "p (r c h) -> p r c h", r=2, c=NT) for _ in range(n)]

        lf, gb, ga, gbl, gt1, mprev, mlast, amax, cmax, mt, xp0, xp1, xp2, xp3 = g48(14)
        rden, dn = sm(4), sm(4)
        mx8 = sm(8)
        nmx = sm(4)
        rsum = sm(8)
        rrec = sm(8)
        hss, hrr = sm(4), sm(4)
        epsc = sm(1)

        hT = cut(zone, 0, "p (k t) -> p k t", 6144, k=KD)
        brT = cut(zone, 6144, "p (b k t) -> p b k t", 9216, b=3, k=KB)
        Z0 = 15360
        qk_tm = cut(zone, 9216, "p (c n) -> p c n", 3072, c=NT)
        hsum = cut(zone, 12288, "p (c n) -> p c n", 3072, c=NT)
        o = Z0
        v_ext = cut(zone, o, "p (c h n) -> p c h n", 3096, c=NT, h=MH); o += 3096
        qT = cut(zone, o, "p (g t) -> p g t", 1536, g=2); o += 1536
        kT = cut(zone, o, "p (g t) -> p g t", 1536, g=2); o += 1536
        Cst = cut(zone, o, "p (r g n) -> p r g n", 516, r=2, g=2); o += 516
        dmat = cut(zone, o, None, 512); o += 512
        sd = cut(zone, o, None, 512); o += 512
        sdT = cut(zone, o, None, 512); o += 512
        qcs = cut(zone, o, "p (g h n) -> p g h n", 516, g=2, h=2); o += 516
        nd = cut(zone, o, "p (g h n) -> p g h n", 516, g=2, h=2); o += 516
        vws = cut(zone, o, "p (h n) -> p h n", 516, h=MH); o += 516
        Cdec = cut(zone, o, "p (g n) -> p g n", 258, g=2); o += 258
        htmp = cut(zone, o, None, 512); o += 512
        osig = cut(zone, o, None, 512); o += 512
        t_rope = [cut(zone, o + 512 * i, None, 512) for i in range(2)]; o += 1024
        assert o <= ZW, o
        o = Z0
        qnL = cut(zone, o, "p (f b q) -> p f b q", 2048, f=KB, b=NB); o += 2048
        qnC = cut(zone, o, "p (f t) -> p f t", 1024, f=KB); o += 1024
        knT = cut(zone, o, "p (f t) -> p f t", 3072, f=KB); o += 3072
        vw = [cut(zone, 9216 + 1024 * i, "p (u n) -> p u n", 1024, u=2) for i in range(2)]
        vctx = cut(zone, 11264, "p (u n) -> p u n", 1024, u=2)
        tab = cut(zone, o, "p (h w) -> p h w", 2048, h=4); o += 2048
        bm = [cut(zone, o + 256 * i, "p (j k) -> p j k", 256, j=ROWS) for i in range(3)]; o += 768
        pr = [cut(zone, o + 512 * i, None, 512) for i in range(2)]; o += 1024
        prT = [cut(zone, o + 512 * i, None, 512) for i in range(2)]; o += 1024
        o_tm = [cut(zone, o + 256 * i, None, 256) for i in range(2)]; o += 512
        vstage = [cut(zone, o + 512 * i, None, 512) for i in range(2)]; o += 1024
        assert o <= ZW, o
        o = Z0
        pu = cut(zone, o, "p (g t) -> p g t", 4 * PADW, g=4); o += 4 * PADW
        pA = cut(zone, o, "p (g t) -> p g t", 4 * PADW, g=4); o += 4 * PADW
        pB = cut(zone, o, "p (g t) -> p g t", 4 * PADW, g=4); o += 4 * PADW
        pin = cut(zone, o, "p (g t) -> p g t", 4 * TOK, g=4); o += 4 * TOK
        pw = cut(zone, o, "p (g n) -> p g n", 512, g=4); o += 512
        assert o <= ZW, o
        acc = cut(zone, Z0, "p (f t) -> p f t", 6144, f=KD)
        sg = [cut(zone, 21504 + 768 * i, None, 768) for i in range(2)]
        mtmp = [cut(zone, 23040 + 768 * i, None, 768) for i in range(2)]
        grow = cut(zone, 26900, "p (s d) -> p s d", 2048, s=2)
        ytmp = [cut(zone, 21504 + 1024 * i, None, 1024) for i in range(2)]
        yjunk = cut(zone, 23552, None, 1024)
        xn = cut(zone, 12288, "p (t d) -> p t d", 6144, t=NT)
        h2T = cut(zone, 18432, "p (k t) -> p k t", 6144, k=KD)
        junk = cut(zone, 24600, None, 1024)
        affn = cut(zone, 24600, "p (t e) -> p t e", NT * NE, t=NT)
        affT = cut(zone, 24700, None, TOK, parts=NE)
        tv = cut(zone, 25500, None, 96, parts=NE)
        ti = cut(zone, 25600, None, 96, parts=NE).bitcast(U32)
        tif = cut(zone, 25700, None, 96, parts=NE)
        gval = cut(zone, 25800, None, NE + 1)
        gidx = cut(zone, 25820, None, NE + 1).bitcast(U32)
        icur = cut(zone, 25840, None, 1).bitcast(U32)
        iprev = cut(zone, 25842, None, 1).bitcast(U32)
        gcur = cut(zone, 25841, None, 1)
        aexp = cut(zone, 25850, "p (t e) -> p t e", NT * NE, t=NT)
        asum, arec = cut(zone, 25950, None, NT), cut(zone, 25960, None, NT)
        xe = cut(zone, 18432, None, 1024)
        xeT = cut(zone, 19456, "p (k c) -> p k c", 768, k=KD)
        gsil = cut(zone, 20224, None, 384)
        hid = cut(zone, 20608, "p (f c) -> p f c", 768, f=KD)
        yfm = cut(zone, 21376, "p (f c) -> p f c", 768, f=KD)
        ytm = cut(zone, 22144, None, 1024)

        PS = [ctx.enter_context(nc.psum_tensor(f"ps{i}", [P, 1024], F32)) for i in range(4)]

        def bank(j):
            return PS[j // 2][:, (j % 2) * 512:(j % 2) * 512 + 512]

        v_dram = [dram(f"v_dram{l}", (S, BW)) for l in range(DEPTH)]
        xn_dram = [dram(f"xn_dram{l}", (TOK, D)) for l in range(DEPTH)]
        moe_dram = [dram(f"moe_dram{l}", (TOK, D)) for l in range(DEPTH)]

        units, filled = {}, [0] * 6

        def add(key, src, slot, pat, **k):
            filled[slot] += 1
            units[key] = (src, slot, filled[slot], pat, k)

        w_in, ada, wbr, wout = A["w_in"], A["ada_w"], A["w_branch"], A["w_out"]

        def kn512(w, c):
            return w[:, c:c + 512].rearrange("(k p) n -> p k n", p=P)

        moe_base = []
        for l in range(DEPTH):
            n = [0]

            def nxt(key, src):
                add((l,) + key, src, n[0] % 3, None)
                n[0] += 1
            for j in range(12):
                nxt(("ada", j), kn512(ada[l], 512 * j))
            for name, c in (("qk", C_QK), ("v", C_V), ("o", C_O), ("kn", C_KN), ("qn", C_QN), ("vn", C_VN),
                            ("pu", C_PU)):
                nxt((name,), kn512(w_in[l], c))
            for b in range(3):
                nxt(("wb", b), wbr[l, b].rearrange("(k p) n -> p k n", p=P))
                for j in range(2):
                    nxt(("bg", b, j), kn512(w_in[l], C_BG + D * b + 512 * j))
            for j in range(2):
                nxt(("wout", j), kn512(wout[l], 512 * j))
            assert n[0] % 3 == 0
            moe_base.append(list(filled))
            for s in range(6):
                filled[s] += NE

        PER = dict(hss=6, hroot=6, fabs=1, ga=1, gexp=1, gsum=1, lf=1, logit=1, aff=1, afftr=1, asub=1, aexp=1, top=1,
                   toptr=1, softp=1, moe_in=16, xn_out=16, m_C0=1, pu=1, pw_in=16, arow=12, amax=12,
                   qk_tr=6, qkT=6, m_arow=12, m_s=12, m_qc=12, m_sd=12, m_sdt=12, m_sdT=12, m_num=12, m_h=12,
                   m_dm=12, m_D=12, m_kv=10, m_vw=10, m_C=10, ada_done=12, mg_mm=24, mg_sg=24, mg_free=26,
                   mg_tfree=26, unit_done=96, gsil=32, hid=33, icur=16, ig_free=17, xe_T=17, xeT=17, y_T=16,
                   yfm=32, ytm=17, xe_in=272, y_added=256, proj=13, proj_out=12, np=14, np_out=14, oproj=6,
                   osig=6, hfin=6, mT=6, mtr=6, tab_in=256, a_bm=32, a_s=48, a_exp=48, a_max=48, a_tr=48,
                   a_pT=48, a_pv=48, a_o=12, a_otr=12, a_fin=12, pup=4, pin=4, pmap=4, y=6, yss=6, y_free=8)

        def w_ready(s):
            return sem(f"w_ready{s}")

        released = {}

        def phase_end(eng, n):
            eng.drain().then_inc(sem("phase"), 1)
            eng.wait_ge(sem("phase"), 4 * n)
        NPH = 13

        def nt(l):
            return NT if l == 0 else LT

        def TW(l):
            return P * nt(l)

        def streams(l):
            return [(0, 0, S)] + ([(1, S, CTX)] if l == 0 else [])

        def both():
            return [(0, 0, S), (1, S, CTX)]

        nslot = [96, 64]
        FW, BWD = [4, 5, 0, 1, 2, 3], [5, 4, 3, 2, 1, 0]

        def att_units(l):
            us = [("L", hg, b, h4) for hg in range(2) for b in range(NB) for h4 in range(4)]
            if l == 0:
                us += [("C", hg, b, h4) for hg in range(2) for b in range(CT) for h4 in range(4)]
            return us

        block = ctx.enter_context(nc.Block())

        @block.tensor
        def _(pe):
            mm, tr = nc.tensor.matmul, nc.tensor.transpose

            def unit(key):
                src, slot, count, _, _ = units[key]
                pe.wait_ge(w_ready(slot), 16 * count)
                return slot_ap(slot)

            def k8(w):
                return w.rearrange("p (k n) -> p k n", k=KD)

            pe.wait_ge(sem("const_in"), 16)
            pe.wait_ge(sem("ones_set"), 1)
            for l in range(DEPTH):
                ph = NPH * l
                first = l == 0
                if l:
                    pe.wait_ge(sem(f"growS1_{l - 1}"), 1)
                pe.wait_ge(sem("stage_in"), 80 * (l + 1))
                tr(bank(0)[:, 0:NP_ROWS], stage[l][0:NP_ROWS, :], ident[0:NP_ROWS, 0:NP_ROWS]).then_inc(sem("stage_T"), 1)
                pe.wait_ge(sem("csil"), 1)
                for j in range(12):
                    w = k8(unit((l, "ada", j)))
                    for c in range(4):
                        for k in range(KD):
                            i = mm(bank(1)[:, (j * 4 + c) * 2:(j * 4 + c) * 2 + 2], w[:, k, c * P:(c + 1) * P],
                                   csil[:, k::8], start=(k == 0), stop=(k == KD - 1))
                    i.then_inc(sem("ada_done"), 1)
                    released[l, "ada", j] = ("ada_done", l * PER["ada_done"] + j + 1)
                phase_end(pe, ph + 1)

                def to_columns(tag, tiles):
                    for k in range(KD):
                        if k == 0:
                            pe.wait_ge(sem(f"{tag}_xn{l}"), tiles)
                        if k >= 4:
                            pe.wait_ge(sem(f"{tag}_colL{l}"), k - 3)
                            if tiles > LT:
                                pe.wait_ge(sem(f"{tag}_colC{l}"), k - 3)
                        for t in range(tiles):
                            i = tr(PS[k % 4][:, t * P:(t + 1) * P], xn[:, t, k * P:(k + 1) * P], ident)
                        i.then_inc(sem(f"{tag}_T{l}"), 1)
                to_columns("n1", NT)
                phase_end(pe, ph + 2)

                g = 0
                for name in ("qk", "v"):
                    w = k8(unit((l, name)))
                    for t in range(NT):
                        if g >= 8:
                            pe.wait_ge(sem("proj_out"), l * PER["proj_out"] + g - 7)
                        for k in range(KD):
                            i = mm(bank(g % 8), hT[:, k, t * P:(t + 1) * P], w[:, k, :], start=(k == 0), stop=(k == KD - 1))
                        g += 1
                        i.then_inc(sem("proj"), 1)
                    released[l, name] = ("proj", l * PER["proj"] + g)
                pe.wait_ge(sem("proj_out"), l * PER["proj_out"] + g - 7)
                pe.wait_ge(sem("gw_in"), 48 * (l + 1))
                for t in range(NT):
                    for k in range(KD):
                        i = mm(bank(g % 8)[:, t * 16:(t + 1) * 16], hT[:, k, t * P:(t + 1) * P], gw[:, k, :],
                               start=(k == 0), stop=(k == KD - 1))
                i.then_inc(sem("proj"), 1)
                phase_end(pe, ph + 3)

                pe.wait_ge(sem("lf"), l * PER["lf"] + 1)
                mm(bank(0)[:, 0:24], tri_f, lf[:, 0].rearrange("p c h -> p (c h)"), start=True, stop=True)
                mm(bank(0)[:, 24:48], tri_b, lf[:, 1].rearrange("p c h -> p (c h)"), start=True, stop=True)
                mm(bank(0)[:, 48:96], ones[:, :], lf.rearrange("p r c h -> p (r c h)"), start=True, stop=True)\
                    .then_inc(sem("gsum"), 1)
                pe.wait_ge(sem("ga"), l * PER["ga"] + 1)

                def a_rows(dst, r, c):
                    for h in range(MH):
                        i = mm(dst[:, h * P:(h + 1) * P], ga[:, r, c, h:h + 1].to_broadcast([P, P]), ident,
                               start=True, stop=True)
                    return i
                n = 0
                for r in range(2):
                    for c in range(NT):
                        if n >= 2:
                            pe.wait_ge(sem("amax"), l * PER["amax"] + n - 1)
                        a_rows(bank(1 + n % 2), r, c).then_inc(sem("arow"), 1)
                        n += 1
                for c in range(NT):
                    if c >= 2:
                        pe.wait_ge(sem("qkT"), l * PER["qkT"] + c - 1)
                    for j in range(4):
                        i = tr(bank(3 + c % 2)[:, j * P:(j + 1) * P], qk_tm[:, c, j * P:(j + 1) * P], ident)
                    i.then_inc(sem("qk_tr"), 1)
                phase_end(pe, ph + 4)

                u = 0
                for st in range(6):
                    for r in range(2):
                        c = (FW, BWD)[r][st]
                        outp = c < nt(l)
                        if outp:
                            if u:
                                pe.wait_ge(sem("m_h"), l * PER["m_h"] + u)
                            a_rows(bank(0), r, c).then_inc(sem("m_arow"), 1)
                            for h in range(MH):
                                q0 = 64 * (h % 2)
                                i = mm(bank(4 + h % 2)[:, (h // 2) * P:(h // 2 + 1) * P], qT[q0:q0 + 64, h // 2, c * P:(c + 1) * P],
                                       kT[q0:q0 + 64, h // 2, c * P:(c + 1) * P], start=True, stop=True)
                            i.then_inc(sem("m_s"), 1)
                            if st:
                                pe.wait_ge(sem("m_C"), l * PER["m_C"] + 2 * st + r - 1)
                            else:
                                pe.wait_ge(sem("m_C0"), l * PER["m_C0"] + 1)
                            for h in range(MH):
                                q0 = 64 * (h % 2)
                                i = mm(bank(2 + h % 2)[:, (h // 2) * 129:(h // 2) * 129 + 129],
                                       qT[q0:q0 + 64, h // 2, c * P:(c + 1) * P], Cst[q0:q0 + 64, r, h // 2, :],
                                       start=True, stop=True)
                            i.then_inc(sem("m_qc"), 1)
                            pe.wait_ge(sem("m_sd"), l * PER["m_sd"] + u + 1)
                            for h in range(MH):
                                i = tr(bank(0)[:, h * P:(h + 1) * P], sd[:, h * P:(h + 1) * P], ident)
                            i.then_inc(sem("m_sdt"), 1)
                            pe.wait_ge(sem("m_sdT"), l * PER["m_sdT"] + u + 1)
                            for h in range(MH):
                                i = mm(bank(4 + h % 2)[:, (h // 2) * 129:(h // 2) * 129 + 129],
                                       sdT[:, h * P:(h + 1) * P], v_ext[:, c, h, :], start=True, stop=True)
                            i.then_inc(sem("m_num"), 1)
                            u += 1
                        if st < 5:
                            pe.wait_ge(sem("m_vw"), l * PER["m_vw"] + 2 * st + r + 1)
                            if 2 * st + r:
                                pe.wait_ge(sem("m_C"), l * PER["m_C"] + 2 * st + r)
                            for h in range(MH):
                                q0 = 64 * (h % 2)
                                i = mm(PS[3][q0:q0 + 64, (h // 2) * 129:(h // 2) * 129 + 129],
                                       qk_tm[:, c, 256 + h * 64:256 + h * 64 + 64], vws[:, h, :], start=True, stop=True)
                            i.then_inc(sem("m_kv"), 1)
                phase_end(pe, ph + 5)
                w = k8(unit((l, "o")))
                for t in range(nt(l)):
                    if t >= 2:
                        pe.wait_ge(sem("osig"), l * PER["osig"] + t - 1)
                    for k in range(KD):
                        i = mm(bank(t % 2), hT[:, k, t * P:(t + 1) * P], w[:, k, :], start=(k == 0), stop=(k == KD - 1))
                    i.then_inc(sem("oproj"), 1)
                    released[l, "o"] = ("oproj", l * PER["oproj"] + nt(l))
                    pe.wait_ge(sem("hfin"), l * PER["hfin"] + t + 1)
                    if t >= 2:
                        pe.wait_ge(sem("mT"), l * PER["mT"] + t - 1)
                    for j in range(KB):
                        i = tr(bank(2 + t % 2)[:, j * P:(j + 1) * P], htmp[:, j * P:(j + 1) * P], ident)
                    i.then_inc(sem("mtr"), 1)
                phase_end(pe, ph + 6)

                g = 0
                for name in ("kn", "qn"):
                    w = k8(unit((l, name)))
                    sts = both() if name == "kn" else streams(l)
                    for f in range(KB):
                        if g >= 4:
                            pe.wait_ge(sem("np_out"), l * PER["np_out"] + g - 3)
                        for _, t0, tw in sts:
                            for k in range(KD):
                                i = mm(PS[g % 4][:, t0:t0 + tw], w[:, k, f * P:(f + 1) * P], hT[:, k, t0:t0 + tw],
                                       start=(k == 0), stop=(k == KD - 1))
                        g += 1
                        i.then_inc(sem("np"), 1)
                    released[l, name] = ("np", l * PER["np"] + g)
                w = k8(unit((l, "vn")))
                for t in range(NT):
                    pe.wait_ge(sem("np_out"), l * PER["np_out"] + g - 3)
                    for k in range(KD):
                        i = mm(PS[g % 4][:, 0:512], hT[:, k, t * P:(t + 1) * P], w[:, k, :], start=(k == 0), stop=(k == KD - 1))
                    g += 1
                    i.then_inc(sem("np"), 1)
                released[l, "vn"] = ("np", l * PER["np"] + g)
                phase_end(pe, ph + 7)

                us = att_units(l)

                def scores(n):
                    kind, hg, b, h4 = us[n]
                    h = hg * 4 + h4
                    q0, f = 64 * (h % 2), h // 2
                    if n >= 2:
                        pe.wait_ge(sem("a_exp"), l * PER["a_exp"] + n - 1)
                    sp = bank(n % 2)
                    if kind == "L":
                        q = qnL[q0:q0 + 64, f, b, :]
                        kk = knT[q0:q0 + 64, f, 0:S].rearrange("p (j c) -> p j c", c=GW)[:, :, KSTART[b]:KSTART[b] + KC]
                        mm(sp[:, 0:256], q, kk, start=True, stop=True)
                        mm(sp[:, 256:512], q, knT[q0:q0 + 64, f, S:TOK], start=True, stop=True).then_inc(sem("a_s"), 1)
                    else:
                        q = qnC[q0:q0 + 64, f, b * P:(b + 1) * P]
                        mm(sp[:, 256:512], q, knT[q0:q0 + 64, f, S:TOK], start=True, stop=True).then_inc(sem("a_s"), 1)

                def rest(n):
                    kind, hg, b, h4 = us[n]
                    grp = n // 4
                    h = hg * 4 + h4
                    pe.wait_ge(sem("a_exp"), l * PER["a_exp"] + n + 1)
                    if n >= 2:
                        pe.wait_ge(sem("a_pT"), l * PER["a_pT"] + n - 1)
                    js = range(4) if kind == "L" else (2, 3)
                    for j in js:
                        i = tr(bank(2 + n % 2)[:, j * P:(j + 1) * P], pr[n % 2][:, j * P:(j + 1) * P], ident)
                    i.then_inc(sem("a_tr"), 1)
                    pe.wait_ge(sem("a_pT"), l * PER["a_pT"] + n + 1)
                    if kind == "L" and h4 == 0:
                        pe.wait_ge(sem(f"vw_in{grp % 2}_{l}"), 128 * (grp // 2 + 1))
                    if h4 == 0 and grp >= 2:
                        pe.wait_ge(sem("a_o"), l * PER["a_o"] + grp - 1)
                    for j in js:
                        v = vw[grp % 2][:, j, :] if j < 2 else vctx[:, j - 2, :]
                        i = mm(bank(4 + grp % 2)[:, h4 * 64:h4 * 64 + 64], prT[n % 2][:, j * P:(j + 1) * P],
                               v[:, h * 64:h * 64 + 64], start=(j == js[0]), stop=(j == 3))
                    i.then_inc(sem("a_pv"), 1)

                def to_cols(grp):
                    pe.wait_ge(sem("a_o"), l * PER["a_o"] + grp + 1)
                    if grp:
                        pe.wait_ge(sem("a_fin"), l * PER["a_fin"] + grp)
                    for j in range(2):
                        i = tr(bank(6)[:, j * P:(j + 1) * P], o_tm[grp % 2][:, j * P:(j + 1) * P], ident)
                    i.then_inc(sem("a_otr"), 1)
                scores(0)
                for n in range(len(us)):
                    if n + 1 < len(us):
                        scores(n + 1)
                    rest(n)
                    if n % 4 == 0 and n:
                        to_cols(n // 4 - 1)
                to_cols(len(us) // 4 - 1)
                phase_end(pe, ph + 8)

                w = k8(unit((l, "pu")))
                for f in range(KB):
                    for _, t0, tw in streams(l):
                        for k in range(KD):
                            i = mm(PS[f][:, t0:t0 + tw], w[:, k, f * P:(f + 1) * P], hT[:, k, t0:t0 + tw],
                                   start=(k == 0), stop=(k == KD - 1))
                    i.then_inc(sem("pup"), 1)
                released[l, "pu"] = ("pup", l * PER["pup"] + 4)
                pe.wait_ge(sem("pw_in"), l * PER["pw_in"] + 16)
                for gi in range(4):
                    pe.wait_ge(sem("pin"), l * PER["pin"] + gi + 1)
                    for _, t0, tw in streams(l):
                        i = mm(PS[gi][:, t0:t0 + tw], pw[:, gi, :], pin[:, gi, t0:t0 + tw], start=True, stop=True)
                    i.then_inc(sem("pmap"), 1)
                phase_end(pe, ph + 9)

                with pe.Fori(0, 3) as bi:
                    pe.wait_ge(w_ready(units[l, "wb", 0][1]), bi * 16 + 16 * units[l, "wb", 0][2])
                    wb = slot_ap(units[l, "wb", 0][1]).rearrange("p (k n) -> p k n", k=KB)
                    for f in range(KD):
                        if f % 4 == 0:
                            key = (l, "bg", 0, f // 4)
                            pe.wait_ge(w_ready(units[key][1]), bi * 16 + 16 * units[key][2])
                            wg = k8(slot_ap(units[key][1]))
                        pe.wait_ge(sem("mg_free"), l * PER["mg_free"] + bi * KD + (f + 1))
                        pb, pg = PS[(f % 2) * 2], PS[(f % 2) * 2 + 1]
                        for _, t0, tw in streams(l):
                            for k in range(KB):
                                mm(pb[:, t0:t0 + tw], wb[:, k, f * P:(f + 1) * P],
                                   brT[:, bass.ds(bi, 1), k, t0:t0 + tw], start=(k == 0), stop=(k == KB - 1))
                            for k in range(KD):
                                i = mm(pg[:, t0:t0 + tw], wg[:, k, (f % 4) * P:(f % 4 + 1) * P], hT[:, k, t0:t0 + tw],
                                       start=(k == 0), stop=(k == KD - 1))
                        i.then_inc(sem("mg_mm"), 1)
                for b in range(3):
                    released[l, "wb", b] = ("mg_mm", l * PER["mg_mm"] + b * KD + KD)
                    for j in range(2):
                        released[l, "bg", b, j] = ("mg_mm", l * PER["mg_mm"] + b * KD + 4 * j + 4)
                phase_end(pe, ph + 10)

                def gain_rows(which):
                    for s in range(2):
                        for k in range(KD):
                            i = mm(PS[s][:, k * P:(k + 1) * P], cG[which][:, k, s:s + 1].to_broadcast([P, P]), ident,
                                   start=True, stop=True)
                        i.then_inc(sem(f"grow{which}_{l}"), 1)
                gain_rows(0)
                w0, w1 = k8(unit((l, "wout", 0))), k8(unit((l, "wout", 1)))
                for t in range(nt(l)):
                    pe.wait_ge(sem("y_free"), l * PER["y_free"] + t + 1)
                    for j, w in enumerate((w0, w1)):
                        for k in range(KD):
                            i = mm(PS[2 + t % 2][:, j * 512:(j + 1) * 512], acc[:, k, t * P:(t + 1) * P], w[:, k, :],
                                   start=(k == 0), stop=(k == KD - 1))
                    i.then_inc(sem("y"), 1)
                for j in range(2):
                    released[l, "wout", j] = ("y", l * PER["y"] + nt(l))
                phase_end(pe, ph + 11)

                to_columns("n2", nt(l))
                pe.wait_ge(sem(f"n2_colL{l}"), KD)
                if first:
                    pe.wait_ge(sem(f"n2_colC{l}"), KD)
                for t in range(nt(l)):
                    for k in range(KD):
                        i = mm(bank(0)[:, t * NE:(t + 1) * NE], h2T[:, k, t * P:(t + 1) * P], rw[:, k, :],
                               start=(k == 0), stop=(k == KD - 1))
                i.then_inc(sem("logit"), 1)
                pe.wait_ge(sem("aff"), l * PER["aff"] + 1)
                for t in range(nt(l)):
                    i = tr(PS[1][0:NE, t * P:(t + 1) * P], affn[:, t, :], ident)
                i.then_inc(sem("afftr"), 1)
                ns = nslot[l]
                pe.wait_ge(sem("top"), l * PER["top"] + 1)
                tr(bank(1)[0:ns, 0:NE], tv[:, 0:ns], ident[0:NE, 0:NE])
                tr(bank(1)[0:ns, 16:16 + NE], tif[:, 0:ns], ident[0:NE, 0:NE]).then_inc(sem("toptr"), 1)
                phase_end(pe, ph + 12)

                def gather_T(e, add_):
                    pe.wait_ge(sem("xe_in"), l * PER["xe_in"] + 16 * e + 16 * (1 + add_))
                    pe.sem_inc(sem("pe_turn"), 1)
                    for k in range(KD):
                        i = tr(PS[0][:, k * 128:k * 128 + ns], xe[0:ns, k * P:(k + 1) * P], ident[0:ns, 0:ns])
                    i.then_inc(sem("xe_T"), 1)
                gather_T(0, 0)
                with pe.Fori(0, NE) as e:
                    pe.wait_ge(sem("xeT"), l * PER["xeT"] + e + 1)
                    for half in range(2):
                        for j in range(2):
                            s = 2 * half + j
                            pe.wait_ge(w_ready(s), e * 16 + 16 * (moe_base[l][s] + 1))
                            w = k8(slot_ap(s))
                            for f in range(4):
                                for k in range(KD):
                                    i = mm(bank(2 + s)[:, f * ns:(f + 1) * ns], w[:, k, f * P:(f + 1) * P],
                                           xeT[:, k, 0:ns], start=(k == 0), stop=(k == KD - 1))
                            i.then_inc(sem("unit_done"), 1)
                    gather_T(e, 1)
                    pe.wait_ge(sem("hid"), l * PER["hid"] + 2 * e + 3)
                    for half in range(2):
                        s = 4 + half
                        pe.wait_ge(w_ready(s), e * 16 + 16 * (moe_base[l][s] + 1))
                        w = k8(slot_ap(s))
                        for f in range(4):
                            for k in range(KD):
                                i = mm(bank(2 + half)[:, f * ns:(f + 1) * ns], w[:, k, f * P:(f + 1) * P],
                                       hid[:, k, 0:ns], start=(k == 0), stop=(k == KD - 1))
                        i.then_inc(sem("unit_done"), 1)
                    pe.wait_ge(sem("yfm"), l * PER["yfm"] + 2 * e + 2)
                    pe.wait_ge(sem("ytm"), l * PER["ytm"] + e + 1)
                    pe.sem_inc(sem("pe_turn"), 1)
                    for k in range(KD):
                        i = tr(PS[3][0:ns, k * P:(k + 1) * P], yfm[:, k, 0:ns], ident)
                    i.then_inc(sem("y_T"), 1)
                phase_end(pe, ph + 13)
                gain_rows(1)

        @block.scalar
        def _(act):
            A_ = nc.scalar.activation
            n_link = [0]

            def link(ins):
                n_link[0] += 1
                ins.then_inc(sem("act_link"), 1)
                act.wait_ge(sem("act_link"), n_link[0])

            for l in range(DEPTH):
                ph = NPH * l
                first = l == 0
                if first:
                    act.wait_ge(sem("pcol"), 1)
                    A_(csil[:, :], pcol[0][:, 0:16], ACT.Silu).then_inc(sem("csil"), 1)
                phase_end(act, ph + 1)

                def squares(tag, tiles, src):
                    for t in range(tiles):
                        link(A_(junk, src[:, t, :], ACT.Square, accum_out=ss[:, t:t + 1]))
                    act.drain()
                    A_(ss[:, 0:tiles], ss[:, 0:tiles], ACT.Sqrt, bias=epsc, scale=1.0 / D).then_inc(sem(f"{tag}_ss{l}"), 1)

                def norm_cols(tag, tiles, dst, which):
                    act.wait_ge(sem(f"{tag}_rstd{l}"), 1)
                    for t in range(0, tiles, 2):
                        A_(xn[:, t, :], x_sb[:, t, :], ACT.Copy, scale=rstd[:, t:t + 1]).then_inc(sem(f"{tag}_xn{l}"), 1)
                    for k in range(KD):
                        act.wait_ge(sem(f"{tag}_T{l}"), k + 1)
                        A_(dst[:, k, 0:S], PS[k % 4][:, 0:S], ACT.Identity, bias=cS[which][:, k, 0:1],
                           scale=cA[which][:, k, 0:1]).then_inc(sem(f"{tag}_colL{l}"), 1)
                if first:
                    act.wait_ge(sem("x_in"), 32)
                squares("n1", NT, x_sb)
                norm_cols("n1", NT, hT, 0)
                phase_end(act, ph + 2)

                g = 0
                for name in ("qk", "v"):
                    for t in range(NT):
                        act.wait_ge(sem("proj"), l * PER["proj"] + g + 1)
                        if name == "qk":
                            A_(qk_tm[:, t, 0:256], bank(g % 8)[:, 0:256], ACT.Copy, scale=DK ** -0.5)
                            A_(qk_tm[:, t, 256:512], bank(g % 8)[:, 256:512], ACT.Copy).then_inc(sem("proj_out"), 1)
                        else:
                            A_(v_ext[:, t, :, 0:DV], bank(g % 8).rearrange("p (h n) -> p h n", h=MH), ACT.Copy)\
                                .then_inc(sem("proj_out"), 1)
                        g += 1
                phase_end(act, ph + 3)

                act.wait_ge(sem("fabs"), l * PER["fabs"] + 1)
                link(A_(gt1, gt1, ACT.Exp, scale=-1.0))
                A_(gt1, gt1, ACT.Ln, bias=1.0).then_inc(sem("softp"), 1)
                for c in range(NT):
                    act.wait_ge(sem("qk_tr"), l * PER["qk_tr"] + c + 1)
                    b4 = bank(3 + c % 2).rearrange("p (j t) -> p j t", j=4)
                    A_(qT[:, :, c * P:(c + 1) * P], b4[:, 0:2, :], ACT.Copy)
                    A_(kT[:, :, c * P:(c + 1) * P], b4[:, 2:4, :], ACT.Copy).then_inc(sem("qkT"), 1)
                act.wait_ge(sem("gexp"), l * PER["gexp"] + 1)
                for t_ in (xp0, xp1, xp2, xp3):
                    A_(t_, t_, ACT.Exp)
                phase_end(act, ph + 4)

                u = 0
                for st in range(6):
                    for r in range(2):
                        c = (FW, BWD)[r][st]
                        if c < nt(l):
                            act.wait_ge(sem("m_dm"), l * PER["m_dm"] + u + 1)
                            A_(dmat, dmat, ACT.Exp).then_inc(sem("m_D"), 1)
                            act.wait_ge(sem("m_sdt"), l * PER["m_sdt"] + u + 1)
                            A_(sdT, bank(0), ACT.Copy).then_inc(sem("m_sdT"), 1)
                            u += 1
                phase_end(act, ph + 5)
                for t in range(nt(l)):
                    act.wait_ge(sem("oproj"), l * PER["oproj"] + t + 1)
                    if t:
                        act.wait_ge(sem("hfin"), l * PER["hfin"] + t)
                    A_(osig, bank(t % 2), ACT.Sigmoid).then_inc(sem("osig"), 1)
                    act.wait_ge(sem("hss"), l * PER["hss"] + t + 1)
                    A_(hss, hss, ACT.Sqrt, bias=epsc, scale=1.0 / DV).then_inc(sem("hroot"), 1)
                    act.wait_ge(sem("mtr"), l * PER["mtr"] + t + 1)
                    A_(brT[:, 0, :, t * P:(t + 1) * P], bank(2 + t % 2).rearrange("p (j t) -> p j t", j=KB), ACT.Copy)\
                        .then_inc(sem("mT"), 1)
                phase_end(act, ph + 6)

                g = 0
                for f in range(KB):
                    act.wait_ge(sem("np"), l * PER["np"] + g + 1)
                    A_(knT[:, f, :], PS[g % 4][:, 0:TOK], ACT.Copy).then_inc(sem("np_out"), 1)
                    g += 1
                for f in range(KB):
                    act.wait_ge(sem("np"), l * PER["np"] + g + 1)
                    if first:
                        A_(qnC[:, f, :], PS[g % 4][:, S:TOK], ACT.Copy, scale=DH ** -0.5)
                    A_(qnL[:, f].rearrange("p b (r q) -> p b r q", r=ROWS),
                       PS[g % 4][:, 0:S].rearrange("p (r b q) -> p b r q", r=ROWS, b=NB)[:, :, :, ::-1], ACT.Copy, scale=DH ** -0.5)\
                        .then_inc(sem("np_out"), 1)
                    g += 1
                for t in range(NT):
                    act.wait_ge(sem("np"), l * PER["np"] + g + 1)
                    if t < LT:
                        if t >= 2:
                            act.wait_ge(sem(f"v_out{t % 2}_{l}"), 16)
                        A_(vstage[t % 2], PS[g % 4][:, 0:512], ACT.Copy).then_inc(sem("np_out"), 1)
                    else:
                        A_(vctx[:, t - LT, :], PS[g % 4][:, 0:512], ACT.Copy).then_inc(sem("np_out"), 1)
                    g += 1
                phase_end(act, ph + 7)

                us = att_units(l)

                def pT(n):
                    kind = us[n][0]
                    lo = 0 if kind == "L" else 256
                    act.wait_ge(sem("a_tr"), l * PER["a_tr"] + n + 1)
                    if n >= 2:
                        act.wait_ge(sem("a_pv"), l * PER["a_pv"] + n - 1)
                    A_(prT[n % 2][:, lo:512], bank(2 + n % 2)[:, lo:512], ACT.Copy).then_inc(sem("a_pT"), 1)
                for n in range(len(us)):
                    lo = 0 if us[n][0] == "L" else 256
                    act.wait_ge(sem("a_max"), l * PER["a_max"] + n + 1)
                    if n >= 2:
                        act.wait_ge(sem("a_tr"), l * PER["a_tr"] + n - 1)
                    if n % 4 == 0 and n >= 8:
                        act.wait_ge(sem("a_o"), l * PER["a_o"] + n // 4 - 1)
                    A_(pr[n % 2][:, lo:512], bank(n % 2)[:, lo:512], ACT.Exp, bias=nmx[:, n % 4:n % 4 + 1],
                       accum_out=rsum[:, n % 8:n % 8 + 1]).then_inc(sem("a_exp"), 1)
                    pT(n)
                phase_end(act, ph + 8)

                for f in range(KB):
                    act.wait_ge(sem("pup"), l * PER["pup"] + f + 1)
                    A_(pu[:, f, LCOL:LCOL + S], PS[f][:, 0:S], ACT.Copy)
                    if first:
                        A_(pu[:, f, CCOL:CCOL + CTX], PS[f][:, S:TOK], ACT.Copy)
                act.drain().then_inc(sem("pu"), 1)
                for gi in range(4):
                    act.wait_ge(sem("pmap"), l * PER["pmap"] + gi + 1)
                    A_(brT[:, 1, gi, 0:TW(l)], PS[gi][:, 0:TW(l)], ACT.Copy, scale=pcol[l][:, 96 + gi:97 + gi])
                phase_end(act, ph + 9)

                with act.Fori(0, 3) as bi:
                    for f in range(KD):
                        act.wait_ge(sem("mg_mm"), l * PER["mg_mm"] + bi * KD + (f + 1))
                        act.wait_ge(sem("mg_free"), l * PER["mg_free"] + bi * KD + (f + 1))
                        A_(sg[f % 2][:, 0:TW(l)], PS[(f % 2) * 2 + 1][:, 0:TW(l)], ACT.Sigmoid).then_inc(sem("mg_sg"), 1)
                phase_end(act, ph + 10)

                def put_rows(which):
                    for s in range(2):
                        act.wait_ge(sem(f"grow{which}_{l}"), s + 1)
                        i = A_(grow[:, s, :], PS[s][:, :], ACT.Copy)
                    i.then_inc(sem(f"growS{which}_{l}"), 1)
                put_rows(0)
                for t in range(nt(l)):
                    act.wait_ge(sem("y"), l * PER["y"] + t + 1)
                    link(A_(yjunk, PS[2 + t % 2][:, :], ACT.Square, accum_out=ss[:, t:t + 1]))
                    act.drain()
                    A_(ss[:, t:t + 1], ss[:, t:t + 1], ACT.Sqrt, bias=epsc, scale=1.0 / D).then_inc(sem("yss"), 1)
                phase_end(act, ph + 11)

                squares("n2", nt(l), x_sb)
                norm_cols("n2", nt(l), h2T, 1)
                act.wait_ge(sem("asub"), l * PER["asub"] + 1)
                A_(aexp[:, 0:nt(l)], aexp[:, 0:nt(l)], ACT.Exp).then_inc(sem("aexp"), 1)
                phase_end(act, ph + 12)

                ns = nslot[l]
                act.drain().then_inc(sem("ytm"), 1)
                with act.Fori(0, NE) as e:
                    for half in range(2):
                        act.wait_ge(sem("unit_done"), l * PER["unit_done"] + 6 * e + (2 * half + 1))
                        act.wait_ge(sem("hid"), l * PER["hid"] + 2 * e + (half + 1))
                        A_(gsil[:, 0:4 * ns], bank(2 + 2 * half)[:, 0:4 * ns], ACT.Silu).then_inc(sem("gsil"), 1)
                    for half in range(2):
                        act.wait_ge(sem("unit_done"), l * PER["unit_done"] + 6 * e + (5 + half))
                        A_(yfm[:, 4 * half:4 * half + 4, 0:ns],
                           bank(2 + half)[:, 0:4 * ns].rearrange("p (f c) -> p f c", f=4), ACT.Copy)\
                            .then_inc(sem("yfm"), 1)
                    act.wait_ge(sem("y_T"), l * PER["y_T"] + e + 1)
                    act.wait_ge(sem("ig_free"), l * PER["ig_free"] + e + 1)
                    A_(ytm[0:ns, :], PS[3][0:ns, :], ACT.Copy, scale=gcur[0:ns, :]).then_inc(sem("ytm"), 1)
                phase_end(act, ph + 13)
                put_rows(1)
                act.wait_ge(sem("moe_in"), l * PER["moe_in"] + 16)
                squares("n3", nt(l), xn)

        @block.vector
        def _(dve):
            V = nc.vector
            n_link = [0]

            def link(ins):
                n_link[0] += 1
                ins.then_inc(sem("dve_link"), 1)
                dve.wait_ge(sem("dve_link"), n_link[0])

            V.memset(epsc, EPS)
            V.memset(ones[:, :], 1.0).then_inc(sem("ones_set"), 1)
            dve.wait_ge(sem("const_in"), 16)
            for l in range(DEPTH):
                ph = NPH * l
                first = l == 0
                dve.wait_ge(sem("stage_T"), l + 1)
                link(V.tensor_copy(pcol[l], bank(0)[:, 0:NP_ROWS]))
                dve.sem_inc(sem("pcol"), 1)
                dve.wait_ge(sem("ada_done"), l * PER["ada_done"] + 12)
                link(V.tensor_tensor(modc, bank(1)[:, 0:96].rearrange("p (m s) -> p m s", s=2),
                                     pcol[l][:, 48:96].unsqueeze(2).to_broadcast([P, 48, 2]), ALU.add))
                for i, (sh, sc, gt, g_in, g_out) in enumerate(((0, 1, 2, 0, 1), (3, 4, 5, 2, 3))):
                    gcol = pcol[l][:, 16:48].rearrange("p (g k) -> p g k", g=4)
                    V.tensor_copy(cS[i], modc[:, sh * 8:sh * 8 + 8, :])
                    link(V.tensor_scalar(cA[i], modc[:, sc * 8:sc * 8 + 8, :], 1.0, None, ALU.add))
                    link(V.tensor_tensor(cA[i], cA[i], gcol[:, g_in, :].unsqueeze(2).to_broadcast([P, 8, 2]), ALU.mult))
                    V.tensor_tensor(cG[i], modc[:, gt * 8:gt * 8 + 8, :],
                                    gcol[:, g_out, :].unsqueeze(2).to_broadcast([P, 8, 2]), ALU.mult)
                phase_end(dve, ph + 1)

                def norm_cols(tag, tiles, dst, which):
                    dve.wait_ge(sem(f"{tag}_ss{l}"), 1)
                    link(V.reciprocal(rstd[:, 0:tiles], ss[:, 0:tiles]))
                    dve.sem_inc(sem(f"{tag}_rstd{l}"), 1)
                    for t in range(1, tiles, 2):
                        V.tensor_scalar(xn[:, t, :], x_sb[:, t, :], rstd[:, t:t + 1], None, ALU.mult)\
                            .then_inc(sem(f"{tag}_xn{l}"), 1)
                    if tiles > LT:
                        for k in range(KD):
                            dve.wait_ge(sem(f"{tag}_T{l}"), k + 1)
                            V.tensor_scalar(dst[:, k, S:TOK], PS[k % 4][:, S:TOK], cA[which][:, k, 1:2],
                                            cS[which][:, k, 1:2], ALU.mult, ALU.add).then_inc(sem(f"{tag}_colC{l}"), 1)
                norm_cols("n1", NT, hT, 0)
                phase_end(dve, ph + 2)

                V.memset(v_ext[:, :, :, DV:DV + 1], 1.0)
                for t in range(LT):
                    dve.wait_ge(sem("proj_out"), l * PER["proj_out"] + t + 1)
                    qk = qk_tm[:, t, :].rearrange("p (h d) -> p h d", d=DK)
                    cos = cst[:, CCOS + t * DK:CCOS + (t + 1) * DK]
                    sin = cst[:, CSIN + t * DK:CSIN + (t + 1) * DK]
                    V.tensor_tensor(t_rope[0].rearrange("p (h d) -> p h d", d=DK), qk,
                                    cos.unsqueeze(1).to_broadcast([P, 8, DK]), ALU.mult)
                    x4 = qk_tm[:, t, :].rearrange("p (h r s d) -> p h r s d", h=8, r=2, s=2)
                    t4 = t_rope[1].rearrange("p (h r s d) -> p h r s d", h=8, r=2, s=2)
                    s4 = sin.rearrange("p (r s d) -> p r s d", r=2, s=2)
                    for s in range(2):
                        i = V.tensor_tensor(t4[:, :, :, s, :], x4[:, :, :, 1 - s, :],
                                            s4[:, :, s, :].unsqueeze(1).to_broadcast([P, 8, 2, 16]), ALU.mult)
                    link(i)
                    link(V.tensor_tensor(qk_tm[:, t, :], t_rope[0], t_rope[1], ALU.add))
                dve.wait_ge(sem("proj"), l * PER["proj"] + 13)
                dve.wait_ge(sem(f"gw_in"), 48 * (l + 1))
                link(V.tensor_tensor(gates, bank(4)[:, 0:96].rearrange("p (c g) -> p c g", c=NT),
                                     gbias.unsqueeze(1).to_broadcast([P, NT, 16]), ALU.add))
                phase_end(dve, ph + 3)

                g5 = gates.rearrange("p c (r i h) -> p r i c h", r=2, i=2)
                for r in range(2):
                    i = V.scalar_tensor_tensor(gt1[:, r], g5[:, r, 1], -1.0, g5[:, r, 1], ALU.mult, ALU.max)
                i.then_inc(sem("fabs"), 1)
                for r in range(2):
                    V.tensor_scalar(lf[:, r], g5[:, r, 1], 0.0, None, ALU.min)
                dve.wait_ge(sem("softp"), l * PER["softp"] + 1)
                dve.drain()
                V.tensor_tensor(lf, lf, gt1, ALU.subtract).then_inc(sem("lf"), 1)
                dve.wait_ge(sem("gsum"), l * PER["gsum"] + 1)
                V.tensor_copy(gbl.rearrange("p r c h -> p (r c h)"), bank(0)[:, 48:96])
                link(V.tensor_copy(gb.rearrange("p r c h -> p (r c h)"), bank(0)[:, 0:48]))
                for r in range(2):
                    i = V.tensor_tensor(ga[:, r], g5[:, r, 0], gb[:, r], ALU.subtract)
                i.then_inc(sem("ga"), 1)
                n = 0
                for r in range(2):
                    for c in range(NT):
                        dve.wait_ge(sem("arow"), l * PER["arow"] + n + 1)
                        b4 = bank(1 + n % 2).rearrange("p (h s) -> p h s", h=MH)
                        V.tensor_reduce(amax[:, r, c, :], b4, AX.X, ALU.max)
                        if n:
                            dve.wait_ge(sem("amax"), l * PER["amax"] + n)
                        d4 = dmat.rearrange("p (h s) -> p h s", h=MH)
                        link(V.tensor_tensor(d4, b4, mask_d[r].unsqueeze(1).to_broadcast([P, MH, P]), ALU.add))
                        V.tensor_reduce(cmax[:, r, c, :], d4, AX.X, ALU.max).then_inc(sem("amax"), 1)
                        n += 1
                for r in range(2):
                    order = (FW, BWD)[r]
                    link(V.memset(mprev[:, r, order[0], :], NEG))
                    for st in range(6):
                        c = order[st]
                        link(V.tensor_tensor(mlast[:, r, c, :], mprev[:, r, c, :], amax[:, r, c, :], ALU.max))
                        if st < 5:
                            link(V.tensor_tensor(mprev[:, r, order[st + 1], :], gbl[:, r, c, :], mlast[:, r, c, :], ALU.add))
                link(V.tensor_tensor(mt, mprev, cmax, ALU.max))
                V.tensor_tensor(xp0, mprev, mt, ALU.subtract)
                V.tensor_tensor(xp1, ga, mlast, ALU.subtract)
                V.tensor_tensor(xp2, mprev, mlast, ALU.subtract)
                link(V.tensor_tensor(xp3, gb, mt, ALU.add))
                link(V.tensor_scalar(xp3, xp3, -1.0, None, ALU.mult))
                dve.sem_inc(sem("gexp"), 1)
                V.memset(hsum[:, 0:nt(l), :], 0.0)
                link(V.memset(Cst, 0.0))
                dve.sem_inc(sem("m_C0"), 1)
                phase_end(dve, ph + 4)

                def two(ps, n):
                    return ps[:, :].rearrange("p (q x) -> p q x", q=2)[:, :, 0:2 * n].rearrange("p q (g n) -> p q g n", g=2)

                def by_parity(row):
                    return row.rearrange("p (g q n) -> p q g n", g=2, q=2)

                def cols(v):
                    return v.rearrange("p (g q) -> p q g", g=2)
                u = 0
                for st in range(6):
                    for r in range(2):
                        c = (FW, BWD)[r][st]
                        d4 = dmat.rearrange("p (h s) -> p h s", h=MH)
                        if c < nt(l):
                            dve.wait_ge(sem("m_arow"), l * PER["m_arow"] + u + 1)
                            link(V.tensor_tensor(d4, bank(0).rearrange("p (h s) -> p h s", h=MH),
                                                 mask_d[r].unsqueeze(1).to_broadcast([P, MH, P]), ALU.add))
                            V.tensor_tensor(d4, d4, mt[:, r, c, :].unsqueeze(2).to_broadcast([P, MH, P]), ALU.subtract)\
                                .then_inc(sem("m_dm"), 1)
                            dve.wait_ge(sem("m_s"), l * PER["m_s"] + u + 1)
                            dve.wait_ge(sem("m_D"), l * PER["m_D"] + u + 1)
                            V.tensor_tensor(by_parity(sd), two(PS[2], P), by_parity(dmat), ALU.mult).then_inc(sem("m_sd"), 1)
                            dve.wait_ge(sem("m_qc"), l * PER["m_qc"] + u + 1)

                            link(V.tensor_tensor(qcs, two(PS[1], 129), cols(xp0[:, r, c, :]).unsqueeze(3).to_broadcast([P, 2, 2, 129]), ALU.mult))
                            dve.wait_ge(sem("m_num"), l * PER["m_num"] + u + 1)
                            link(V.tensor_tensor(nd, qcs, two(PS[2], 129), ALU.add))
                            dn2 = dn.rearrange("p (q g) -> p q g", q=2)
                            link(V.scalar_tensor_tensor(dn2, nd[:, :, :, 128], -1.0,
                                                        nd[:, :, :, 128], ALU.mult, ALU.max))
                            link(V.tensor_tensor(dn2, dn2, cols(xp3[:, r, c, :]), ALU.max))
                            link(V.reciprocal(rden, dn))
                            link(V.tensor_tensor(by_parity(htmp), nd[:, :, :, 0:128], rden.rearrange("p (q g) -> p q g", q=2)
                                                 .unsqueeze(3).to_broadcast([P, 2, 2, 128]), ALU.mult))
                            V.tensor_tensor(hsum[:, c, :], hsum[:, c, :], htmp, ALU.add).then_inc(sem("m_h"), 1)
                            u += 1
                        if st < 5:
                            dve.wait_ge(sem("m_kv"), l * PER["m_kv"] + 2 * st + r + 1)
                            for q in range(2):
                                V.tensor_tensor(Cdec[64 * q:64 * q + 64], Cst[64 * q:64 * q + 64, r],
                                                xp2[64 * q:64 * q + 64, r, c, q::2].unsqueeze(2).to_broadcast([64, 2, 129]),
                                                ALU.mult)
                            dve.drain()
                            V.tensor_tensor(Cst[:, r], Cdec, PS[3][:, 0:258].rearrange("p (g n) -> p g n", g=2), ALU.add)\
                                .then_inc(sem("m_C"), 1)
                phase_end(dve, ph + 5)
                for t in range(nt(l)):
                    if t:
                        dve.wait_ge(sem("mtr"), l * PER["mtr"] + t)
                    hs = hsum[:, t, :].rearrange("p (h n) -> p h n", h=MH)
                    link(V.tensor_tensor(htmp, hsum[:, t, :], hsum[:, t, :], ALU.mult))
                    V.tensor_reduce(hss, htmp.rearrange("p (h n) -> p h n", h=MH), AX.X, ALU.add).then_inc(sem("hss"), 1)
                    dve.wait_ge(sem("hroot"), l * PER["hroot"] + t + 1)
                    link(V.reciprocal(hrr, hss))
                    link(V.tensor_tensor(hs, hs, hrr.unsqueeze(2).to_broadcast([P, MH, DV]), ALU.mult))
                    dve.wait_ge(sem("osig"), l * PER["osig"] + t + 1)
                    V.tensor_tensor(htmp, hsum[:, t, :], osig, ALU.mult).then_inc(sem("hfin"), 1)
                phase_end(dve, ph + 6)
                phase_end(dve, ph + 7)

                us = att_units(l)
                ng = len(us) // 4

                def fin(grp):
                    kind, hg, b, _ = us[grp * 4]
                    dve.wait_ge(sem("a_otr"), l * PER["a_otr"] + grp + 1)
                    src = bank(6)[:, 0:256]
                    if kind == "L":
                        dst = brT[:, 2, 2 * hg:2 * hg + 2, 0:S].rearrange("p f (r b q) -> p f r b q", r=ROWS, b=NB)[:, :, :, b, ::-1]
                        src = src.rearrange("p (f r q) -> p f r q", f=2, r=ROWS)
                    else:
                        dst = brT[:, 2, 2 * hg:2 * hg + 2, S + b * P:S + (b + 1) * P]
                        src = src.rearrange("p (f q) -> p f q", f=2)
                    V.tensor_copy(dst, src).then_inc(sem("a_fin"), 1)

                def out_rows(grp):
                    dve.wait_ge(sem("a_pv"), l * PER["a_pv"] + 4 * grp + 4)
                    if grp >= 2:
                        dve.wait_ge(sem("a_otr"), l * PER["a_otr"] + grp - 1)
                    link(V.reciprocal(rrec[:, (grp % 2) * 4:(grp % 2) * 4 + 4], rsum[:, (grp % 2) * 4:(grp % 2) * 4 + 4]))
                    V.tensor_tensor(o_tm[grp % 2].rearrange("p (h n) -> p h n", h=4),
                                    bank(4 + grp % 2)[:, 0:256].rearrange("p (h n) -> p h n", h=4),
                                    rrec[:, (grp % 2) * 4:(grp % 2) * 4 + 4].unsqueeze(2).to_broadcast([P, 4, 64]), ALU.mult)\
                        .then_inc(sem("a_o"), 1)
                for n, (kind, hg, b, h4) in enumerate(us):
                    dve.wait_ge(sem("a_s"), l * PER["a_s"] + n + 1)
                    sp = bank(n % 2)
                    if n >= 4:
                        dve.wait_ge(sem("a_exp"), l * PER["a_exp"] + n - 3)
                    if kind == "L":
                        dve.wait_ge(sem("a_bm"), l * PER["a_bm"] + n + 1)
                        s3 = sp[:, 0:256].rearrange("p (j k) -> p j k", j=ROWS)
                        link(V.tensor_tensor(s3, s3, bm[n % 3], ALU.add))
                        V.tensor_reduce(nmx[:, n % 4:n % 4 + 1], sp, AX.X, ALU.max, negate=True).then_inc(sem("a_max"), 1)
                    else:
                        V.tensor_reduce(nmx[:, n % 4:n % 4 + 1], sp[:, 256:512], AX.X, ALU.max, negate=True)\
                            .then_inc(sem("a_max"), 1)
                    if n % 4 == 1 and n > 4:
                        out_rows(n // 4 - 1)
                    if n % 4 == 2 and n > 4:
                        fin(n // 4 - 1)
                out_rows(ng - 1)
                fin(ng - 1)
                phase_end(dve, ph + 8)

                V.memset(pu[:, :, 0:LCOL], 0.0)
                V.memset(pu[:, :, LCOL + S:CCOL], 0.0)
                if first:
                    V.memset(pu[:, :, CCOL + CTX:PADW], 0.0)
                else:
                    V.memset(pu[:, :, CCOL:PADW], 0.0)
                dve.drain()
                dve.wait_ge(sem("pu"), l * PER["pu"] + 1)
                link(V.tensor_tensor(pA[:, :, 0:PADW - 1], pu[:, :, 0:PADW - 1], pu[:, :, 1:PADW], ALU.add))
                link(V.tensor_tensor(pB[:, 1:4, 0:PADW - 3], pA[:, 1:4, 0:PADW - 3], pA[:, 1:4, 2:PADW - 1], ALU.add))
                link(V.tensor_tensor(pA[:, 2:4, 0:PADW - 7], pB[:, 2:4, 0:PADW - 7], pB[:, 2:4, 4:PADW - 3], ALU.add))
                link(V.tensor_tensor(pB[:, 3:4, 0:PADW - 15], pA[:, 3:4, 0:PADW - 15], pA[:, 3:4, 8:PADW - 7], ALU.add))
                for gi, w in enumerate(WINDOWS):
                    src = (pA, pB)[gi % 2]
                    for _, base, cnt in [(0, LCOL, S)] + ([(1, CCOL, CTX)] if first else []):
                        for side, p0 in enumerate((base, base + cnt - 8)):
                            e0 = CED + gi * 16 + side * 8
                            lo = p0 - w // 2
                            V.tensor_tensor(src[:, gi, lo:lo + 8], src[:, gi, lo:lo + 8], cst[:, e0:e0 + 8], ALU.mult)
                dve.drain()
                for gi, w in enumerate(WINDOWS):
                    src = (pA, pB)[gi % 2]
                    for _, base, t0, cnt in [(0, LCOL, 0, S)] + ([(1, CCOL, S, CTX)] if first else []):
                        lo = base - w // 2
                        i = V.scalar_tensor_tensor(pin[:, gi, t0:t0 + cnt], src[:, gi, lo:lo + cnt], 1.0 / w,
                                                   pu[:, gi, base:base + cnt], ALU.mult, ALU.subtract)
                    i.then_inc(sem("pin"), 1)
                phase_end(dve, ph + 9)

                dve.drain().then_inc(sem("mg_free"), 2)
                with dve.Fori(0, 3) as bi:
                    for f in range(KD):
                        dve.wait_ge(sem("mg_sg"), l * PER["mg_sg"] + bi * KD + (f + 1))
                        dve.wait_ge(sem("mg_tfree"), l * PER["mg_tfree"] + bi * KD + (f + 1))
                        V.tensor_tensor(mtmp[f % 2][:, 0:TW(l)], sg[f % 2][:, 0:TW(l)], PS[(f % 2) * 2][:, 0:TW(l)],
                                        ALU.mult).then_inc(sem("mg_free"), 1)
                phase_end(dve, ph + 10)

                dve.drain().then_inc(sem("y_free"), 2)
                dve.wait_ge(sem(f"growS0_{l}"), 1)
                for t in range(nt(l)):
                    dve.wait_ge(sem("yss"), l * PER["yss"] + t + 1)
                    link(V.reciprocal(rstd[:, t:t + 1], ss[:, t:t + 1]))
                    link(V.scalar_tensor_tensor(ytmp[t % 2], PS[2 + t % 2][:, :], rstd[:, t:t + 1], grow[:, t // LT, :],
                                                ALU.mult, ALU.mult))
                    V.tensor_tensor(x_sb[:, t, :], x_sb[:, t, :], ytmp[t % 2], ALU.add).then_inc(sem("y_free"), 1)
                phase_end(dve, ph + 11)

                norm_cols("n2", nt(l), h2T, 1)
                n_t = nt(l)
                dve.wait_ge(sem("logit"), l * PER["logit"] + 1)
                lg = bank(0)[:, 0:n_t * NE].rearrange("p (t e) -> p t e", t=n_t)
                link(V.tensor_reduce(asum[:, 0:n_t], lg, AX.X, ALU.max))
                V.tensor_tensor(aexp[:, 0:n_t], lg, asum[:, 0:n_t].unsqueeze(2).to_broadcast([P, n_t, NE]), ALU.subtract)\
                    .then_inc(sem("asub"), 1)
                dve.wait_ge(sem("aexp"), l * PER["aexp"] + 1)
                link(V.tensor_reduce(asum[:, 0:n_t], aexp[:, 0:n_t], AX.X, ALU.add))
                link(V.reciprocal(arec[:, 0:n_t], asum[:, 0:n_t]))
                V.tensor_tensor(affn[:, 0:n_t], aexp[:, 0:n_t], arec[:, 0:n_t].unsqueeze(2).to_broadcast([P, n_t, NE]),
                                ALU.mult).then_inc(sem("aff"), 1)
                dve.wait_ge(sem("afftr"), l * PER["afftr"] + 1)
                link(V.tensor_copy(affT[:, 0:TW(l)], PS[1][0:NE, 0:TW(l)]))
                for s, t0, cnt in streams(l):
                    rows = affT[:, t0:t0 + cnt]
                    for j in range(cnt // 64):
                        o8 = s * 64 + 8 * j
                        link(V.max(tv[:, o8:o8 + 8], rows))
                        V.max_index(ti[:, o8:o8 + 8], tv[:, o8:o8 + 8], rows)
                        dve.drain()
                        if j < cnt // 64 - 1:
                            link(V.match_replace(rows, tv[:, o8:o8 + 8], rows, -1.0))
                link(V.tensor_copy(tif[:, 0:nslot[l]], ti[:, 0:nslot[l]]))
                if first:
                    link(V.tensor_scalar(tif[:, 64:96], tif[:, 64:96], float(S), None, ALU.add))
                dve.sem_inc(sem("top"), 1)
                dve.wait_ge(sem("toptr"), l * PER["toptr"] + 1)
                ns = nslot[l]
                V.tensor_copy(gval[0:ns, 0:NE], bank(1)[0:ns, 0:NE])
                V.tensor_copy(gidx[0:ns, 0:NE], bank(1)[0:ns, 16:16 + NE])
                link(V.tensor_copy(gidx[0:ns, NE:NE + 1], bank(1)[0:ns, 16 + NE - 1:16 + NE]))
                link(V.tensor_copy(icur[0:ns, :], gidx[0:ns, 0:1]))
                phase_end(dve, ph + 12)

                def modulate(tag_e):
                    ps = PS[0][:, :].rearrange("p (k c) -> p k c", k=KD)
                    for s, c0, cw in [(0, 0, 64)] + ([(1, 64, 32)] if first else []):
                        V.tensor_tensor(xeT[:, :, c0:c0 + cw], ps[:, :, c0:c0 + cw],
                                        cA[1][:, :, s:s + 1].to_broadcast([P, KD, cw]), ALU.mult)
                    dve.drain()
                    for s, c0, cw in [(0, 0, 64)] + ([(1, 64, 32)] if first else []):
                        i = V.tensor_tensor(xeT[:, :, c0:c0 + cw], xeT[:, :, c0:c0 + cw],
                                            cS[1][:, :, s:s + 1].to_broadcast([P, KD, cw]), ALU.add)
                    i.then_inc(sem("xeT"), 1)
                dve.drain().then_inc(sem("hid"), 1)
                dve.wait_ge(sem("xe_T"), l * PER["xe_T"] + 1)
                modulate(0)
                with dve.Fori(0, NE) as e:
                    V.tensor_copy(gcur[0:ns, :], gval[0:ns, bass.ds(e, 1)])
                    dve.wait_ge(sem("ig_free"), l * PER["ig_free"] + e + 1)
                    V.tensor_copy(iprev[0:ns, :], gidx[0:ns, bass.ds(e, 1)])
                    V.tensor_copy(icur[0:ns, :], gidx[0:ns, bass.ds(e + 1, 1)]).then_inc(sem("icur"), 1)
                    for half in range(2):
                        dve.wait_ge(sem("unit_done"), l * PER["unit_done"] + 6 * e + (2 * half + 2))
                        dve.wait_ge(sem("gsil"), l * PER["gsil"] + 2 * e + (half + 1))
                        V.tensor_tensor(hid[:, 4 * half:4 * half + 4, 0:ns],
                                        gsil[:, 0:4 * ns].rearrange("p (f c) -> p f c", f=4),
                                        bank(3 + 2 * half)[:, 0:4 * ns].rearrange("p (f c) -> p f c", f=4), ALU.mult)\
                            .then_inc(sem("hid"), 1)
                    dve.wait_ge(sem("xe_T"), l * PER["xe_T"] + e + 2)
                    modulate(e)
                    dve.wait_ge(sem("ytm"), l * PER["ytm"] + e + 2)
                phase_end(dve, ph + 13)

                dve.wait_ge(sem(f"growS1_{l}"), 1)
                dve.wait_ge(sem(f"n3_ss{l}"), 1)
                link(V.reciprocal(rstd[:, 0:n_t], ss[:, 0:n_t]))
                for t in range(n_t):
                    link(V.scalar_tensor_tensor(xn[:, t, :], xn[:, t, :], rstd[:, t:t + 1], grow[:, t // LT, :],
                                                ALU.mult, ALU.mult))
                    link(V.tensor_tensor(x_sb[:, t, :], x_sb[:, t, :], xn[:, t, :], ALU.add))
                dve.sem_inc(sem(f"x_done{l}"), 1)

        @block.gpsimd
        def _(pool):
            G = nc.gpsimd
            pool.wait_ge(sem("const_in"), 16)
            for l in range(DEPTH):
                ph = NPH * l
                first = l == 0
                if not first:
                    pool.wait_ge(sem(f"x_done{l - 1}"), 1)
                for n in range(1, 5):
                    phase_end(pool, ph + n)
                for st in range(5):
                    for r in range(2):
                        c = (FW, BWD)[r][st]
                        if 2 * st + r:
                            pool.wait_ge(sem("m_kv"), l * PER["m_kv"] + 2 * st + r)
                        G.tensor_tensor(vws, v_ext[:, c], xp1[:, r, c, :].unsqueeze(2).to_broadcast([P, MH, 129]), ALU.mult)\
                            .then_inc(sem("m_vw"), 1)
                for n in range(5, 7):
                    phase_end(pool, ph + n)
                for t in range(LT):
                    pool.wait_ge(sem("np_out"), l * PER["np_out"] + 2 * KB + t + 1)
                    pool.dma_start(v_dram[l][t * P:(t + 1) * P, :], vstage[t % 2]).then_inc(sem(f"v_out{t % 2}_{l}"), 16)
                for i in range(2):
                    pool.wait_ge(sem(f"v_out{i}_{l}"), 32)
                phase_end(pool, ph + 7)

                def load_tables(hg):
                    for r in range(ROWS):
                        src = A["rpb"]
                        src = bass.AP(src.tensor, src.offset + (l * NH + hg * 4) * 15 * RPW + (7 - r) * RPW,
                                      [[1, QC], [15 * RPW, 4], [1, 496]])
                        pool.dma_start(tab[r * QC:(r + 1) * QC, :, 0:496], src).then_inc(sem("tab_in"), 16)

                def load_values(grp):
                    b = grp % NB
                    if grp >= 2:
                        pool.wait_ge(sem("a_pv"), l * PER["a_pv"] + 4 * (grp - 1))
                    rows = v_dram[l].rearrange("(j c) n -> j c n", c=GW)
                    for j in range(ROWS):
                        pool.dma_start(vw[grp % 2][(j % 4) * KC:(j % 4 + 1) * KC, j // 4, :],
                                       rows[j, KSTART[b]:KSTART[b] + KC, :]).then_inc(sem(f"vw_in{grp % 2}_{l}"), 16)
                load_values(0)
                load_values(1)
                for n, (kind, hg, b, h4) in enumerate(att_units(l)):
                    if kind != "L":
                        continue
                    if n % 16 == 0:
                        if n:
                            pool.wait_ge(sem("a_bm"), l * PER["a_bm"] + n)
                        load_tables(hg)
                    if n % 4 == 0 and n >= 4 and n // 4 + 1 < 8:
                        load_values(n // 4 + 1)
                    if n % 16 == 0:
                        pool.wait_ge(sem("tab_in"), l * PER["tab_in"] + 128 * (hg + 1))
                    if n >= 3:
                        pool.wait_ge(sem("a_max"), l * PER["a_max"] + n - 2)
                    off = KSTART[b] - QC * b + 16
                    t3 = tab[:, h4, :].rearrange("p (j w) -> p j w", j=ROWS)[:, :, off:off + KC]
                    G.tensor_tensor(bm[n % 3], t3, cst[:, CNM + b * KC:CNM + (b + 1) * KC].unsqueeze(1)
                                    .to_broadcast([P, ROWS, KC]), ALU.add).then_inc(sem("a_bm"), 1)
                phase_end(pool, ph + 8)
                pool.dma_start(pw, A["pool_w"][l].rearrange("g p n -> p g n")).then_inc(sem("pw_in"), 16)
                phase_end(pool, ph + 9)
                G.memset(acc[:, :, 0:TW(l)], 0.0)
                pool.drain().then_inc(sem("mg_tfree"), 2)
                with pool.Fori(0, 3) as bi:
                    for f in range(KD):
                        pool.wait_ge(sem("mg_free"), l * PER["mg_free"] + bi * KD + (f + 3))
                        G.tensor_tensor(acc[:, f, 0:TW(l)], acc[:, f, 0:TW(l)], mtmp[f % 2][:, 0:TW(l)], ALU.add)\
                            .then_inc(sem("mg_tfree"), 1)
                for n in range(10, 12):
                    phase_end(pool, ph + n)
                pool.wait_ge(sem(f"n2_xn{l}"), nt(l))
                pool.dma_start(xn_dram[l][0:TW(l), :].rearrange("(t p) d -> p t d", p=P), xn[:, 0:nt(l), :])\
                    .then_inc(sem("xn_out"), 16)
                phase_end(pool, ph + 12)
                ns = nslot[l]
                pool.wait_ge(sem("xn_out"), l * PER["xn_out"] + 16)
                pool.wait_ge(sem("zero_out"), 16 * NT * (l + 1))

                def gather():
                    G.indirect_dma_start(xe[0:ns, :], None, xn_dram[l][0:TW(l), :],
                                         bass.IndirectOffsetOnAxis(ap=icur[0:ns, 0:1], axis=0)).then_inc(sem("xe_in"), 16)
                gather()
                pool.wait_ge(sem("xe_in"), l * PER["xe_in"] + 16)
                pool.drain().then_inc(sem("ig_free"), 1)
                with pool.Fori(0, NE) as e:
                    pool.wait_ge(sem("icur"), l * PER["icur"] + e + 1)
                    pool.wait_ge(sem("xe_T"), l * PER["xe_T"] + e + 1)
                    pool.sem_inc(sem("pool_turn"), 1)
                    gather()
                    pool.wait_ge(sem("ytm"), l * PER["ytm"] + e + 2)
                    pool.sem_inc(sem("pool_turn"), 1)
                    G.indirect_dma_start(moe_dram[l][0:TW(l), :], bass.IndirectOffsetOnAxis(ap=iprev[0:ns, 0:1], axis=0),
                                         ytm[0:ns, :], None, compute_op=ALU.add).then_inc(sem("y_added"), 16)
                    pool.wait_ge(sem("xe_in"), l * PER["xe_in"] + 16 * e + 32)
                    pool.wait_ge(sem("y_added"), l * PER["y_added"] + 16 * e + 16)
                    pool.sem_inc(sem("ig_free"), 1)
                pool.dma_start(xn[:, 0:nt(l), :], moe_dram[l][0:TW(l), :].rearrange("(t p) d -> p t d", p=P))\
                    .then_inc(sem("moe_in"), 16)
                phase_end(pool, ph + 13)

        @block.sync
        def _(sp):
            last = [None] * 6

            def load(key):
                src, slot, count, _, _ = units[key]
                if last[slot]:
                    sp.wait_ge(sem(last[slot][0]), last[slot][1])
                nk = src.shape[1]
                sp.dma_start(slot_ap(slot).rearrange("p (k n) -> p k n", k=nk), src).then_inc(w_ready(slot), 16)
                last[slot] = released[key]

            for l in range(DEPTH):
                if l == 0:
                    sp.dma_start(cst[:, :], A["tables"]).then_inc(sem("const_in"), 16)
                rows = ((0, 8, A["c"][0].rearrange("(k p) -> k p", p=P)),
                        (8, 16, A["c_ctx"].rearrange("(k p) -> k p", p=P)),
                        (16, 48, A["norm_gain"][l].rearrange("g (k p) -> (g k) p", p=P)),
                        (48, 96, A["ada_b"][l].rearrange("(k p) -> k p", p=P)),
                        (96, 100, A["pool_scale"][l].rearrange("(k p) -> k p", p=P)))
                for r0, r1, src in rows:
                    sp.dma_start(stage[l][r0:r1, :], src).then_inc(sem("stage_in"), 16)
                if l == 0:
                    sp.dma_start(x_sb[:, 0:LT, :], A["x"][0].rearrange("(t p) d -> p t d", p=P)).then_inc(sem("x_in"), 16)
                    sp.dma_start(x_sb[:, LT:NT, :], A["ctx"][0].rearrange("(t p) d -> p t d", p=P)).then_inc(sem("x_in"), 16)
                sp.dma_start(gw, w_in[l][:, C_G:C_G + 16].rearrange("(k p) n -> p k n", p=P)).then_inc(sem("gw_in"), 16)
                sp.dma_start(rw, A["router_w"][l].rearrange("(k p) n -> p k n", p=P)).then_inc(sem("gw_in"), 16)
                sp.dma_start(gbias, A["mlstm_gate_bias"][l].rearrange("(o g) h -> o (g h)", o=1).to_broadcast([P, 16]))\
                    .then_inc(sem("gw_in"), 16)
                for t in range(NT):
                    sp.dma_start(moe_dram[l][t * P:(t + 1) * P, :], A["zeros"]).then_inc(sem("zero_out"), 16)
                for key in units:
                    if key[0] == l:
                        load(key)


                exp_src = [(A["w_gate"], 0), (A["w_up"], 0), (A["w_gate"], 512), (A["w_up"], 512),
                           (A["w_down"], 0), (A["w_down"], 512)]

                def expert_unit(e, s):
                    w, c = exp_src[s]
                    sp.dma_start(slot_ap(s).rearrange("p (k n) -> p k n", k=KD),
                                 w[l][bass.ds(e, 1), :, c:c + 512].rearrange("o (k p) n -> p (o k) n", p=P))\
                        .then_inc(w_ready(s), 16)
                for s in range(6):
                    if s < 3:
                        sp.wait_ge(sem(last[s][0]), last[s][1])
                    elif s == 3:
                        sp.wait_ge(sem("phase"), 4 * (NPH * l + 10))
                    expert_unit(0, s)
                with sp.Fori(1, NE) as e:
                    for s in range(6):
                        sp.wait_ge(sem("unit_done"), l * PER["unit_done"] + 6 * e + (s - 5))
                        expert_unit(e, s)
                for s in range(6):
                    last[s] = ("unit_done", l * PER["unit_done"] + 6 * NE - 5 + s)
            sp.wait_ge(sem(f"x_done{DEPTH - 1}"), 1)
            sp.dma_start(out[0].rearrange("(t p) d -> p t d", p=P), x_sb[:, 0:LT, :]).then_inc(sem("out"), 16)
            sp.wait_ge(sem("out"), 16)


_INS = ["x", "c", "ctx", "c_ctx", "norm_gain", "ada_w", "ada_b", "w_in", "mlstm_gate_bias", "pool_w", "pool_scale",
        "w_branch", "w_out", "router_w", "w_gate", "w_up", "w_down"]


def kernel(**inputs):
    import numpy as np
    import concourse.bacc as bacc
    from concourse.bass_utils import run_bass_kernel_spmd

    nc = bacc.Bacc("TRN2", target_bir_lowering=False, num_devices=1)
    arrays = {n: np.ascontiguousarray(inputs[n]) for n in _INS}
    rpb = np.asarray(inputs["na_rpb"])
    wide = np.zeros(rpb.shape[:3] + (RPW,), rpb.dtype)
    wide[..., 16:16 + rpb.shape[3]] = rpb
    arrays["rpb"] = wide
    arrays["tables"] = constants()
    arrays["zeros"] = np.zeros((P, D), np.float32)
    args = {n: nc.dram_tensor(f"in_{n}", a.shape, F32, kind="ExternalInput").ap() for n, a in arrays.items()}
    out = nc.dram_tensor("out_0_dram", (1, S, D), F32, kind="ExternalOutput").ap()
    build(nc, args, out)
    r = run_bass_kernel_spmd(nc, [{f"in_{n}": a for n, a in arrays.items()}], core_ids=[0])
    return r.results[0]["out_0_dram"]
```

```python
import concourse.bass as bass
from concourse import mybir
from contextlib import ExitStack

F32 = mybir.dt.float32
U32 = mybir.dt.uint32
ALU = mybir.AluOpType
ACT = mybir.ActivationFunctionType
AX = mybir.AxisListType

D, S, CTX, DEPTH = 1024, 512, 256, 2
TOK = S + CTX
P = 128
KD = D // P
LT, CT = S // P, CTX // P
NT = LT + CT
BW = D // 2
KB = BW // P
MH, DV, DK = 4, 128, 64
NH, DH = 8, 64
GW, ROWS = 64, 8
NB, QC, KC = 4, 16, 32
KSTART = [0, 8, 24, 32]
WINDOWS = (2, 4, 8, 16)
NE, FF = 16, 1024
EPS = 1e-6
C_QK, C_V, C_O, C_G, C_PU, C_QN, C_KN, C_VN, C_BG = 0, 512, 1024, 1536, 1552, 2064, 2576, 3088, 3600
NEG = -1.0e30
PADW = 8 + S + 8 + CTX + 8
RPW = 64
LCOL, CCOL = 8, 8 + S + 8

CI, CU, CL, CMF, CMB, CNM, CED, CCOS, CSIN = 0, 128, 256, 384, 512, 640, 768, 832, 1088
CW = 1344


def constants():
    import numpy as np
    t = np.zeros((P, CW), np.float32)
    i = np.arange(P)
    t[:, CI:CI + P] = np.eye(P)
    t[:, CU:CU + P] = i[:, None] <= i[None, :]
    t[:, CL:CL + P] = i[:, None] >= i[None, :]
    t[:, CMF:CMF + P] = np.where(i[None, :] <= i[:, None], 0, NEG)
    t[:, CMB:CMB + P] = np.where(i[None, :] >= i[:, None], 0, NEG)
    for b in range(NB):
        qc = QC * b + QC - 1 - i % QC
        cs = np.clip(qc - 8, 0, GW - 16)
        kc = KSTART[b] + np.arange(KC)
        ok = (kc[None] >= cs[:, None]) & (kc[None] < cs[:, None] + 16)
        t[:, CNM + b * KC:CNM + (b + 1) * KC] = np.where(ok, 0, NEG)
    for g, w in enumerate(WINDOWS):
        for side, tt in enumerate((np.arange(8), np.arange(CTX - 8, CTX))):
            lo = np.clip(tt - w // 2, 0, CTX - 1)
            hi = np.clip(tt - w // 2 + w - 1, 0, CTX - 1)
            t[:, CED + g * 16 + side * 8:CED + g * 16 + side * 8 + 8] = w / (hi - lo + 1).astype(np.float32)
    half = DK // 2
    inv = (10000.0 ** (-np.arange(0, half, 2, dtype=np.float32) / half)).astype(np.float32)
    for lt in range(LT):
        tk = lt * P + i
        for part, pos in enumerate((tk // GW, tk % GW)):
            a = pos[:, None].astype(np.float32) * inv[None]
            c, s = np.cos(a), np.sin(a)
            o = lt * DK + part * 32
            t[:, CCOS + o:CCOS + o + 32] = np.concatenate([c, c], 1)
            t[:, CSIN + o:CSIN + o + 32] = np.concatenate([-s, s], 1)
    return t


def build(nc, A, out):
    ctx = ExitStack()
    with ctx:
        def sb(name, width, dt=F32, parts=P):
            return ctx.enter_context(nc.sbuf_tensor(name, [parts, width], dt))

        made = {}

        def sem(name):
            if name not in made:
                made[name] = ctx.enter_context(nc.semaphore(name))
            return made[name]

        def dram(name, shape):
            return nc.dram_tensor(name, shape, F32, kind="Internal").ap()

        SLOT = KD * 512
        x_sb = sb("x_sb", NT * D)[:, :].rearrange("p (t d) -> p t d", t=NT)
        ring_lo = sb("ring_lo", 3 * SLOT)
        ZW = 29000
        zone = sb("zone", ZW)
        cst = sb("cst", CW)
        ones = sb("ones", P)
        small = sb("small", 2992)

        def slot_ap(s):
            return ring_lo[:, s * SLOT:(s + 1) * SLOT] if s < 3 else zone[:, (s - 3) * SLOT:(s - 2) * SLOT]

        def cut(area, off, pattern=None, width=None, parts=P, **k):
            ap = area[0:parts, off:off + width]
            return ap.rearrange(pattern, **k) if pattern else ap

        mg_buf = [ring_lo[:, 6144:12288], ring_lo[:, 0:6144]]
        mg_wb = [b_[:, 0:2048].rearrange("p (k n) -> p k n", k=KB) for b_ in mg_buf]
        mg_wg = [b_[:, 2048:6144].rearrange("p (k n) -> p k n", k=KD) for b_ in mg_buf]

        ident = cst[:, CI:CI + P]
        tri_f, tri_b = cst[:, CU:CU + P], cst[:, CL:CL + P]
        mask_d = [cst[:, CMF:CMF + P], cst[:, CMB:CMB + P]]

        at = [0]

        def sm(width, pattern=None, **k):
            o = at[0]
            at[0] += width
            assert at[0] <= 2992
            return cut(small, o, pattern, width, **k)

        NP_ROWS = 100
        stage = [sm(P) for _ in range(DEPTH)]
        pcol = [sm(NP_ROWS) for _ in range(DEPTH)]
        csil = sm(KD * 32, "p (k m) -> p k m", k=KD)
        modc = [sm(96, "p (m s) -> p m s", m=48) for _ in range(DEPTH)]
        cA = [sm(16, "p (k s) -> p k s", k=KD) for _ in range(2)]
        cS = [sm(16, "p (k s) -> p k s", k=KD) for _ in range(2)]
        cG = [sm(16, "p (k s) -> p k s", k=KD) for _ in range(2)]
        ss, ssx, rstd = sm(NT), sm(NT), sm(NT)
        gw = sm(KD * 16, "p (k n) -> p k n", k=KD)
        rw = sm(KD * NE, "p (k n) -> p k n", k=KD)
        gbias = sm(16)
        gates = sm(NT * 16, "p (c g) -> p c g", c=NT)

        def g48(n=1):
            return [sm(48, "p (r c h) -> p r c h", r=2, c=NT) for _ in range(n)]

        lf, gb, ga, gbl, gt1, mprev, mlast, amax, cmax, mt, xp0, xp1, xp2, xp3 = g48(14)
        rden, dn = sm(4), sm(4)
        mx8 = sm(8)
        nmx = sm(4)
        rsum = sm(4)
        rrec = sm(4)
        hss, hrr = sm(4 * NT), sm(4 * NT)
        epsc = sm(1)

        hT = cut(zone, 0, "p (k t) -> p k t", 6144, k=KD)
        brT = cut(zone, 6144, "p (b k t) -> p b k t", 9216, b=3, k=KB)
        Z0 = 15360
        qk_tm = cut(zone, 9216, "p (c n) -> p c n", 3072, c=NT)
        hsum = cut(zone, 12288, "p (c n) -> p c n", 3072, c=NT)
        o = Z0
        v_ext = cut(zone, o, "p (c h n) -> p c h n", 3096, c=NT, h=MH); o += 3096
        qT = cut(zone, o, "p (g t) -> p g t", 1536, g=2); o += 1536
        kT = cut(zone, o, "p (g t) -> p g t", 1536, g=2); o += 1536
        Cst = cut(zone, o, "p (r g n) -> p r g n", 516, r=2, g=2); o += 516
        dmat = cut(zone, o, None, 512); o += 512
        sd = cut(zone, o, None, 512); o += 512
        sdT = cut(zone, o, None, 512); o += 512
        qcs = cut(zone, o, "p (g h n) -> p g h n", 516, g=2, h=2); o += 516
        nd = cut(zone, o, "p (g h n) -> p g h n", 516, g=2, h=2); o += 516
        vws = cut(zone, o, "p (h n) -> p h n", 516, h=MH); o += 516
        Cdec = cut(zone, o, "p (g n) -> p g n", 258, g=2); o += 258
        htmp = cut(zone, o, None, 512); o += 512
        osig = [cut(zone, o, None, 512), sdT]; o += 512
        hfin = [htmp, sd]
        t_rope = [cut(zone, o + 512 * i, None, 512) for i in range(2)]; o += 1024
        assert o <= ZW, o
        o = Z0
        qnL = cut(zone, o, "p (f b q) -> p f b q", 2048, f=KB, b=NB); o += 2048
        qnC = cut(zone, o, "p (f t) -> p f t", 1024, f=KB); o += 1024
        knT = cut(zone, o, "p (f t) -> p f t", 3072, f=KB); o += 3072
        vw = [cut(zone, 9216 + 1024 * i, "p (u n) -> p u n", 1024, u=2) for i in range(2)]
        vctx = cut(zone, 11264, "p (u n) -> p u n", 1024, u=2)
        tab = cut(zone, o, "p (h w) -> p h w", 2048, h=4); o += 2048
        bm = [cut(zone, o + 512 * i, "p (h j k) -> p h j k", 512, h=2, j=ROWS) for i in range(2)]; o += 1024
        vstage = [cut(zone, o + 512 * i, None, 512) for i in range(2)]
        pr = [[cut(zone, o + 1024 * i + 512 * q, None, 512) for q in range(2)] for i in range(2)]; o += 2048
        prT = [cut(zone, o + 512 * q, None, 512) for q in range(2)]; o += 1024
        dg = [[cut(zone, o + 256 * i + P * q, None, P) for q in range(2)] for i in range(2)]; o += 512
        assert o <= ZW, o
        modr = cut(zone, 26900, "p (u n) -> p u n", 1536, u=12)
        o = Z0
        pu = cut(zone, o, "p (g t) -> p g t", 4 * PADW, g=4); o += 4 * PADW
        pA = cut(zone, o, "p (g t) -> p g t", 4 * PADW, g=4); o += 4 * PADW
        pB = cut(zone, o, "p (g t) -> p g t", 4 * PADW, g=4); o += 4 * PADW
        pin = cut(zone, o, "p (g t) -> p g t", 4 * TOK, g=4); o += 4 * TOK
        pw = cut(zone, o, "p (g n) -> p g n", 512, g=4); o += 512
        assert o <= ZW, o
        acc = cut(zone, Z0, "p (f t) -> p f t", 6144, f=KD)
        sg = [cut(zone, 21504 + 768 * i, None, 768) for i in range(2)]
        mtmp = [cut(zone, 23040 + 768 * i, None, 768) for i in range(2)]
        grow = cut(zone, 26900, "p (s d) -> p s d", 2048, s=2)
        ytmp = [cut(zone, 21504 + 1024 * i, None, 1024) for i in range(2)]
        yjunk = cut(zone, 23552, None, 1024)
        xn = cut(zone, 12288, "p (t d) -> p t d", 6144, t=NT)
        h2T = cut(zone, 18432, "p (k t) -> p k t", 6144, k=KD)
        junk = cut(zone, 24600, None, 1024)
        affn = cut(zone, 24600, "p (t e) -> p t e", NT * NE, t=NT)
        affT = cut(zone, 24700, None, TOK, parts=NE)
        tv = cut(zone, 25500, None, 96, parts=NE)
        ti = cut(zone, 25600, None, 96, parts=NE).bitcast(U32)
        tif = cut(zone, 25700, None, 96, parts=NE)
        gidx = cut(zone, 25800, None, NE + 2).bitcast(U32)
        icur = cut(zone, 25820, None, 1).bitcast(U32)
        twide = cut(zone, 26100, "p (x g n) -> p x g n", 512, parts=NE, x=2, g=2)
        gval = cut(zone, 25822, "p (g e) -> p g e", 2 * NE, g=2)
        sidx = cut(zone, 25854, "p (g e) -> p g e", 2 * NE, g=2).bitcast(U32)
        gcur = cut(zone, 25886, None, 2)
        iprev = cut(zone, 25888, None, 2).bitcast(U32)
        aexp = cut(zone, 25900, "p (t e) -> p t e", NT * NE, t=NT)
        asum, arec = cut(zone, 26000, None, NT), cut(zone, 26010, None, NT)
        xe = cut(zone, 18432, None, 1024)
        xeT = cut(zone, 19456, "p (k c) -> p k c", 768, k=KD)
        gsil = cut(zone, 20224, None, 768)
        hidm = cut(zone, 20992, None, 768)
        hidL = cut(zone, 21760, "p (b g m) -> p b g m", 512, b=4, g=2)
        hidC = cut(zone, 22272, "p (b g m) -> p b g m", 256, b=2, g=4)
        ytm = cut(zone, 22528, None, 768)

        PS = [ctx.enter_context(nc.psum_tensor(f"ps{i}", [P, 1024], F32)) for i in range(4)]

        def bank(j):
            return PS[j // 2][:, (j % 2) * 512:(j % 2) * 512 + 512]

        v_dram = [dram(f"v_dram{l}", (S, BW)) for l in range(DEPTH)]
        xn_dram = [dram(f"xn_dram{l}", (TOK, D)) for l in range(DEPTH)]
        moe_dram = [dram(f"moe_dram{l}", (TOK, D)) for l in range(DEPTH)]

        units, filled = {}, [0] * 6

        def add(key, src, slot, pat, **k):
            filled[slot] += 1
            units[key] = (src, slot, filled[slot], pat, k)

        w_in, ada, wbr, wout = A["w_in"], A["ada_w"], A["w_branch"], A["w_out"]

        def kn512(w, c):
            return w[:, c:c + 512].rearrange("(k p) n -> p k n", p=P)

        moe_base = []
        for l in range(DEPTH):
            n = [0]

            def nxt(key, src):
                add((l,) + key, src, n[0] % 3, None)
                n[0] += 1
            if l == 0:
                for j in range(12):
                    nxt(("ada", 0, j), kn512(ada[0], 512 * j))
            for name, c in (("qk", C_QK), ("v", C_V), ("o", C_O), ("kn", C_KN), ("qn", C_QN), ("vn", C_VN),
                            ("pu", C_PU)):
                nxt((name,), kn512(w_in[l], c))
                if name == "v" and l + 1 < DEPTH:
                    for j in range(12):
                        nxt(("ada", l + 1, j), kn512(ada[l + 1], 512 * j))
            assert n[0] % 3 == 1
            for j in range(2):
                add((l, "wout", j), kn512(wout[l], 512 * j), 2 - j, None)
            moe_base.append(list(filled))
            for s in range(6):
                filled[s] += NE

        PER = dict(hss=1, hroot=1, m_nd=12, m_qcs=12, fabs=1, ga=1, gexp=1, gsum=1, lf=1, logit=1, aff=1, afftr=1, asub=1, aexp=1, top=1,
                   toptr=1, softp=1, n3_ss=6, x_tile=6, xn_out=16, m_C0=1, pu=1, pw_in=16, arow=12, amax=12,
                   qk_tr=6, qkT=6, m_arow=12, m_s=12, m_qc=12, m_sd=12, m_sdt=12, m_sdT=12, m_num=12, m_h=12,
                   m_dm=12, m_D=12, m_kv=10, m_vw=10, m_C=10, mg_mm=24, mg_sg=24, mg_free=26,
                   mg_tfree=26, unit_done=96, gsil=16, hid=17, hid_T=16, hidL=16, icur=17, iprev=16, ig_free=17, xe_T=17, xeT=17, y_T=16,
                   yfm=32, ytm=17, xe_in=288, y_added=512, proj=13, proj_out=12, np=14, np_out=14, oproj=6,
                   osig=6, hfin=6, mT=6, mtr=6, tab_in=256, a_bm=16, a_s=48, a_exp=48, a_max=48, a_tr=48, a_dg=24,
                   a_pT0=24, a_pT1=24, a_pv=24, a_fin=12, pup=4, pin=4, pmap=4, y=6, yss=6, y_free=8)

        def w_ready(s):
            return sem(f"w_ready{s}")

        released = {}

        def phase_end(eng, n):
            eng.drain().then_inc(sem("phase"), 1)
            eng.wait_ge(sem("phase"), 4 * n)
        NPH = 13

        def nt(l):
            return NT if l == 0 else LT

        def TW(l):
            return P * nt(l)

        def streams(l):
            return [(0, 0, S)] + ([(1, S, CTX)] if l == 0 else [])

        def both():
            return [(0, 0, S), (1, S, CTX)]

        SETS = [[(0, 0, 64, 2, 0), (1, 64, 32, 4, 512)], [(0, 0, 64, 2, 0)]]
        nslot = [96, 64]
        FW, BWD = [4, 5, 0, 1, 2, 3], [5, 4, 3, 2, 1, 0]

        def scan_outputs(l):
            return [(r, (FW, BWD)[r][st]) for st in range(6) for r in range(2) if (FW, BWD)[r][st] < nt(l)]

        def att_steps(l):
            st = [("L", hg, b, 2 * hg + i) for hg in range(2) for b in range(NB) for i in range(2)]
            if l == 0:
                st += [("C", hg, b, 2 * hg + i) for hg in range(2) for b in range(CT) for i in range(2)]
            return st

        block = ctx.enter_context(nc.Block())

        @block.tensor
        def _(pe):
            mm, tr = nc.tensor.matmul, nc.tensor.transpose

            def unit(key):
                src, slot, count, _, _ = units[key]
                pe.wait_ge(w_ready(slot), 16 * count)
                return slot_ap(slot)

            def k8(w):
                return w.rearrange("p (k n) -> p k n", k=KD)

            def ada_unit(l, la, j, b):
                w = k8(unit((l, "ada", la, j)))
                for k in range(KD):
                    for q in range(4):
                        i = mm(bank(b)[32 * q:32 * q + 32, (j % 4) * P:(j % 4 + 1) * P], csil[:, k, :],
                               w[:, k, q * P:(q + 1) * P], start=(k == 0), stop=(k == KD - 1),
                               skip_group_check=True)
                i.then_inc(sem("ada_done"), 1)
                released[l, "ada", la, j] = ("ada_done", 12 * la + j + 1)

            def ada_columns(la, banks):
                pe.wait_ge(sem("ada_rows"), 3 * la + 3)
                for j in range(12):
                    i = tr(bank(banks[j // 4])[:, (j % 4) * P:(j % 4 + 1) * P], modr[:, j, :], ident)
                i.then_inc(sem("ada_T"), 1)

            pe.wait_ge(sem("const_in"), 16)
            pe.wait_ge(sem("ones_set"), 1)
            for l in range(DEPTH):
                ph = NPH * l
                first = l == 0
                if first:
                    pe.wait_ge(sem("stage_in"), 80 * DEPTH)
                    for j in range(DEPTH):
                        i = tr(bank(0)[:, j * P:j * P + NP_ROWS], stage[j][0:NP_ROWS, :], ident[0:NP_ROWS, 0:NP_ROWS])
                    i.then_inc(sem("stage_T"), 1)
                    pe.wait_ge(sem("csil"), 1)
                    for j in range(12):
                        ada_unit(0, 0, j, 1 + j // 4)
                    ada_columns(0, (4, 5, 6))
                phase_end(pe, ph + 1)

                def to_columns(tag, tiles):
                    for k in range(KD):
                        if k == 0:
                            pe.wait_ge(sem(f"{tag}_xn{l}"), tiles)
                        if k >= 4:
                            pe.wait_ge(sem(f"{tag}_colL{l}"), k - 3)
                            if tiles > LT:
                                pe.wait_ge(sem(f"{tag}_colC{l}"), k - 3)
                        for t in range(tiles):
                            i = tr(PS[k % 4][:, t * P:(t + 1) * P], xn[:, t, k * P:(k + 1) * P], ident)
                        i.then_inc(sem(f"{tag}_T{l}"), 1)
                to_columns("n1", NT)
                phase_end(pe, ph + 2)

                g = 0
                for name in ("qk", "v"):
                    w = k8(unit((l, name)))
                    for t in range(NT):
                        if g >= 8:
                            pe.wait_ge(sem("proj_out"), l * PER["proj_out"] + g - 7)
                        for k in range(KD):
                            i = mm(bank(g % 8), hT[:, k, t * P:(t + 1) * P], w[:, k, :], start=(k == 0), stop=(k == KD - 1))
                        g += 1
                        i.then_inc(sem("proj"), 1)
                    released[l, name] = ("proj", l * PER["proj"] + g)
                pe.wait_ge(sem("proj_out"), l * PER["proj_out"] + g - 7)
                pe.wait_ge(sem("gw_in"), 48 * (l + 1))
                for t in range(NT):
                    for k in range(KD):
                        i = mm(bank(g % 8)[:, t * 16:(t + 1) * 16], hT[:, k, t * P:(t + 1) * P], gw[:, k, :],
                               start=(k == 0), stop=(k == KD - 1))
                i.then_inc(sem("proj"), 1)
                phase_end(pe, ph + 3)

                pe.wait_ge(sem("lf"), l * PER["lf"] + 1)
                mm(bank(0)[:, 0:24], tri_f, lf[:, 0].rearrange("p c h -> p (c h)"), start=True, stop=True)
                mm(bank(0)[:, 24:48], tri_b, lf[:, 1].rearrange("p c h -> p (c h)"), start=True, stop=True)
                mm(bank(0)[:, 48:96], ones[:, :], lf.rearrange("p r c h -> p (r c h)"), start=True, stop=True)\
                    .then_inc(sem("gsum"), 1)
                pe.wait_ge(sem("ga"), l * PER["ga"] + 1)

                def a_rows(dst, r, c):
                    for h in range(MH):
                        i = mm(dst[:, h * P:(h + 1) * P], ga[:, r, c, h:h + 1].to_broadcast([P, P]), ident,
                               start=True, stop=True)
                    return i
                n = 0
                for r in range(2):
                    for c in range(NT):
                        if n >= 2:
                            pe.wait_ge(sem("amax"), l * PER["amax"] + n - 1)
                        a_rows(bank(1 + n % 2), r, c).then_inc(sem("arow"), 1)
                        n += 1
                for c in range(NT):
                    if c >= 2:
                        pe.wait_ge(sem("qkT"), l * PER["qkT"] + c - 1)
                    for j in range(4):
                        i = tr(bank(3 + c % 2)[:, j * P:(j + 1) * P], qk_tm[:, c, j * P:(j + 1) * P], ident)
                    i.then_inc(sem("qk_tr"), 1)
                phase_end(pe, ph + 4)

                outs = scan_outputs(l)

                def prep(u):
                    r, c = outs[u]
                    if u:
                        pe.wait_ge(sem("m_dm"), l * PER["m_dm"] + u)
                    a_rows(bank(0), r, c).then_inc(sem("m_arow"), 1)
                    if u:
                        pe.wait_ge(sem("m_sd"), l * PER["m_sd"] + u)
                    for h in range(MH):
                        q0 = 64 * (h % 2)
                        i = mm(bank(4 + h % 2)[:, (h // 2) * P:(h // 2 + 1) * P], qT[q0:q0 + 64, h // 2, c * P:(c + 1) * P],
                               kT[q0:q0 + 64, h // 2, c * P:(c + 1) * P], start=True, stop=True)
                    i.then_inc(sem("m_s"), 1)
                prep(0)
                for n in range(12):
                    st, r = n // 2, n % 2
                    c = (FW, BWD)[r][st]
                    if first:
                        if n in (4, 8):
                            pe.wait_ge(sem("ada_rows"), 3 + n // 4)
                        ada_unit(0, 1, n, 1)
                    outp = c < nt(l)
                    if outp:
                        u = outs.index((r, c))
                        if st:
                            pe.wait_ge(sem("m_C"), l * PER["m_C"] + n - 1)
                        else:
                            pe.wait_ge(sem("m_C0"), l * PER["m_C0"] + 1)
                        if u:
                            pe.wait_ge(sem("m_nd"), l * PER["m_nd"] + u)
                        for h in range(MH):
                            q0 = 64 * (h % 2)
                            i = mm(bank(2 + h % 2)[:, (h // 2) * 129:(h // 2) * 129 + 129],
                                   qT[q0:q0 + 64, h // 2, c * P:(c + 1) * P], Cst[q0:q0 + 64, r, h // 2, :],
                                   start=True, stop=True)
                        i.then_inc(sem("m_qc"), 1)
                        pe.wait_ge(sem("m_sd"), l * PER["m_sd"] + u + 1)
                        for h in range(MH):
                            i = tr(bank(7)[:, h * P:(h + 1) * P], sd[:, h * P:(h + 1) * P], ident)
                        i.then_inc(sem("m_sdt"), 1)
                        if u + 1 < len(outs):
                            prep(u + 1)
                    if st < 5:
                        pe.wait_ge(sem("m_vw"), l * PER["m_vw"] + n + 1)
                        if n:
                            pe.wait_ge(sem("m_C"), l * PER["m_C"] + n)
                        for h in range(MH):
                            q0 = 64 * (h % 2)
                            i = mm(PS[3][q0:q0 + 64, (h // 2) * 129:(h // 2) * 129 + 129],
                                   qk_tm[:, c, 256 + h * 64:256 + h * 64 + 64], vws[:, h, :], start=True, stop=True)
                        i.then_inc(sem("m_kv"), 1)
                    if outp:
                        pe.wait_ge(sem("m_sdT"), l * PER["m_sdT"] + u + 1)
                        pe.wait_ge(sem("m_qcs"), l * PER["m_qcs"] + u + 1)
                        for h in range(MH):
                            i = mm(bank(2 + h % 2)[:, (h // 2) * 129:(h // 2) * 129 + 129],
                                   sdT[:, h * P:(h + 1) * P], v_ext[:, c, h, :], start=True, stop=True)
                        i.then_inc(sem("m_num"), 1)
                if first:
                    ada_columns(1, (1, 7, 0))
                phase_end(pe, ph + 5)
                w = k8(unit((l, "o")))
                def head_cols(t):
                    pe.wait_ge(sem("hfin"), l * PER["hfin"] + t + 1)
                    if t >= 2:
                        pe.wait_ge(sem("mT"), l * PER["mT"] + t - 1)
                    for j in range(KB):
                        i = tr(bank(2 + t % 2)[:, j * P:(j + 1) * P], hfin[t % 2][:, j * P:(j + 1) * P], ident)
                    i.then_inc(sem("mtr"), 1)
                for t in range(nt(l)):
                    if t >= 2:
                        pe.wait_ge(sem("osig"), l * PER["osig"] + t - 1)
                    for k in range(KD):
                        i = mm(bank(t % 2), hT[:, k, t * P:(t + 1) * P], w[:, k, :], start=(k == 0), stop=(k == KD - 1))
                    i.then_inc(sem("oproj"), 1)
                    if t:
                        head_cols(t - 1)
                head_cols(nt(l) - 1)
                released[l, "o"] = ("oproj", l * PER["oproj"] + nt(l))
                phase_end(pe, ph + 6)

                g = 0
                for name in ("kn", "qn"):
                    w = k8(unit((l, name)))
                    sts = both() if name == "kn" else streams(l)
                    for f in range(KB):
                        if g >= 4:
                            pe.wait_ge(sem("np_out"), l * PER["np_out"] + g - 3)
                        for _, t0, tw in sts:
                            for k in range(KD):
                                i = mm(PS[g % 4][:, t0:t0 + tw], w[:, k, f * P:(f + 1) * P], hT[:, k, t0:t0 + tw],
                                       start=(k == 0), stop=(k == KD - 1))
                        g += 1
                        i.then_inc(sem("np"), 1)
                    released[l, name] = ("np", l * PER["np"] + g)
                w = k8(unit((l, "vn")))
                for t in range(NT):
                    pe.wait_ge(sem("np_out"), l * PER["np_out"] + g - 3)
                    for k in range(KD):
                        i = mm(PS[g % 4][:, 0:512], hT[:, k, t * P:(t + 1) * P], w[:, k, :], start=(k == 0), stop=(k == KD - 1))
                    g += 1
                    i.then_inc(sem("np"), 1)
                released[l, "vn"] = ("np", l * PER["np"] + g)
                phase_end(pe, ph + 7)

                steps = att_steps(l)

                def lo_cols(n):
                    return (0, 1, 2, 3) if steps[n][0] == "L" else (2, 3)

                def scores(n):
                    kind, hg, b, f = steps[n]
                    if n >= 2:
                        pe.wait_ge(sem("a_exp"), l * PER["a_exp"] + 2 * (n - 1))
                    for part in ((0, 1) if kind == "L" else (1,)):
                        for q in range(2):
                            q0 = 64 * q
                            sp_ = bank(2 * (n % 2) + q)
                            if part == 0:
                                mm(sp_[:, 0:256], qnL[q0:q0 + 64, f, b, :],
                                   knT[q0:q0 + 64, f, 0:S].rearrange("p (j c) -> p j c", c=GW)[:, :, KSTART[b]:KSTART[b] + KC],
                                   start=True, stop=True)
                            else:
                                qs = qnL[q0:q0 + 64, f, b, :] if kind == "L" else qnC[q0:q0 + 64, f, b * P:(b + 1) * P]
                                mm(sp_[:, 256:512], qs, knT[q0:q0 + 64, f, S:TOK], start=True, stop=True)\
                                    .then_inc(sem("a_s"), 1)

                def turn(n):
                    pe.wait_ge(sem("a_dg"), l * PER["a_dg"] + n + 1)
                    for q in range(2):
                        if n:
                            pe.wait_ge(sem(f"a_pT{q}"), l * PER[f"a_pT{q}"] + n)
                        for j in lo_cols(n):
                            i = mm(bank(4 + q)[:, j * P:(j + 1) * P], pr[n % 2][q][:, j * P:(j + 1) * P], dg[n % 2][q],
                                   start=True, stop=True)
                        i.then_inc(sem("a_tr"), 1)

                def values(n):
                    kind, hg, b, f = steps[n]
                    grp = n // 2
                    if kind == "L" and n % 2 == 0:
                        pe.wait_ge(sem(f"vw_in{grp % 2}_{l}"), 128 * (grp // 2 + 1))
                    if n % 2 == 0 and grp >= 2:
                        pe.wait_ge(sem("a_fin"), l * PER["a_fin"] + grp - 1)
                    for q in range(2):
                        pe.wait_ge(sem(f"a_pT{q}"), l * PER[f"a_pT{q}"] + n + 1)
                    for j in lo_cols(n):
                        v = vw[grp % 2][:, j, :] if j < 2 else vctx[:, j - 2, :]
                        for q in range(2):
                            h = 2 * f + q
                            i = mm(bank(6 + grp % 2)[64 * q:64 * q + 64, (n % 2) * P:(n % 2 + 1) * P],
                                   v[:, h * 64:h * 64 + 64], prT[q][:, j * P:(j + 1) * P],
                                   start=(j == lo_cols(n)[0]), stop=(j == 3))
                    i.then_inc(sem("a_pv"), 1)
                scores(0)
                scores(1)
                for n in range(len(steps)):
                    turn(n)
                    if n + 2 < len(steps):
                        scores(n + 2)
                    values(n)
                phase_end(pe, ph + 8)

                w = k8(unit((l, "pu")))
                for f in range(KB):
                    for _, t0, tw in streams(l):
                        for k in range(KD):
                            i = mm(PS[f][:, t0:t0 + tw], w[:, k, f * P:(f + 1) * P], hT[:, k, t0:t0 + tw],
                                   start=(k == 0), stop=(k == KD - 1))
                    i.then_inc(sem("pup"), 1)
                released[l, "pu"] = ("pup", l * PER["pup"] + 4)
                pe.wait_ge(sem("pw_in"), l * PER["pw_in"] + 16)
                for gi in range(4):
                    pe.wait_ge(sem("pin"), l * PER["pin"] + gi + 1)
                    for _, t0, tw in streams(l):
                        i = mm(PS[gi][:, t0:t0 + tw], pw[:, gi, :], pin[:, gi, t0:t0 + tw], start=True, stop=True)
                    i.then_inc(sem("pmap"), 1)
                phase_end(pe, ph + 9)

                with pe.Fori(0, 3) as bi:
                    for f in range(KD):
                        if f % 4 == 0:
                            half = f // 4
                            pe.wait_ge(sem(f"mg_in{half}"), bi * 32 + (96 * l + 32))
                            pe.sem_inc(sem("pe_turn"), 1)
                        pe.wait_ge(sem("mg_free"), l * PER["mg_free"] + bi * KD + (f + 1))
                        pb, pg = PS[(f % 2) * 2], PS[(f % 2) * 2 + 1]
                        for _, t0, tw in streams(l):
                            for k in range(KB):
                                mm(pb[:, t0:t0 + tw], mg_wb[half][:, k, (f % 4) * P:(f % 4 + 1) * P],
                                   brT[:, bass.ds(bi, 1), k, t0:t0 + tw], start=(k == 0), stop=(k == KB - 1))
                            for k in range(KD):
                                i = mm(pg[:, t0:t0 + tw], mg_wg[half][:, k, (f % 4) * P:(f % 4 + 1) * P], hT[:, k, t0:t0 + tw],
                                       start=(k == 0), stop=(k == KD - 1))
                        i.then_inc(sem("mg_mm"), 1)
                phase_end(pe, ph + 10)

                def gain_rows(which, b):
                    for s in range(2):
                        for k in range(KD):
                            i = mm(PS[b + s][:, k * P:(k + 1) * P], cG[which][:, k, s:s + 1].to_broadcast([P, P]), ident,
                                   start=True, stop=True)
                        i.then_inc(sem(f"grow{which}_{l}"), 1)
                gain_rows(0, 0)
                w0, w1 = k8(unit((l, "wout", 0))), k8(unit((l, "wout", 1)))
                for t in range(nt(l)):
                    pe.wait_ge(sem("y_free"), l * PER["y_free"] + t + 1)
                    for j, w in enumerate((w0, w1)):
                        for k in range(KD):
                            i = mm(PS[2 + t % 2][:, j * 512:(j + 1) * 512], acc[:, k, t * P:(t + 1) * P], w[:, k, :],
                                   start=(k == 0), stop=(k == KD - 1))
                    i.then_inc(sem("y"), 1)
                for j in range(2):
                    released[l, "wout", j] = ("y", l * PER["y"] + nt(l))
                phase_end(pe, ph + 11)

                to_columns("n2", nt(l))
                pe.wait_ge(sem(f"n2_colL{l}"), KD)
                if first:
                    pe.wait_ge(sem(f"n2_colC{l}"), KD)
                for t in range(nt(l)):
                    for k in range(KD):
                        i = mm(bank(0)[:, t * NE:(t + 1) * NE], h2T[:, k, t * P:(t + 1) * P], rw[:, k, :],
                               start=(k == 0), stop=(k == KD - 1))
                i.then_inc(sem("logit"), 1)
                pe.wait_ge(sem("aff"), l * PER["aff"] + 1)
                for t in range(nt(l)):
                    i = tr(PS[1][0:NE, t * P:(t + 1) * P], affn[:, t, :], ident)
                i.then_inc(sem("afftr"), 1)
                gain_rows(1, 2)
                ns = nslot[l]
                pe.wait_ge(sem("top"), l * PER["top"] + 1)
                tr(bank(1)[0:ns, 0:NE], tif[:, 0:ns], ident[0:NE, 0:NE])
                for x in range(2):
                    for g in range(len(SETS[l])):
                        c = 16 + (2 * x + g) * NE
                        i = tr(bank(1)[:, c:c + NE], twide[:, x, g, :], ident[0:NE, 0:NE])
                i.then_inc(sem("toptr"), 1)
                phase_end(pe, ph + 12)

                def gather_T(e, add_):
                    pe.wait_ge(sem("xe_in"), l * PER["xe_in"] + 16 * e + 16 * (1 + add_))
                    pe.sem_inc(sem("pe_turn"), 1)
                    for k in range(KD):
                        i = tr(PS[0][:, k * 128:k * 128 + ns], xe[0:ns, k * P:(k + 1) * P], ident[0:ns, 0:ns])
                    i.then_inc(sem("xe_T"), 1)
                gather_T(0, 0)

                def products(src, s, lhs, banks):
                    w = slot_ap(s).rearrange("p (k n) -> p k n", k=4)
                    hk = s % 2
                    for gi, (_, c0, M, G, _) in enumerate(SETS[l]):
                        W = D // G
                        for k in range(4 * hk, 4 * hk + 4):
                            for j in range(G):
                                i = mm(bank(banks[gi])[j * M:(j + 1) * M, 0:W], lhs(gi, k), w[:, k % 4, j * W:(j + 1) * W],
                                       start=(k == 0), stop=(k == KD - 1))
                    i.then_inc(sem("unit_done"), 1)

                with pe.Fori(0, NE) as e:
                    pe.wait_ge(sem("xeT"), l * PER["xeT"] + e + 1)
                    for s in range(4):
                        if s == 2:
                            pe.wait_ge(sem("ytm"), l * PER["ytm"] + e + 1)
                            pe.sem_inc(sem("pe_turn"), 1)
                        pe.wait_ge(w_ready(s), e * 16 + 16 * (moe_base[l][s] + 1))
                        products(e, s, lambda gi, k: xeT[:, k, SETS[l][gi][1]:SETS[l][gi][1] + SETS[l][gi][2]],
                                 ((2, 4), (3, 5))[s // 2])
                    gather_T(e, 1)
                    pe.wait_ge(sem("hid"), l * PER["hid"] + e + 2)
                    for b in range(4):
                        i = tr(bank(6)[:, b * P:(b + 1) * P], hidm[:, b * P:(b + 1) * P], ident)
                    if first:
                        for b in range(2):
                            i = tr(bank(7)[:, b * P:(b + 1) * P], hidm[:, 512 + b * P:512 + (b + 1) * P], ident)
                    i.then_inc(sem("hid_T"), 1)
                    pe.wait_ge(sem("hidL"), l * PER["hidL"] + e + 1)
                    if first:
                        pe.wait_ge(sem("hidC"), e + 1)
                    for s in range(4, 6):
                        pe.wait_ge(w_ready(s), e * 16 + 16 * (moe_base[l][s] + 1))
                        products(e, s, lambda gi, k: hidL[:, k % 4, k // 4, :] if gi == 0 else hidC[:, k % 2, k // 2, :],
                                 (3, 5))
                phase_end(pe, ph + 13)

        @block.scalar
        def _(act):
            A_ = nc.scalar.activation
            n_link = [0]

            def link(ins):
                n_link[0] += 1
                ins.then_inc(sem("act_link"), 1)
                act.wait_ge(sem("act_link"), n_link[0])

            def ada_rows(la, j, b):
                act.wait_ge(sem("ada_done"), 12 * la + 4 * j + 4)
                A_(modr[:, 4 * j:4 * j + 4, :], bank(b).rearrange("p (u n) -> p u n", u=4), ACT.Copy)\
                    .then_inc(sem("ada_rows"), 1)

            for l in range(DEPTH):
                ph = NPH * l
                first = l == 0

                def root(tag, l_, tiles):
                    A_(ssx[:, 0:tiles], ssx[:, 0:tiles], ACT.Sqrt, bias=epsc, scale=1.0 / D).then_inc(sem(f"{tag}_ss{l_}"), 1)

                if first:
                    act.wait_ge(sem("pcol"), 1)
                    A_(csil[:, :, 0:2], pcol[0][:, 0:16].rearrange("p (s k) -> p k s", s=2), ACT.Silu)\
                        .then_inc(sem("csil"), 1)
                    act.wait_ge(sem("x_in"), 32)
                    for t in range(NT):
                        link(A_(junk, x_sb[:, t, :], ACT.Square, accum_out=ssx[:, t:t + 1]))
                    root("n1", 0, NT)
                    for j in range(3):
                        ada_rows(0, j, 1 + j)
                phase_end(act, ph + 1)

                def norm_cols(tag, tiles, dst, which):
                    act.wait_ge(sem(f"{tag}_rstd{l}"), 1)
                    for t in range(0, tiles, 2):
                        A_(xn[:, t, :], x_sb[:, t, :], ACT.Copy, scale=rstd[:, t:t + 1]).then_inc(sem(f"{tag}_xn{l}"), 1)
                    for k in range(KD):
                        act.wait_ge(sem(f"{tag}_T{l}"), k + 1)
                        A_(dst[:, k, 0:S], PS[k % 4][:, 0:S], ACT.Identity, bias=cS[which][:, k, 0:1],
                           scale=cA[which][:, k, 0:1]).then_inc(sem(f"{tag}_colL{l}"), 1)
                norm_cols("n1", NT, hT, 0)
                phase_end(act, ph + 2)

                g = 0
                for name in ("qk", "v"):
                    for t in range(NT):
                        act.wait_ge(sem("proj"), l * PER["proj"] + g + 1)
                        if name == "qk":
                            A_(qk_tm[:, t, 0:256], bank(g % 8)[:, 0:256], ACT.Copy, scale=DK ** -0.5)
                            A_(qk_tm[:, t, 256:512], bank(g % 8)[:, 256:512], ACT.Copy).then_inc(sem("proj_out"), 1)
                        else:
                            A_(v_ext[:, t, :, 0:DV], bank(g % 8).rearrange("p (h n) -> p h n", h=MH), ACT.Copy)\
                                .then_inc(sem("proj_out"), 1)
                        g += 1
                phase_end(act, ph + 3)

                act.wait_ge(sem("fabs"), l * PER["fabs"] + 1)
                link(A_(gt1, gt1, ACT.Exp, scale=-1.0))
                A_(gt1, gt1, ACT.Ln, bias=1.0).then_inc(sem("softp"), 1)
                for c in range(NT):
                    act.wait_ge(sem("qk_tr"), l * PER["qk_tr"] + c + 1)
                    b4 = bank(3 + c % 2).rearrange("p (j t) -> p j t", j=4)
                    A_(qT[:, :, c * P:(c + 1) * P], b4[:, 0:2, :], ACT.Copy)
                    A_(kT[:, :, c * P:(c + 1) * P], b4[:, 2:4, :], ACT.Copy).then_inc(sem("qkT"), 1)
                act.wait_ge(sem("gexp"), l * PER["gexp"] + 1)
                for t_ in (xp0, xp1, xp2, xp3):
                    A_(t_, t_, ACT.Exp)
                phase_end(act, ph + 4)

                outs = scan_outputs(l)

                def decays(u):
                    act.wait_ge(sem("m_dm"), l * PER["m_dm"] + u + 1)
                    A_(dmat, dmat, ACT.Exp).then_inc(sem("m_D"), 1)
                decays(0)
                for n in range(12):
                    r, c = n % 2, (FW, BWD)[n % 2][n // 2]
                    if c < nt(l):
                        u = outs.index((r, c))
                        act.wait_ge(sem("m_sdt"), l * PER["m_sdt"] + u + 1)
                        A_(sdT, bank(7), ACT.Copy).then_inc(sem("m_sdT"), 1)
                        if u + 1 < len(outs):
                            decays(u + 1)
                    if first and n % 4 == 3:
                        ada_rows(1, n // 4, 1)
                phase_end(act, ph + 5)
                def gate(t):
                    act.wait_ge(sem("oproj"), l * PER["oproj"] + t + 1)
                    if t >= 2:
                        act.wait_ge(sem("hfin"), l * PER["hfin"] + t - 1)
                    A_(osig[t % 2], bank(t % 2), ACT.Sigmoid).then_inc(sem("osig"), 1)
                act.wait_ge(sem("hss"), l * PER["hss"] + 1)
                A_(hss[:, 0:4 * nt(l)], hss[:, 0:4 * nt(l)], ACT.Sqrt, bias=epsc, scale=1.0 / DV).then_inc(sem("hroot"), 1)
                gate(0)
                for t in range(nt(l)):
                    if t + 1 < nt(l):
                        gate(t + 1)
                    act.wait_ge(sem("mtr"), l * PER["mtr"] + t + 1)
                    A_(brT[:, 0, :, t * P:(t + 1) * P], bank(2 + t % 2).rearrange("p (j t) -> p j t", j=KB), ACT.Copy)\
                        .then_inc(sem("mT"), 1)
                phase_end(act, ph + 6)

                g = 0
                for f in range(KB):
                    act.wait_ge(sem("np"), l * PER["np"] + g + 1)
                    A_(knT[:, f, :], PS[g % 4][:, 0:TOK], ACT.Copy).then_inc(sem("np_out"), 1)
                    g += 1
                for f in range(KB):
                    act.wait_ge(sem("np"), l * PER["np"] + g + 1)
                    if first:
                        A_(qnC[:, f, :], PS[g % 4][:, S:TOK], ACT.Copy, scale=DH ** -0.5)
                    A_(qnL[:, f].rearrange("p b (r q) -> p b r q", r=ROWS),
                       PS[g % 4][:, 0:S].rearrange("p (r b q) -> p b r q", r=ROWS, b=NB)[:, :, :, ::-1], ACT.Copy, scale=DH ** -0.5)\
                        .then_inc(sem("np_out"), 1)
                    g += 1
                for t in range(NT):
                    act.wait_ge(sem("np"), l * PER["np"] + g + 1)
                    if t < LT:
                        if t >= 2:
                            act.wait_ge(sem(f"v_out{t % 2}_{l}"), 16)
                        A_(vstage[t % 2], PS[g % 4][:, 0:512], ACT.Copy).then_inc(sem("np_out"), 1)
                    else:
                        A_(vctx[:, t - LT, :], PS[g % 4][:, 0:512], ACT.Copy).then_inc(sem("np_out"), 1)
                    g += 1
                phase_end(act, ph + 7)

                steps = att_steps(l)

                def probs(n):
                    lo = 0 if steps[n][0] == "L" else 256
                    if n >= 2:
                        act.wait_ge(sem("a_tr"), l * PER["a_tr"] + 2 * (n - 1))
                    for q in range(2):
                        x = 2 * (n % 2) + q
                        act.wait_ge(sem("a_max"), l * PER["a_max"] + 2 * n + q + 1)
                        A_(pr[n % 2][q][:, lo:512], bank(x)[:, lo:512], ACT.Exp, bias=nmx[:, x:x + 1],
                           accum_out=rsum[:, x:x + 1]).then_inc(sem("a_exp"), 1)
                probs(0)
                probs(1)
                for n in range(len(steps)):
                    lo = 0 if steps[n][0] == "L" else 256
                    act.wait_ge(sem("a_tr"), l * PER["a_tr"] + 2 * n + 1)
                    if n:
                        act.wait_ge(sem("a_pv"), l * PER["a_pv"] + n)
                    A_(prT[0][:, lo:512], bank(4)[:, lo:512], ACT.Copy).then_inc(sem("a_pT0"), 1)
                    if n + 2 < len(steps):
                        probs(n + 2)
                phase_end(act, ph + 8)

                for f in range(KB):
                    act.wait_ge(sem("pup"), l * PER["pup"] + f + 1)
                    A_(pu[:, f, LCOL:LCOL + S], PS[f][:, 0:S], ACT.Copy)
                    if first:
                        A_(pu[:, f, CCOL:CCOL + CTX], PS[f][:, S:TOK], ACT.Copy)
                act.drain().then_inc(sem("pu"), 1)
                for gi in range(4):
                    act.wait_ge(sem("pmap"), l * PER["pmap"] + gi + 1)
                    A_(brT[:, 1, gi, 0:TW(l)], PS[gi][:, 0:TW(l)], ACT.Copy, scale=pcol[l][:, 96 + gi:97 + gi])
                phase_end(act, ph + 9)

                with act.Fori(0, 3) as bi:
                    for f in range(KD):
                        act.wait_ge(sem("mg_mm"), l * PER["mg_mm"] + bi * KD + (f + 1))
                        act.wait_ge(sem("mg_free"), l * PER["mg_free"] + bi * KD + (f + 1))
                        A_(sg[f % 2][:, 0:TW(l)], PS[(f % 2) * 2 + 1][:, 0:TW(l)], ACT.Sigmoid).then_inc(sem("mg_sg"), 1)
                phase_end(act, ph + 10)

                def put_rows(which, b):
                    for s in range(2):
                        act.wait_ge(sem(f"grow{which}_{l}"), s + 1)
                        i = A_(grow[:, s, :], PS[b + s][:, :], ACT.Copy)
                    i.then_inc(sem(f"growS{which}_{l}"), 1)
                put_rows(0, 0)
                for t in range(nt(l) + 1):
                    if t < nt(l):
                        act.wait_ge(sem("y"), l * PER["y"] + t + 1)
                        link(A_(yjunk, PS[2 + t % 2][:, :], ACT.Square, accum_out=ss[:, t:t + 1]))
                        A_(ss[:, t:t + 1], ss[:, t:t + 1], ACT.Sqrt, bias=epsc, scale=1.0 / D).then_inc(sem("yss"), 1)
                    if t:
                        act.wait_ge(sem("y_free"), l * PER["y_free"] + 2 + t)
                        link(A_(yjunk, x_sb[:, t - 1, :], ACT.Square, accum_out=ssx[:, t - 1:t]))
                root("n2", l, nt(l))
                phase_end(act, ph + 11)

                norm_cols("n2", nt(l), h2T, 1)
                act.wait_ge(sem("asub"), l * PER["asub"] + 1)
                A_(aexp[:, 0:nt(l)], aexp[:, 0:nt(l)], ACT.Exp).then_inc(sem("aexp"), 1)
                put_rows(1, 2)
                phase_end(act, ph + 12)

                ns = nslot[l]
                act.drain().then_inc(sem("ytm"), 1)
                with act.Fori(0, NE) as e:
                    act.wait_ge(sem("unit_done"), l * PER["unit_done"] + 6 * e + 2)
                    act.wait_ge(sem("hid"), l * PER["hid"] + e + 1)
                    i = A_(gsil[:, 0:512], bank(2), ACT.Silu)
                    if first:
                        i = A_(gsil[:, 512:768], bank(4)[:, 0:256], ACT.Silu)
                    i.then_inc(sem("gsil"), 1)
                    act.wait_ge(sem("hid_T"), l * PER["hid_T"] + e + 1)
                    A_(hidL.rearrange("p b g m -> p (b g m)"), bank(6), ACT.Copy).then_inc(sem("hidL"), 1)
                    act.wait_ge(sem("iprev"), l * PER["iprev"] + e + 1)
                    act.wait_ge(sem("ig_free"), l * PER["ig_free"] + e + 1)
                    act.wait_ge(sem("unit_done"), l * PER["unit_done"] + 6 * e + 6)
                    i = A_(ytm[:, 0:512], bank(3), ACT.Copy, scale=gcur[:, 0:1])
                    if first:
                        i = A_(ytm[:, 512:768], bank(5)[:, 0:256], ACT.Copy, scale=gcur[:, 1:2])
                    i.then_inc(sem("ytm"), 1)
                phase_end(act, ph + 13)
                for t in range(nt(l) + 1):
                    if t < nt(l):
                        act.wait_ge(sem(f"moe_in{t}"), 16 * l + 16)
                        link(A_(junk, xn[:, t, :], ACT.Square, accum_out=ss[:, t:t + 1]))
                        A_(ss[:, t:t + 1], ss[:, t:t + 1], ACT.Sqrt, bias=epsc, scale=1.0 / D).then_inc(sem("n3_ss"), 1)
                    if t and l + 1 < DEPTH:
                        act.wait_ge(sem("x_tile"), l * PER["x_tile"] + t)
                        link(A_(junk, x_sb[:, t - 1, :], ACT.Square, accum_out=ssx[:, t - 1:t]))
                if l + 1 < DEPTH:
                    root("n1", l + 1, NT)

        @block.vector
        def _(dve):
            V = nc.vector
            n_link = [0]

            def link(ins):
                n_link[0] += 1
                ins.then_inc(sem("dve_link"), 1)
                dve.wait_ge(sem("dve_link"), n_link[0])

            def ada_cols(la, banks):
                dve.wait_ge(sem("ada_T"), la + 1)
                for j, b in enumerate(banks):
                    src = bank(b).rearrange("p (u q m) -> p u q m", u=4, q=4)[:, :, :, 0:2]
                    i = V.tensor_tensor(modc[la][:, 16 * j:16 * j + 16, :].rearrange("p (u q) s -> p u q s", u=4), src,
                                        pcol[la][:, 48 + 16 * j:64 + 16 * j].rearrange("p (u q) -> p u q", u=4)
                                        .unsqueeze(3).to_broadcast([P, 4, 4, 2]), ALU.add)
                link(i)

            link(V.memset(csil, 0.0))
            V.memset(epsc, EPS)
            V.memset(ones[:, :], 1.0).then_inc(sem("ones_set"), 1)
            dve.wait_ge(sem("const_in"), 16)
            for l in range(DEPTH):
                ph = NPH * l
                first = l == 0
                if first:
                    dve.wait_ge(sem("stage_T"), 1)
                    for j in range(DEPTH):
                        link(V.tensor_copy(pcol[j], bank(0)[:, j * P:j * P + NP_ROWS]))
                    dve.sem_inc(sem("pcol"), 1)
                    ada_cols(0, (4, 5, 6))
                for i, (sh, sc, gt, g_in, g_out) in enumerate(((0, 1, 2, 0, 1), (3, 4, 5, 2, 3))):
                    gcol = pcol[l][:, 16:48].rearrange("p (g k) -> p g k", g=4)
                    V.tensor_copy(cS[i], modc[l][:, sh * 8:sh * 8 + 8, :])
                    link(V.tensor_scalar(cA[i], modc[l][:, sc * 8:sc * 8 + 8, :], 1.0, None, ALU.add))
                    link(V.tensor_tensor(cA[i], cA[i], gcol[:, g_in, :].unsqueeze(2).to_broadcast([P, 8, 2]), ALU.mult))
                    V.tensor_tensor(cG[i], modc[l][:, gt * 8:gt * 8 + 8, :],
                                    gcol[:, g_out, :].unsqueeze(2).to_broadcast([P, 8, 2]), ALU.mult)
                phase_end(dve, ph + 1)

                def norm_cols(tag, tiles, dst, which):
                    dve.wait_ge(sem(f"{tag}_ss{l}"), 1)
                    link(V.reciprocal(rstd[:, 0:tiles], ssx[:, 0:tiles]))
                    dve.sem_inc(sem(f"{tag}_rstd{l}"), 1)
                    for t in range(1, tiles, 2):
                        V.tensor_scalar(xn[:, t, :], x_sb[:, t, :], rstd[:, t:t + 1], None, ALU.mult)\
                            .then_inc(sem(f"{tag}_xn{l}"), 1)
                    if tiles > LT:
                        for k in range(KD):
                            dve.wait_ge(sem(f"{tag}_T{l}"), k + 1)
                            V.tensor_scalar(dst[:, k, S:TOK], PS[k % 4][:, S:TOK], cA[which][:, k, 1:2],
                                            cS[which][:, k, 1:2], ALU.mult, ALU.add).then_inc(sem(f"{tag}_colC{l}"), 1)
                norm_cols("n1", NT, hT, 0)
                phase_end(dve, ph + 2)

                V.memset(v_ext[:, :, :, DV:DV + 1], 1.0)
                for t in range(LT):
                    dve.wait_ge(sem("proj_out"), l * PER["proj_out"] + t + 1)
                    qk = qk_tm[:, t, :].rearrange("p (h d) -> p h d", d=DK)
                    cos = cst[:, CCOS + t * DK:CCOS + (t + 1) * DK]
                    sin = cst[:, CSIN + t * DK:CSIN + (t + 1) * DK]
                    V.tensor_tensor(t_rope[0].rearrange("p (h d) -> p h d", d=DK), qk,
                                    cos.unsqueeze(1).to_broadcast([P, 8, DK]), ALU.mult)
                    x4 = qk_tm[:, t, :].rearrange("p (h r s d) -> p h r s d", h=8, r=2, s=2)
                    t4 = t_rope[1].rearrange("p (h r s d) -> p h r s d", h=8, r=2, s=2)
                    s4 = sin.rearrange("p (r s d) -> p r s d", r=2, s=2)
                    for s in range(2):
                        i = V.tensor_tensor(t4[:, :, :, s, :], x4[:, :, :, 1 - s, :],
                                            s4[:, :, s, :].unsqueeze(1).to_broadcast([P, 8, 2, 16]), ALU.mult)
                    link(i)
                    link(V.tensor_tensor(qk_tm[:, t, :], t_rope[0], t_rope[1], ALU.add))
                dve.wait_ge(sem("proj"), l * PER["proj"] + 13)
                dve.wait_ge(sem(f"gw_in"), 48 * (l + 1))
                link(V.tensor_tensor(gates, bank(4)[:, 0:96].rearrange("p (c g) -> p c g", c=NT),
                                     gbias.unsqueeze(1).to_broadcast([P, NT, 16]), ALU.add))
                phase_end(dve, ph + 3)

                g5 = gates.rearrange("p c (r i h) -> p r i c h", r=2, i=2)
                for r in range(2):
                    i = V.scalar_tensor_tensor(gt1[:, r], g5[:, r, 1], -1.0, g5[:, r, 1], ALU.mult, ALU.max)
                i.then_inc(sem("fabs"), 1)
                for r in range(2):
                    V.tensor_scalar(lf[:, r], g5[:, r, 1], 0.0, None, ALU.min)
                dve.wait_ge(sem("softp"), l * PER["softp"] + 1)
                dve.drain()
                V.tensor_tensor(lf, lf, gt1, ALU.subtract).then_inc(sem("lf"), 1)
                dve.wait_ge(sem("gsum"), l * PER["gsum"] + 1)
                V.tensor_copy(gbl.rearrange("p r c h -> p (r c h)"), bank(0)[:, 48:96])
                link(V.tensor_copy(gb.rearrange("p r c h -> p (r c h)"), bank(0)[:, 0:48]))
                for r in range(2):
                    i = V.tensor_tensor(ga[:, r], g5[:, r, 0], gb[:, r], ALU.subtract)
                i.then_inc(sem("ga"), 1)
                n = 0
                for r in range(2):
                    for c in range(NT):
                        dve.wait_ge(sem("arow"), l * PER["arow"] + n + 1)
                        b4 = bank(1 + n % 2).rearrange("p (h s) -> p h s", h=MH)
                        V.tensor_reduce(amax[:, r, c, :], b4, AX.X, ALU.max)
                        if n:
                            dve.wait_ge(sem("amax"), l * PER["amax"] + n)
                        d4 = dmat.rearrange("p (h s) -> p h s", h=MH)
                        link(V.tensor_tensor(d4, b4, mask_d[r].unsqueeze(1).to_broadcast([P, MH, P]), ALU.add))
                        V.tensor_reduce(cmax[:, r, c, :], d4, AX.X, ALU.max).then_inc(sem("amax"), 1)
                        n += 1
                for r in range(2):
                    order = (FW, BWD)[r]
                    link(V.memset(mprev[:, r, order[0], :], NEG))
                    for st in range(6):
                        c = order[st]
                        link(V.tensor_tensor(mlast[:, r, c, :], mprev[:, r, c, :], amax[:, r, c, :], ALU.max))
                        if st < 5:
                            link(V.tensor_tensor(mprev[:, r, order[st + 1], :], gbl[:, r, c, :], mlast[:, r, c, :], ALU.add))
                link(V.tensor_tensor(mt, mprev, cmax, ALU.max))
                V.tensor_tensor(xp0, mprev, mt, ALU.subtract)
                V.tensor_tensor(xp1, ga, mlast, ALU.subtract)
                V.tensor_tensor(xp2, mprev, mlast, ALU.subtract)
                link(V.tensor_tensor(xp3, gb, mt, ALU.add))
                link(V.tensor_scalar(xp3, xp3, -1.0, None, ALU.mult))
                dve.sem_inc(sem("gexp"), 1)
                V.memset(hsum[:, 0:nt(l), :], 0.0)
                link(V.memset(Cst, 0.0))
                dve.sem_inc(sem("m_C0"), 1)
                phase_end(dve, ph + 4)

                def two(ps, n):
                    return ps[:, :].rearrange("p (q x) -> p q x", q=2)[:, :, 0:2 * n].rearrange("p q (g n) -> p q g n", g=2)

                def by_parity(row):
                    return row.rearrange("p (g q n) -> p q g n", g=2, q=2)

                def cols(v):
                    return v.rearrange("p (g q) -> p q g", g=2)
                outs = scan_outputs(l)

                def exponents(u):
                    r, c = outs[u]
                    d4 = dmat.rearrange("p (h s) -> p h s", h=MH)
                    dve.wait_ge(sem("m_arow"), l * PER["m_arow"] + u + 1)
                    link(V.tensor_tensor(d4, bank(0).rearrange("p (h s) -> p h s", h=MH),
                                         mask_d[r].unsqueeze(1).to_broadcast([P, MH, P]), ALU.add))
                    V.tensor_tensor(d4, d4, mt[:, r, c, :].unsqueeze(2).to_broadcast([P, MH, P]), ALU.subtract)\
                        .then_inc(sem("m_dm"), 1)
                exponents(0)
                for n in range(12):
                    st, r = n // 2, n % 2
                    c = (FW, BWD)[r][st]
                    outp = c < nt(l)
                    if outp:
                        u = outs.index((r, c))
                        dve.wait_ge(sem("m_s"), l * PER["m_s"] + u + 1)
                        dve.wait_ge(sem("m_D"), l * PER["m_D"] + u + 1)
                        V.tensor_tensor(by_parity(sd), two(PS[2], P), by_parity(dmat), ALU.mult).then_inc(sem("m_sd"), 1)
                        dve.wait_ge(sem("m_qc"), l * PER["m_qc"] + u + 1)
                        V.tensor_tensor(qcs, two(PS[1], 129), cols(xp0[:, r, c, :]).unsqueeze(3).to_broadcast([P, 2, 2, 129]),
                                        ALU.mult).then_inc(sem("m_qcs"), 1)
                        if u + 1 < len(outs):
                            exponents(u + 1)
                    if st < 5:
                        dve.wait_ge(sem("m_kv"), l * PER["m_kv"] + n + 1)
                        for q in range(2):
                            V.tensor_tensor(Cdec[64 * q:64 * q + 64], Cst[64 * q:64 * q + 64, r],
                                            xp2[64 * q:64 * q + 64, r, c, q::2].unsqueeze(2).to_broadcast([64, 2, 129]),
                                            ALU.mult)
                        dve.drain()
                        V.tensor_tensor(Cst[:, r], Cdec, PS[3][:, 0:258].rearrange("p (g n) -> p g n", g=2), ALU.add)\
                            .then_inc(sem("m_C"), 1)
                    if outp:
                        dve.wait_ge(sem("m_num"), l * PER["m_num"] + u + 1)
                        V.tensor_tensor(nd, qcs, two(PS[1], 129), ALU.add).then_inc(sem("m_nd"), 1)
                        dve.wait_ge(sem("m_nd"), l * PER["m_nd"] + u + 1)
                        dn2 = dn.rearrange("p (q g) -> p q g", q=2)
                        link(V.scalar_tensor_tensor(dn2, nd[:, :, :, 128], -1.0,
                                                    nd[:, :, :, 128], ALU.mult, ALU.max))
                        link(V.tensor_tensor(dn2, dn2, cols(xp3[:, r, c, :]), ALU.max))
                        link(V.reciprocal(rden, dn))
                        link(V.tensor_tensor(by_parity(htmp), nd[:, :, :, 0:128], rden.rearrange("p (q g) -> p q g", q=2)
                                             .unsqueeze(3).to_broadcast([P, 2, 2, 128]), ALU.mult))
                        link(V.tensor_tensor(hsum[:, c, :], hsum[:, c, :], htmp, ALU.add))
                if first:
                    ada_cols(1, (1, 7, 0))
                phase_end(dve, ph + 5)
                for t in range(nt(l)):
                    link(V.tensor_tensor(dmat, hsum[:, t, :], hsum[:, t, :], ALU.mult))
                    link(V.tensor_reduce(hss[:, 4 * t:4 * t + 4], dmat.rearrange("p (h n) -> p h n", h=MH), AX.X, ALU.add))
                dve.sem_inc(sem("hss"), 1)
                dve.wait_ge(sem("hroot"), l * PER["hroot"] + 1)
                link(V.reciprocal(hrr[:, 0:4 * nt(l)], hss[:, 0:4 * nt(l)]))
                for t in range(nt(l)):
                    hs = hsum[:, t, :].rearrange("p (h n) -> p h n", h=MH)
                    link(V.tensor_tensor(hs, hs, hrr[:, 4 * t:4 * t + 4].unsqueeze(2).to_broadcast([P, MH, DV]), ALU.mult))
                    if t >= 2:
                        dve.wait_ge(sem("mtr"), l * PER["mtr"] + t - 1)
                    dve.wait_ge(sem("osig"), l * PER["osig"] + t + 1)
                    V.tensor_tensor(hfin[t % 2], hsum[:, t, :], osig[t % 2], ALU.mult).then_inc(sem("hfin"), 1)
                phase_end(dve, ph + 6)
                phase_end(dve, ph + 7)

                steps = att_steps(l)

                def fin(grp):
                    kind, hg, b, _ = steps[grp * 2]
                    dve.wait_ge(sem("a_pv"), l * PER["a_pv"] + 2 * grp + 2)
                    src = bank(6 + grp % 2)[:, 0:256]
                    if kind == "L":
                        dst = brT[:, 2, 2 * hg:2 * hg + 2, 0:S].rearrange("p f (r b q) -> p f r b q", r=ROWS, b=NB)[:, :, :, b, ::-1]
                        src = src.rearrange("p (f r q) -> p f r q", f=2, r=ROWS)
                    else:
                        dst = brT[:, 2, 2 * hg:2 * hg + 2, S + b * P:S + (b + 1) * P]
                        src = src.rearrange("p (f q) -> p f q", f=2)
                    V.tensor_copy(dst, src).then_inc(sem("a_fin"), 1)

                def maxima(n):
                    for q in range(2):
                        x = 2 * (n % 2) + q
                        sp_ = bank(x)
                        dve.wait_ge(sem("a_s"), l * PER["a_s"] + 2 * n + q + 1)
                        if steps[n][0] == "L":
                            if q == 0:
                                dve.wait_ge(sem("a_bm"), l * PER["a_bm"] + n + 1)
                            s3 = sp_[:, 0:256].rearrange("p (j k) -> p j k", j=ROWS)
                            link(V.tensor_tensor(s3, s3, bm[n % 2][:, q], ALU.add))
                            V.tensor_reduce(nmx[:, x:x + 1], sp_, AX.X, ALU.max, negate=True).then_inc(sem("a_max"), 1)
                        else:
                            V.tensor_reduce(nmx[:, x:x + 1], sp_[:, 256:512], AX.X, ALU.max, negate=True)\
                                .then_inc(sem("a_max"), 1)

                def scales(n):
                    x = 2 * (n % 2)
                    dve.wait_ge(sem("a_exp"), l * PER["a_exp"] + 2 * n + 2)
                    link(V.reciprocal(rrec[:, x:x + 2], rsum[:, x:x + 2]))
                    for q in range(2):
                        i = V.tensor_scalar(dg[n % 2][q], ident, rrec[:, x + q:x + q + 1], None, ALU.mult)
                    i.then_inc(sem("a_dg"), 1)
                maxima(0)
                maxima(1)
                scales(0)
                for n in range(len(steps)):
                    if n + 1 < len(steps):
                        scales(n + 1)
                    lo = 0 if steps[n][0] == "L" else 256
                    dve.wait_ge(sem("a_tr"), l * PER["a_tr"] + 2 * n + 2)
                    if n:
                        dve.wait_ge(sem("a_pv"), l * PER["a_pv"] + n)
                    V.tensor_copy(prT[1][:, lo:512], bank(5)[:, lo:512]).then_inc(sem("a_pT1"), 1)
                    if n % 2 == 0 and n:
                        fin(n // 2 - 1)
                    if n + 2 < len(steps):
                        maxima(n + 2)
                fin(len(steps) // 2 - 1)
                phase_end(dve, ph + 8)

                V.memset(pu[:, :, 0:LCOL], 0.0)
                V.memset(pu[:, :, LCOL + S:CCOL], 0.0)
                if first:
                    V.memset(pu[:, :, CCOL + CTX:PADW], 0.0)
                else:
                    V.memset(pu[:, :, CCOL:PADW], 0.0)
                dve.drain()
                dve.wait_ge(sem("pu"), l * PER["pu"] + 1)
                link(V.tensor_tensor(pA[:, :, 0:PADW - 1], pu[:, :, 0:PADW - 1], pu[:, :, 1:PADW], ALU.add))
                link(V.tensor_tensor(pB[:, 1:4, 0:PADW - 3], pA[:, 1:4, 0:PADW - 3], pA[:, 1:4, 2:PADW - 1], ALU.add))
                link(V.tensor_tensor(pA[:, 2:4, 0:PADW - 7], pB[:, 2:4, 0:PADW - 7], pB[:, 2:4, 4:PADW - 3], ALU.add))
                link(V.tensor_tensor(pB[:, 3:4, 0:PADW - 15], pA[:, 3:4, 0:PADW - 15], pA[:, 3:4, 8:PADW - 7], ALU.add))
                for gi, w in enumerate(WINDOWS):
                    src = (pA, pB)[gi % 2]
                    for _, base, cnt in [(0, LCOL, S)] + ([(1, CCOL, CTX)] if first else []):
                        for side, p0 in enumerate((base, base + cnt - 8)):
                            e0 = CED + gi * 16 + side * 8
                            lo = p0 - w // 2
                            V.tensor_tensor(src[:, gi, lo:lo + 8], src[:, gi, lo:lo + 8], cst[:, e0:e0 + 8], ALU.mult)
                dve.drain()
                for gi, w in enumerate(WINDOWS):
                    src = (pA, pB)[gi % 2]
                    for _, base, t0, cnt in [(0, LCOL, 0, S)] + ([(1, CCOL, S, CTX)] if first else []):
                        lo = base - w // 2
                        i = V.scalar_tensor_tensor(pin[:, gi, t0:t0 + cnt], src[:, gi, lo:lo + cnt], 1.0 / w,
                                                   pu[:, gi, base:base + cnt], ALU.mult, ALU.subtract)
                    i.then_inc(sem("pin"), 1)
                phase_end(dve, ph + 9)

                dve.drain().then_inc(sem("mg_free"), 2)
                with dve.Fori(0, 3) as bi:
                    for f in range(KD):
                        dve.wait_ge(sem("mg_sg"), l * PER["mg_sg"] + bi * KD + (f + 1))
                        dve.wait_ge(sem("mg_tfree"), l * PER["mg_tfree"] + bi * KD + (f + 1))
                        V.tensor_tensor(mtmp[f % 2][:, 0:TW(l)], sg[f % 2][:, 0:TW(l)], PS[(f % 2) * 2][:, 0:TW(l)],
                                        ALU.mult).then_inc(sem("mg_free"), 1)
                phase_end(dve, ph + 10)

                dve.drain().then_inc(sem("y_free"), 2)
                dve.wait_ge(sem(f"growS0_{l}"), 1)
                for t in range(nt(l)):
                    dve.wait_ge(sem("yss"), l * PER["yss"] + t + 1)
                    link(V.reciprocal(rstd[:, t:t + 1], ss[:, t:t + 1]))
                    link(V.scalar_tensor_tensor(ytmp[t % 2], PS[2 + t % 2][:, :], rstd[:, t:t + 1], grow[:, t // LT, :],
                                                ALU.mult, ALU.mult))
                    V.tensor_tensor(x_sb[:, t, :], x_sb[:, t, :], ytmp[t % 2], ALU.add).then_inc(sem("y_free"), 1)
                phase_end(dve, ph + 11)

                norm_cols("n2", nt(l), h2T, 1)
                n_t = nt(l)
                dve.wait_ge(sem("logit"), l * PER["logit"] + 1)
                lg = bank(0)[:, 0:n_t * NE].rearrange("p (t e) -> p t e", t=n_t)
                link(V.tensor_reduce(asum[:, 0:n_t], lg, AX.X, ALU.max))
                V.tensor_tensor(aexp[:, 0:n_t], lg, asum[:, 0:n_t].unsqueeze(2).to_broadcast([P, n_t, NE]), ALU.subtract)\
                    .then_inc(sem("asub"), 1)
                dve.wait_ge(sem("aexp"), l * PER["aexp"] + 1)
                link(V.tensor_reduce(asum[:, 0:n_t], aexp[:, 0:n_t], AX.X, ALU.add))
                link(V.reciprocal(arec[:, 0:n_t], asum[:, 0:n_t]))
                V.tensor_tensor(affn[:, 0:n_t], aexp[:, 0:n_t], arec[:, 0:n_t].unsqueeze(2).to_broadcast([P, n_t, NE]),
                                ALU.mult).then_inc(sem("aff"), 1)
                dve.wait_ge(sem("afftr"), l * PER["afftr"] + 1)
                link(V.tensor_copy(affT[:, 0:TW(l)], PS[1][0:NE, 0:TW(l)]))
                for s, t0, cnt in streams(l):
                    rows = affT[:, t0:t0 + cnt]
                    for j in range(cnt // 64):
                        o8 = s * 64 + 8 * j
                        link(V.max(tv[:, o8:o8 + 8], rows))
                        V.max_index(ti[:, o8:o8 + 8], tv[:, o8:o8 + 8], rows)
                        dve.drain()
                        if j < cnt // 64 - 1:
                            link(V.match_replace(rows, tv[:, o8:o8 + 8], rows, -1.0))
                link(V.tensor_copy(tif[:, 0:nslot[l]], ti[:, 0:nslot[l]]))
                if first:
                    link(V.tensor_scalar(tif[:, 64:96], tif[:, 64:96], float(S), None, ALU.add))
                for g, (s, c0, M, G, _) in enumerate(SETS[l]):
                    wv = twide.rearrange("p x g (j m) -> p x g j m", m=M)
                    V.tensor_copy(wv[:, 0, g], tv[:, c0:c0 + M].unsqueeze(1).to_broadcast([NE, G, M]))
                    for j in range(G):
                        i = V.tensor_scalar(wv[:, 1, g, j], tif[:, c0:c0 + M], float(G), float(j), ALU.mult, ALU.add)
                link(i)
                dve.sem_inc(sem("top"), 1)
                dve.wait_ge(sem("toptr"), l * PER["toptr"] + 1)
                ns = nslot[l]
                V.tensor_copy(gidx[0:ns, 0:NE], bank(1)[0:ns, 0:NE])
                V.tensor_copy(gidx[0:ns, NE:NE + 2], bank(1)[0:ns, 0:2])
                for g in range(len(SETS[l])):
                    V.tensor_copy(gval[:, g, :], bank(1)[:, 16 + g * NE:16 + (g + 1) * NE])
                    i = V.tensor_copy(sidx[:, g, :], bank(1)[:, 48 + g * NE:48 + (g + 1) * NE])
                link(i)
                link(V.tensor_copy(icur[0:ns, :], gidx[0:ns, 0:1]))
                phase_end(dve, ph + 12)

                def modulate(tag_e):
                    ps = PS[0][:, :].rearrange("p (k c) -> p k c", k=KD)
                    for s, c0, cw in [(0, 0, 64)] + ([(1, 64, 32)] if first else []):
                        V.tensor_tensor(xeT[:, :, c0:c0 + cw], ps[:, :, c0:c0 + cw],
                                        cA[1][:, :, s:s + 1].to_broadcast([P, KD, cw]), ALU.mult)
                    dve.drain()
                    for s, c0, cw in [(0, 0, 64)] + ([(1, 64, 32)] if first else []):
                        i = V.tensor_tensor(xeT[:, :, c0:c0 + cw], xeT[:, :, c0:c0 + cw],
                                            cS[1][:, :, s:s + 1].to_broadcast([P, KD, cw]), ALU.add)
                    i.then_inc(sem("xeT"), 1)
                dve.drain().then_inc(sem("hid"), 1)
                dve.wait_ge(sem("xe_T"), l * PER["xe_T"] + 1)
                V.tensor_copy(icur[0:ns, :], gidx[0:ns, 1:2]).then_inc(sem("icur"), 1)
                modulate(0)
                with dve.Fori(0, NE) as e:
                    dve.wait_ge(sem("ig_free"), l * PER["ig_free"] + e + 1)
                    ng = len(SETS[l])
                    V.tensor_copy(gcur[:, 0:ng], gval[:, 0:ng, bass.ds(e, 1)].rearrange("p g o -> p (g o)"))
                    V.tensor_copy(iprev[:, 0:ng], sidx[:, 0:ng, bass.ds(e, 1)].rearrange("p g o -> p (g o)"))\
                        .then_inc(sem("iprev"), 1)
                    dve.wait_ge(sem("unit_done"), l * PER["unit_done"] + 6 * e + 4)
                    dve.wait_ge(sem("gsil"), l * PER["gsil"] + e + 1)
                    i = V.tensor_tensor(hidm[:, 0:512], gsil[:, 0:512], bank(3), ALU.mult)
                    if first:
                        i = V.tensor_tensor(hidm[:, 512:768], gsil[:, 512:768], bank(5)[:, 0:256], ALU.mult)
                    i.then_inc(sem("hid"), 1)
                    if first:
                        dve.wait_ge(sem("hid_T"), e + 1)
                        V.tensor_copy(hidC.rearrange("p b g m -> p (b g m)"), bank(7)[:, 0:256]).then_inc(sem("hidC"), 1)
                    dve.wait_ge(sem("xe_T"), l * PER["xe_T"] + e + 2)
                    V.tensor_copy(icur[0:ns, :], gidx[0:ns, bass.ds(e + 2, 1)]).then_inc(sem("icur"), 1)
                    modulate(e)
                phase_end(dve, ph + 13)

                dve.wait_ge(sem(f"growS1_{l}"), 1)
                for t in range(n_t):
                    dve.wait_ge(sem("n3_ss"), l * PER["n3_ss"] + t + 1)
                    link(V.reciprocal(rstd[:, t:t + 1], ss[:, t:t + 1]))
                    link(V.scalar_tensor_tensor(xn[:, t, :], xn[:, t, :], rstd[:, t:t + 1], grow[:, t // LT, :],
                                                ALU.mult, ALU.mult))
                    V.tensor_tensor(x_sb[:, t, :], x_sb[:, t, :], xn[:, t, :], ALU.add).then_inc(sem("x_tile"), 1)

        @block.gpsimd
        def _(pool):
            G = nc.gpsimd
            pool.wait_ge(sem("const_in"), 16)
            for l in range(DEPTH):
                ph = NPH * l
                first = l == 0
                if not first:
                    pool.wait_ge(sem("x_tile"), NT)
                for n in range(1, 5):
                    phase_end(pool, ph + n)
                for st in range(5):
                    for r in range(2):
                        c = (FW, BWD)[r][st]
                        if 2 * st + r:
                            pool.wait_ge(sem("m_kv"), l * PER["m_kv"] + 2 * st + r)
                        G.tensor_tensor(vws, v_ext[:, c], xp1[:, r, c, :].unsqueeze(2).to_broadcast([P, MH, 129]), ALU.mult)\
                            .then_inc(sem("m_vw"), 1)
                for n in range(5, 7):
                    phase_end(pool, ph + n)
                for t in range(LT):
                    pool.wait_ge(sem("np_out"), l * PER["np_out"] + 2 * KB + t + 1)
                    pool.dma_start(v_dram[l][t * P:(t + 1) * P, :], vstage[t % 2]).then_inc(sem(f"v_out{t % 2}_{l}"), 16)
                phase_end(pool, ph + 7)

                for n, (kind, hg, b, f) in enumerate(att_steps(l)):
                    if kind != "L":
                        continue
                    if n % 8 == 0:
                        pool.wait_ge(sem("tab_in"), l * PER["tab_in"] + 128 * (hg + 1))
                    if n >= 2:
                        pool.wait_ge(sem("a_max"), l * PER["a_max"] + 2 * (n - 1))
                    off = KSTART[b] - QC * b + 16
                    h4 = 2 * (n % 2)
                    for q in range(2):
                        t3 = tab[:, h4 + q, :].rearrange("p (j w) -> p j w", j=ROWS)[:, :, off:off + KC]
                        i = G.tensor_tensor(bm[n % 2][:, q], t3, cst[:, CNM + b * KC:CNM + (b + 1) * KC].unsqueeze(1)
                                            .to_broadcast([P, ROWS, KC]), ALU.add)
                    i.then_inc(sem("a_bm"), 1)
                phase_end(pool, ph + 8)
                pool.dma_start(pw, A["pool_w"][l].rearrange("g p n -> p g n")).then_inc(sem("pw_in"), 16)
                phase_end(pool, ph + 9)
                G.memset(acc[:, :, 0:TW(l)], 0.0)
                pool.drain().then_inc(sem("mg_tfree"), 2)
                with pool.Fori(0, 3) as bi:
                    for f in range(KD):
                        pool.wait_ge(sem("mg_free"), l * PER["mg_free"] + bi * KD + (f + 3))
                        G.tensor_tensor(acc[:, f, 0:TW(l)], acc[:, f, 0:TW(l)], mtmp[f % 2][:, 0:TW(l)], ALU.add)\
                            .then_inc(sem("mg_tfree"), 1)
                for n in range(10, 12):
                    phase_end(pool, ph + n)
                pool.wait_ge(sem(f"n2_xn{l}"), nt(l))
                pool.dma_start(xn_dram[l][0:TW(l), :].rearrange("(t p) d -> p t d", p=P), xn[:, 0:nt(l), :])\
                    .then_inc(sem("xn_out"), 16)
                phase_end(pool, ph + 12)
                ns = nslot[l]
                pool.wait_ge(sem("xn_out"), l * PER["xn_out"] + 16)
                pool.wait_ge(sem("zero_out"), 16 * NT * (l + 1))

                def gather():
                    G.indirect_dma_start(xe[0:ns, :], None, xn_dram[l][0:TW(l), :],
                                         bass.IndirectOffsetOnAxis(ap=icur[0:ns, 0:1], axis=0)).then_inc(sem("xe_in"), 16)
                gather()
                pool.drain().then_inc(sem("ig_free"), 1)
                pool.wait_ge(sem("icur"), l * PER["icur"] + 1)
                gather()
                with pool.Fori(0, NE) as e:
                    pool.wait_ge(sem("icur"), l * PER["icur"] + e + 2)
                    pool.sem_inc(sem("pool_turn"), 1)
                    gather()
                    pool.wait_ge(sem("iprev"), l * PER["iprev"] + e + 1)
                    pool.wait_ge(sem("ytm"), l * PER["ytm"] + e + 2)
                    pool.sem_inc(sem("pool_turn"), 1)
                    nset = len(SETS[l])
                    for g, (_, _, M, parts, c) in enumerate(SETS[l]):
                        W = D // parts
                        G.indirect_dma_start(moe_dram[l][0:TW(l), :].rearrange("t (j n) -> (t j) n", n=W),
                                             bass.IndirectOffsetOnAxis(ap=iprev[:, g:g + 1], axis=0),
                                             ytm[:, c:c + W], None, compute_op=ALU.add).then_inc(sem("y_added"), 16)
                    pool.wait_ge(sem("y_added"), l * PER["y_added"] + 16 * nset * e + 16 * nset)
                    pool.sem_inc(sem("ig_free"), 1)
                pool.wait_ge(sem("xe_in"), (l + 1) * PER["xe_in"])
                phase_end(pool, ph + 13)

        @block.sync
        def _(sp):
            last = [None] * 6

            def load(key):
                src, slot, count, _, _ = units[key]
                if last[slot]:
                    sp.wait_ge(sem(last[slot][0]), last[slot][1])
                nk = src.shape[1]
                sp.dma_start(slot_ap(slot).rearrange("p (k n) -> p k n", k=nk), src).then_inc(w_ready(slot), 16)
                last[slot] = released[key]

            sp.dma_start(cst[:, :], A["tables"]).then_inc(sem("const_in"), 16)
            for l in range(DEPTH):
                rows = ((0, 8, A["c"][0].rearrange("(k p) -> k p", p=P)),
                        (8, 16, A["c_ctx"].rearrange("(k p) -> k p", p=P)),
                        (16, 48, A["norm_gain"][l].rearrange("g (k p) -> (g k) p", p=P)),
                        (48, 96, A["ada_b"][l].rearrange("(k p) -> k p", p=P)),
                        (96, 100, A["pool_scale"][l].rearrange("(k p) -> k p", p=P)))
                for r0, r1, src in rows:
                    sp.dma_start(stage[l][r0:r1, :], src).then_inc(sem("stage_in"), 16)
            for l in range(DEPTH):
                def load_tables(hg):
                    for r in range(ROWS):
                        src = A["rpb"]
                        src = bass.AP(src.tensor, src.offset + (l * NH + hg * 4) * 15 * RPW + (7 - r) * RPW,
                                      [[1, QC], [15 * RPW, 4], [1, 496]])
                        sp.dma_start(tab[r * QC:(r + 1) * QC, :, 0:496], src).then_inc(sem("tab_in"), 16)

                def load_values(grp):
                    b = grp % NB
                    if grp >= 2:
                        sp.wait_ge(sem("a_pv"), l * PER["a_pv"] + 2 * (grp - 1))
                    rows = v_dram[l].rearrange("(j c) n -> j c n", c=GW)
                    for j in range(ROWS):
                        sp.dma_start(vw[grp % 2][(j % 4) * KC:(j % 4 + 1) * KC, j // 4, :],
                                     rows[j, KSTART[b]:KSTART[b] + KC, :]).then_inc(sem(f"vw_in{grp % 2}_{l}"), 16)
                def load_merge(b, half):
                    sp.dma_start(mg_wb[half], wbr[l, b, :, 512 * half:512 * half + 512].rearrange("(k p) n -> p k n", p=P))\
                        .then_inc(sem(f"mg_in{half}"), 16)
                    sp.dma_start(mg_wg[half], kn512(w_in[l], C_BG + D * b + 512 * half)).then_inc(sem(f"mg_in{half}"), 16)

                def load_vectors():
                    sp.dma_start(gw, w_in[l][:, C_G:C_G + 16].rearrange("(k p) n -> p k n", p=P)).then_inc(sem("gw_in"), 16)
                    sp.dma_start(rw, A["router_w"][l].rearrange("(k p) n -> p k n", p=P)).then_inc(sem("gw_in"), 16)
                    sp.dma_start(gbias, A["mlstm_gate_bias"][l].rearrange("(o g) h -> o (g h)", o=1).to_broadcast([P, 16]))\
                        .then_inc(sem("gw_in"), 16)

                for key in [k_ for k_ in units if k_[0] == l and k_[1] != "wout"]:
                    load(key)
                    if key[1:] == ("ada", 0, 2):
                        sp.dma_start(x_sb[:, 0:LT, :], A["x"][0].rearrange("(t p) d -> p t d", p=P)).then_inc(sem("x_in"), 16)
                        sp.dma_start(x_sb[:, LT:NT, :], A["ctx"][0].rearrange("(t p) d -> p t d", p=P)).then_inc(sem("x_in"), 16)
                    if key[1] == "qk":
                        load_vectors()
                    if key[1] == "vn":
                        for t in range(NT):
                            sp.dma_start(moe_dram[l][t * P:(t + 1) * P, :], A["zeros"]).then_inc(sem("zero_out"), 16)
                        sp.wait_ge(sem("phase"), 4 * (NPH * l + 6))
                        load_tables(0)
                for s in (1, 2):
                    sp.wait_ge(sem(last[s][0]), last[s][1])
                load_merge(0, 0)
                for i in range(2):
                    sp.wait_ge(sem(f"v_out{i}_{l}"), 32)
                for grp in range(2 * NB):
                    if grp == NB:
                        sp.wait_ge(sem("a_bm"), l * PER["a_bm"] + 2 * NB)
                        load_tables(1)
                    load_values(grp)
                sp.wait_ge(sem(last[0][0]), last[0][1])
                load_merge(0, 1)
                for b in range(1, 3):
                    for half in range(2):
                        sp.wait_ge(sem("mg_mm"), l * PER["mg_mm"] + (b - 1) * KD + 4 * half + 4)
                        load_merge(b, half)
                last[2] = ("mg_mm", l * PER["mg_mm"] + 2 * KD + 4)
                last[0] = last[1] = ("mg_mm", l * PER["mg_mm"] + 3 * KD)
                for j in range(2):
                    load((l, "wout", j))

                exp_src = [(A["w_gate"], 0), (A["w_gate"], 512), (A["w_up"], 0), (A["w_up"], 512),
                           (A["w_down"], 0), (A["w_down"], 512)]

                def expert_unit(e, s):
                    w, c = exp_src[s]
                    sp.dma_start(slot_ap(s).rearrange("p (k n) -> p k n", k=4),
                                 w[l][bass.ds(e, 1), c:c + 512, :].rearrange("o (k p) n -> p (o k) n", p=P))\
                        .then_inc(w_ready(s), 16)
                for s in range(6):
                    if s < 3:
                        sp.wait_ge(sem(last[s][0]), last[s][1])
                    elif s == 3:
                        sp.wait_ge(sem("phase"), 4 * (NPH * l + 10))
                    expert_unit(0, s)
                with sp.Fori(1, NE) as e:
                    for s in range(6):
                        sp.wait_ge(sem("unit_done"), l * PER["unit_done"] + 6 * e + (s - 5))
                        sp.sem_inc(sem("sp_turn"), 1)
                        s2, back = (s - 2) % 6, 1 if s < 2 else 0
                        sp.wait_ge(w_ready(s2), 16 * e + 16 * (moe_base[l][s2] + 1 - back))
                        sp.sem_inc(sem("sp_turn"), 1)
                        expert_unit(e, s)
                sp.wait_ge(sem("y_added"), l * PER["y_added"] + 16 * len(SETS[l]) * NE)
                for t in range(nt(l)):
                    sp.dma_start(xn[:, t, :], moe_dram[l][t * P:(t + 1) * P, :]).then_inc(sem(f"moe_in{t}"), 16)
                for s in range(6):
                    last[s] = ("unit_done", l * PER["unit_done"] + 6 * NE - 5 + s)
            for t in range(LT):
                sp.wait_ge(sem("x_tile"), (DEPTH - 1) * PER["x_tile"] + t + 1)
                sp.dma_start(out[0, t * P:(t + 1) * P, :], x_sb[:, t, :]).then_inc(sem("out"), 16)
            sp.wait_ge(sem("out"), 16 * LT)


_INS = ["x", "c", "ctx", "c_ctx", "norm_gain", "ada_w", "ada_b", "w_in", "mlstm_gate_bias", "pool_w", "pool_scale",
        "w_branch", "w_out", "router_w", "w_gate", "w_up", "w_down"]


def kernel(**inputs):
    import numpy as np
    import concourse.bacc as bacc
    from concourse.bass_utils import run_bass_kernel_spmd

    nc = bacc.Bacc("TRN2", target_bir_lowering=False, num_devices=1)
    arrays = {n: np.ascontiguousarray(inputs[n]) for n in _INS}
    rpb = np.asarray(inputs["na_rpb"])
    wide = np.zeros(rpb.shape[:3] + (RPW,), rpb.dtype)
    wide[..., 16:16 + rpb.shape[3]] = rpb
    arrays["rpb"] = wide
    arrays["tables"] = constants()
    arrays["zeros"] = np.zeros((P, D), np.float32)
    args = {n: nc.dram_tensor(f"in_{n}", a.shape, F32, kind="ExternalInput").ap() for n, a in arrays.items()}
    out = nc.dram_tensor("out_0_dram", (1, S, D), F32, kind="ExternalOutput").ap()
    build(nc, args, out)
    r = run_bass_kernel_spmd(nc, [{f"in_{n}": a for n, a in arrays.items()}], core_ids=[0])
    return r.results[0]["out_0_dram"]
```

```python
import concourse.bass as bass
from concourse import mybir
from contextlib import ExitStack

F32 = mybir.dt.float32
F32R = mybir.dt.float32r
U32 = mybir.dt.uint32
ALU = mybir.AluOpType
ACT = mybir.ActivationFunctionType
AX = mybir.AxisListType

D, S, CTX, DEPTH = 1024, 512, 256, 2
TOK = S + CTX
P = 128
KD = D // P
LT, CT = S // P, CTX // P
NT = LT + CT
BW = D // 2
KB = BW // P
MH, DV, DK = 4, 128, 64
NH, DH = 8, 64
GW, ROWS = 64, 8
NB, QC, KC = 4, 16, 32
KSTART = [0, 8, 24, 32]
WINDOWS = (2, 4, 8, 16)
NE, FF = 16, 1024
EPS = 1e-6
C_QK, C_V, C_O, C_G, C_PU, C_QN, C_KN, C_VN, C_BG = 0, 512, 1024, 1536, 1552, 2064, 2576, 3088, 3600
NEG = -1.0e30
PADW = 8 + S + 8 + CTX + 8
RPW = 64
LCOL, CCOL = 8, 8 + S + 8

CI, CU, CL, CMF, CMB, CNM, CED, CCOS, CSIN, CSEL = 0, 128, 256, 384, 512, 640, 768, 832, 1088, 1344
CW = 1360


def constants():
    import numpy as np
    t = np.zeros((P, CW), np.float32)
    i = np.arange(P)
    t[:, CI:CI + P] = np.eye(P)
    t[:, CSEL:CSEL + 16] = i[:, None] % 32 == np.arange(16)[None]
    t[:, CU:CU + P] = i[:, None] <= i[None, :]
    t[:, CL:CL + P] = i[:, None] >= i[None, :]
    t[:, CMF:CMF + P] = np.where(i[None, :] <= i[:, None], 0, NEG)
    t[:, CMB:CMB + P] = np.where(i[None, :] >= i[:, None], 0, NEG)
    for b in range(NB):
        qc = QC * b + QC - 1 - i % QC
        cs = np.clip(qc - 8, 0, GW - 16)
        kc = KSTART[b] + np.arange(KC)
        ok = (kc[None] >= cs[:, None]) & (kc[None] < cs[:, None] + 16)
        t[:, CNM + b * KC:CNM + (b + 1) * KC] = np.where(ok, 0, NEG)
    for g, w in enumerate(WINDOWS):
        for side, tt in enumerate((np.arange(8), np.arange(CTX - 8, CTX))):
            lo = np.clip(tt - w // 2, 0, CTX - 1)
            hi = np.clip(tt - w // 2 + w - 1, 0, CTX - 1)
            t[:, CED + g * 16 + side * 8:CED + g * 16 + side * 8 + 8] = w / (hi - lo + 1).astype(np.float32)
    half = DK // 2
    inv = (10000.0 ** (-np.arange(0, half, 2, dtype=np.float32) / half)).astype(np.float32)
    for lt in range(LT):
        tk = lt * P + i
        for part, pos in enumerate((tk // GW, tk % GW)):
            a = pos[:, None].astype(np.float32) * inv[None]
            c, s = np.cos(a), np.sin(a)
            o = lt * DK + part * 32
            t[:, CCOS + o:CCOS + o + 32] = np.concatenate([c, c], 1)
            t[:, CSIN + o:CSIN + o + 32] = np.concatenate([-s, s], 1)
    return t


def build(nc, A, out):
    ctx = ExitStack()
    with ctx:
        def sb(name, width, dt=F32, parts=P):
            return ctx.enter_context(nc.sbuf_tensor(name, [parts, width], dt))

        made = {}

        def sem(name):
            if name not in made:
                made[name] = ctx.enter_context(nc.semaphore(name))
            return made[name]

        def dram(name, shape):
            return nc.dram_tensor(name, shape, F32, kind="Internal").ap()

        SLOT = KD * 512
        x_at = (nc.sbuf_base + 31) // 32 * 32
        x_raw = sb("x_sb", NT * D)[:, :]
        x_sb = x_raw.rearrange("p (t d) -> p t d", t=NT)
        ring_at = (nc.sbuf_base + 31) // 32 * 32
        ring_lo = sb("ring_lo", 3 * SLOT)
        ZW = 29000
        zone_at = (nc.sbuf_base + 31) // 32 * 32
        zone = sb("zone", ZW)

        def rounded(name, width, at_):
            return nc.alloc_sbuf_tensor_at(name, [P, width], F32R, offset=at_)[:, :]

        hi_r = rounded("hi_r", NT * D, zone_at).rearrange("p (k t) -> p k t", k=KD)
        lo_r = rounded("lo_r", NT * D, x_at).rearrange("p (k t) -> p k t", k=KD)
        ring_r = rounded("ring_r", 3 * SLOT, ring_at)
        cst = sb("cst", CW)
        ones = sb("ones", P)
        small = sb("small", 3260)

        def slot_ap(s):
            return ring_lo[:, s * SLOT:(s + 1) * SLOT] if s < 3 else zone[:, (s - 3) * SLOT:(s - 2) * SLOT]

        def cut(area, off, pattern=None, width=None, parts=P, **k):
            ap = area[0:parts, off:off + width]
            return ap.rearrange(pattern, **k) if pattern else ap

        mg_wb = [ring_lo[:, 2048 * i:2048 * i + 2048].rearrange("p (k n) -> p k n", k=KB) for i in range(2)]

        def unit_hi(s, area=ring_lo):
            return area[:, s * SLOT + 2048:s * SLOT + 4096]

        def unit_lo(s, area=ring_lo):
            return area[:, s * SLOT:s * SLOT + 2048]

        ident = cst[:, CI:CI + P]
        tri_f, tri_b = cst[:, CU:CU + P], cst[:, CL:CL + P]
        mask_d = [cst[:, CMF:CMF + P], cst[:, CMB:CMB + P]]

        at = [0]

        def sm(width, pattern=None, **k):
            o = at[0]
            at[0] += width
            assert at[0] <= 3260
            return cut(small, o, pattern, width, **k)

        NP_ROWS = 100
        stage = [sm(P) for _ in range(DEPTH)]
        pcol = [sm(NP_ROWS) for _ in range(DEPTH)]
        csil = sm(KD * 32, "p (k m) -> p k m", k=KD)
        modc = [sm(96, "p (m s) -> p m s", m=48) for _ in range(DEPTH)]
        cA = [sm(16, "p (k s) -> p k s", k=KD) for _ in range(2)]
        cS = [sm(16, "p (k s) -> p k s", k=KD) for _ in range(2)]
        cG = [sm(16, "p (k s) -> p k s", k=KD) for _ in range(2)]
        ss, ssx, rstd = sm(NT), sm(NT), sm(NT)
        gw = sm(KD * 32, "p (k n) -> p k n", k=KD)
        rw = sm(KD * 32, "p (k n) -> p k n", k=KD)
        gbias = sm(16)
        gates = sm(NT * 16, "p (c g) -> p c g", c=NT)

        def g48(n=1):
            return [sm(48, "p (r c h) -> p r c h", r=2, c=NT) for _ in range(n)]

        lf, gb, ga, gbl, gt1, mprev, mlast, amax, cmax, mt, xp0, xp1, xp2, xp3 = g48(14)
        rden, dn = sm(4), sm(4)
        mx8 = sm(8)
        nmx = sm(4)
        rsum = sm(4)
        rrec = sm(4)
        hss, hrr = sm(4 * NT), sm(4 * NT)
        epsc = sm(1)

        hF = cut(zone, 18432, "p (k t) -> p k t", 6144, k=KD)
        part = cut(zone, 27440, None, TOK)
        brT = cut(zone, 6144, "p (b k t) -> p b k t", 9216, b=3, k=KB)
        Z0 = 15360
        qk_tm = cut(zone, 9216, "p (c n) -> p c n", 3072, c=NT)
        hsum = cut(zone, 12288, "p (c n) -> p c n", 3072, c=NT)
        o = Z0
        v_ext = cut(zone, o, "p (c h n) -> p c h n", 3096, c=NT, h=MH); o += 3096
        qT = cut(zone, o, "p (g t) -> p g t", 1536, g=2); o += 1536
        kT = cut(zone, o, "p (g t) -> p g t", 1536, g=2); o += 1536
        Cst = cut(zone, o, "p (r g n) -> p r g n", 516, r=2, g=2); o += 516
        dmat = cut(zone, o, None, 512); o += 512
        sd = cut(zone, o, None, 512); o += 512
        sdT = cut(zone, o, None, 512); o += 512
        qcs = cut(zone, o, "p (g h n) -> p g h n", 516, g=2, h=2); o += 516
        nd = cut(zone, o, "p (g h n) -> p g h n", 516, g=2, h=2); o += 516
        vws = cut(zone, o, "p (h n) -> p h n", 516, h=MH); o += 516
        Cdec = cut(zone, o, "p (g n) -> p g n", 258, g=2); o += 258
        htmp = cut(zone, o, None, 512); o += 512
        osig = [cut(zone, o, None, 512), sdT]; o += 512
        hfin = [htmp, sd]
        t_rope = [cut(zone, o + 512 * i, None, 512) for i in range(2)]; o += 1024
        assert o <= ZW, o
        o = Z0
        qnL = cut(zone, o, "p (f b q) -> p f b q", 2048, f=KB, b=NB); o += 2048
        qnC = cut(zone, o, "p (f t) -> p f t", 1024, f=KB); o += 1024
        knT = cut(zone, o, "p (f t) -> p f t", 3072, f=KB); o += 3072
        vw = [cut(zone, 9216 + 1024 * i, "p (u n) -> p u n", 1024, u=2) for i in range(2)]
        vctx = cut(zone, 11264, "p (u n) -> p u n", 1024, u=2)
        tab = cut(zone, o, "p (h w) -> p h w", 2048, h=4); o += 2048
        bm = [cut(zone, o + 512 * i, "p (h j k) -> p h j k", 512, h=2, j=ROWS) for i in range(2)]; o += 1024
        vstage = [cut(zone, o + 512 * i, None, 512) for i in range(2)]
        pr = [[cut(zone, o + 1024 * i + 512 * q, None, 512) for q in range(2)] for i in range(2)]; o += 2048
        prT = [cut(zone, o + 512 * q, None, 512) for q in range(2)]; o += 1024
        dg = [[cut(zone, o + 256 * i + P * q, None, P) for q in range(2)] for i in range(2)]; o += 512
        assert o <= ZW, o
        modr = cut(zone, 26900, "p (u n) -> p u n", 1536, u=12)
        o = Z0
        pu = cut(zone, o, "p (g t) -> p g t", 4 * PADW, g=4); o += 4 * PADW
        pA = cut(zone, o, "p (g t) -> p g t", 4 * PADW, g=4); o += 4 * PADW
        pB = cut(zone, o, "p (g t) -> p g t", 4 * PADW, g=4); o += 4 * PADW
        pin = cut(zone, o, "p (g t) -> p g t", 4 * TOK, g=4); o += 4 * TOK
        pw = cut(zone, o, "p (g n) -> p g n", 512, g=4); o += 512
        assert o <= ZW, o
        acc = cut(zone, Z0, "p (f t) -> p f t", 6144, f=KD)
        sg = [cut(zone, 21504 + 768 * i, None, 768) for i in range(2)]
        mtmp = [cut(zone, 23040 + 768 * i, None, 768) for i in range(2)]
        grow = cut(zone, 26900, "p (s d) -> p s d", 2048, s=2)
        ytmp = [cut(zone, 21504 + 1024 * i, None, 1024) for i in range(2)]
        yjunk = cut(zone, 23552, None, 1024)
        xn = cut(zone, 12288, "p (t d) -> p t d", 6144, t=NT)
        h2T = cut(zone, 18432, "p (k t) -> p k t", 6144, k=KD)
        junk = cut(zone, 24600, None, 1024)
        affn = cut(zone, 24600, "p (t e) -> p t e", NT * NE, t=NT)
        affT = cut(zone, 24700, None, TOK, parts=NE)
        tv = cut(zone, 25500, None, 96, parts=NE)
        ti = cut(zone, 25600, None, 96, parts=NE).bitcast(U32)
        tif = cut(zone, 25700, None, 96, parts=NE)
        gidx = cut(zone, 25800, None, NE + 2).bitcast(U32)
        icur = cut(zone, 25820, None, 1).bitcast(U32)
        twide = cut(zone, 26100, "p (x g n) -> p x g n", 512, parts=NE, x=2, g=2)
        gval = cut(zone, 25822, "p (g e) -> p g e", 2 * NE, g=2)
        sidx = cut(zone, 25854, "p (g e) -> p g e", 2 * NE, g=2).bitcast(U32)
        gcur = cut(zone, 25886, None, 2)
        iprev = cut(zone, 25888, None, 2).bitcast(U32)
        aexp = cut(zone, 25900, "p (t e) -> p t e", NT * NE, t=NT)
        asum, arec = cut(zone, 26000, None, NT), cut(zone, 26010, None, NT)
        xe = cut(zone, 18432, None, 1024)
        xeT = cut(zone, 19456, "p (k c) -> p k c", 768, k=KD)
        gsil = cut(zone, 20224, None, 768)
        hidm = cut(zone, 20992, None, 768)
        hidL = cut(zone, 21760, "p (b g m) -> p b g m", 512, b=4, g=2)
        hidC = cut(zone, 22272, "p (b g m) -> p b g m", 256, b=2, g=4)
        ytm = cut(zone, 22528, None, 768)

        PS = [ctx.enter_context(nc.psum_tensor(f"ps{i}", [P, 1024], F32)) for i in range(4)]

        def bank(j):
            return PS[j // 2][:, (j % 2) * 512:(j % 2) * 512 + 512]

        v_dram = [dram(f"v_dram{l}", (S, BW)) for l in range(DEPTH)]
        xn_dram = [dram(f"xn_dram{l}", (TOK, D)) for l in range(DEPTH)]
        x_dram = [dram(f"x_dram{l}", (S, D)) for l in range(DEPTH)]
        moe_dram = [dram(f"moe_dram{l}", (TOK, D)) for l in range(DEPTH)]

        units, filled = {}, [0] * 6

        def add(key, src, slot, pat, **k):
            filled[slot] += 1
            units[key] = (src, slot, filled[slot], pat, k)

        w_in, ada, wbr, wout = A["w_in"], A["ada_w"], A["w_branch"], A["w_out"]

        def kn512(w, c):
            return w[:, c:c + 512].rearrange("(k p) n -> p k n", p=P)

        moe_base = []
        for l in range(DEPTH):
            n = [0]

            def nxt(key, src):
                add((l,) + key, src, n[0] % 3, None)
                n[0] += 1
            if l == 0:
                for j in range(12):
                    nxt(("ada", 0, j), kn512(ada[0], 512 * j))
            for name, c in (("qk", C_QK), ("v", C_V), ("o", C_O), ("kn", C_KN), ("qn", C_QN), ("vn", C_VN),
                            ("pu", C_PU)):
                for half in range(2):
                    nxt((name, half), w_in[l][512 * half:512 * half + 512, c:c + 512].rearrange("(k p) n -> p k n", p=P))
                if name == "v" and l + 1 < DEPTH:
                    for j in range(12):
                        nxt(("ada", l + 1, j), kn512(ada[l + 1], 512 * j))
            assert n[0] % 3 == 2
            for q in range(12):
                c = C_BG + 256 * q
                add((l, "bg", q), w_in[l][:, c:c + 256].rearrange("(k p) n -> p k n", p=P), 2 - q % 2, None)
            for j in range(2):
                add((l, "wout", j), kn512(wout[l], 512 * j), 2 - j, None)
            moe_base.append(list(filled))
            for s in range(6):
                filled[s] += NE

        SPLITS = [(name, half) for name in ("qk", "v", "o", "kn", "qn", "vn", "pu") for half in range(2)] \
            + [("bg", q) for q in range(12)]
        NSP = len(SPLITS)

        PER = dict(half=7, h_hi=8, x_back=32, hss=1, hroot=1, m_nd=12, m_qcs=12, fabs=1, ga=1, gexp=1, gsum=1, lf=1, logit=1, aff=1, afftr=1, asub=1, aexp=1, top=1,
                   toptr=1, softp=1, n3_ss=6, x_tile=6, xn_out=16, m_C0=1, pu=4, pw_in=16, arow=12, amax=12,
                   qk_tr=6, qkT=6, m_arow=12, m_s=12, m_qc=12, m_sd=12, m_sdt=12, m_sdT=12, m_num=12, m_h=12,
                   m_dm=12, m_D=12, m_kv=10, m_vw=10, m_C=10, mg_mm=24, mg_sg=24, mg_free=26,
                   mg_tfree=26, unit_done=96, gsil=16, hid=17, hid_T=16, hidL=16, icur=17, iprev=16, ig_free=17, xe_T=17, xeT=17, y_T=16,
                   yfm=32, ytm=17, xe_in=288, y_added=512, proj=13, proj_out=12, np=14, np_out=14, oproj=6,
                   osig=6, hfin=6, mT=6, mtr=6, tab_in=256, a_bm=16, a_s=48, a_exp=48, a_max=48, a_tr=48, a_dg=24,
                   a_pT0=24, a_pT1=24, a_pv=24, a_fin=12, pup=4, pin=4, pmap=4, y=6, yss=6, y_free=8)

        def w_ready(s):
            return sem(f"w_ready{s}")

        released = {}

        def phase_end(eng, n):
            eng.drain().then_inc(sem("phase"), 1)
            eng.wait_ge(sem("phase"), 4 * n)
        NPH = 13

        def nt(l):
            return NT if l == 0 else LT

        def TW(l):
            return P * nt(l)

        def streams(l):
            return [(0, 0, S)] + ([(1, S, CTX)] if l == 0 else [])

        def both():
            return [(0, 0, S), (1, S, CTX)]

        SETS = [[(0, 0, 64, 2, 0), (1, 64, 32, 4, 512)], [(0, 0, 64, 2, 0)]]
        nslot = [96, 64]
        FW, BWD = [4, 5, 0, 1, 2, 3], [5, 4, 3, 2, 1, 0]

        def scan_outputs(l):
            return [(r, (FW, BWD)[r][st]) for st in range(6) for r in range(2) if (FW, BWD)[r][st] < nt(l)]

        def att_steps(l):
            st = [("L", hg, b, 2 * hg + i) for hg in range(2) for b in range(NB) for i in range(2)]
            if l == 0:
                st += [("C", hg, b, 2 * hg + i) for hg in range(2) for b in range(CT) for i in range(2)]
            return st

        POOL_ORDER = (3, 2, 1, 0)

        block = ctx.enter_context(nc.Block())

        @block.tensor
        def _(pe):
            mm, tr = nc.tensor.matmul, nc.tensor.transpose

            def unit(key):
                src, slot, count, _, _ = units[key]
                pe.wait_ge(w_ready(slot), 16 * count)
                return slot_ap(slot)

            def k8(w):
                return w.rearrange("p (k n) -> p k n", k=KD)

            def split_unit(l, *key):
                pe.wait_ge(sem("w_lo"), l * NSP + SPLITS.index(key) + 1)
                s = units[(l,) + key][1]
                return [x(s, ring_r).rearrange("p (k n) -> p k n", k=4) for x in (unit_hi, unit_lo)]

            def rows3(dst, k, kk, t, w, start, stop):
                for n, (a, b) in enumerate(((hi_r, w[0]), (hi_r, w[1]), (lo_r, w[0]))):
                    i = mm(dst, a[:, k, t * P:(t + 1) * P], b[:, kk, :], start=start and n == 0, stop=stop and n == 2)
                return i

            def cols3(dst, k, kk, f, t0, tw, w, start, stop):
                for n, (a, b) in enumerate(((hi_r, w[0]), (hi_r, w[1]), (lo_r, w[0]))):
                    i = mm(dst[:, t0:t0 + tw], b[:, kk, f * P:(f + 1) * P], a[:, k, t0:t0 + tw],
                           start=start and n == 0, stop=stop and n == 2)
                return i

            def ada_unit(l, la, j, b):
                w = k8(unit((l, "ada", la, j)))
                for k in range(KD):
                    for q in range(4):
                        i = mm(bank(b)[32 * q:32 * q + 32, (j % 4) * P:(j % 4 + 1) * P], csil[:, k, :],
                               w[:, k, q * P:(q + 1) * P], start=(k == 0), stop=(k == KD - 1),
                               skip_group_check=True)
                i.then_inc(sem("ada_done"), 1)
                released[l, "ada", la, j] = ("ada_done", 12 * la + j + 1)

            def ada_columns(la, banks):
                pe.wait_ge(sem("ada_rows"), 3 * la + 3)
                for j in range(12):
                    i = tr(bank(banks[j // 4])[:, (j % 4) * P:(j % 4 + 1) * P], modr[:, j, :], ident)
                i.then_inc(sem("ada_T"), 1)

            pe.wait_ge(sem("const_in"), 16)
            pe.wait_ge(sem("ones_set"), 1)
            for l in range(DEPTH):
                ph = NPH * l
                first = l == 0
                if first:
                    pe.wait_ge(sem("stage_in"), 80 * DEPTH)
                    for j in range(DEPTH):
                        i = tr(bank(0)[:, j * P:j * P + NP_ROWS], stage[j][0:NP_ROWS, :], ident[0:NP_ROWS, 0:NP_ROWS])
                    i.then_inc(sem("stage_T"), 1)
                    pe.wait_ge(sem("csil"), 1)
                    for j in range(12):
                        ada_unit(0, 0, j, 1 + j // 4)
                    ada_columns(0, (4, 5, 6))
                phase_end(pe, ph + 1)

                def to_columns(tag, tiles):
                    for k in range(KD):
                        if k == 0:
                            pe.wait_ge(sem(f"{tag}_xn{l}"), tiles)
                        if k >= 4:
                            pe.wait_ge(sem(f"{tag}_colL"), l * KD + k - 3)
                            if tiles > LT:
                                pe.wait_ge(sem(f"{tag}_colC{l}"), k - 3)
                        for t in range(tiles):
                            i = tr(PS[k % 4][:, t * P:(t + 1) * P], xn[:, t, k * P:(k + 1) * P], ident)
                        i.then_inc(sem(f"{tag}_T"), 1)
                to_columns("n1", NT)
                phase_end(pe, ph + 2)

                for u, name in enumerate(("qk", "v")):
                    for half in range(2):
                        w = split_unit(l, name, half)
                        for t in range(NT):
                            g = NT * u + t
                            if g >= 8 and half == 0:
                                pe.wait_ge(sem("proj_out"), l * PER["proj_out"] + g - 7)
                            for k in range(4):
                                i = rows3(bank(g % 8), 4 * half + k, k, t, w, half == 0 and k == 0, half == 1 and k == 3)
                            if half:
                                i.then_inc(sem("proj"), 1)
                            elif t == NT - 1:
                                i.then_inc(sem("half"), 1)
                        released[l, name, half] = ("proj", l * PER["proj"] + NT * u + NT) if half else \
                            ("half", l * PER["half"] + u + 1)
                pe.wait_ge(sem("proj_out"), l * PER["proj_out"] + 8)
                pe.wait_ge(sem("gw_in"), 48 * (l + 1))
                for n, (src, k) in enumerate([(src, k) for src in (hi_r, lo_r) for k in range(KD)]):
                    q = k % 4
                    for _, t0, tw in both():
                        i = mm(PS[2][32 * q:32 * q + 32, t0:t0 + tw], gw[:, k, :], src[:, k, t0:t0 + tw].bitcast(F32),
                               start=(n < 4), stop=(n >= 12), skip_group_check=True)
                i.then_inc(sem("narrow"), 1)
                pe.wait_ge(sem("part"), 2 * l + 1)
                for t in range(NT):
                    i = mm(bank(6)[:, t * 16:(t + 1) * 16], part[:, t * P:(t + 1) * P], cst[:, CSEL:CSEL + 16],
                           start=True, stop=True)
                i.then_inc(sem("proj"), 1)
                phase_end(pe, ph + 3)

                pe.wait_ge(sem("lf"), l * PER["lf"] + 1)
                mm(bank(0)[:, 0:24], tri_f, lf[:, 0].rearrange("p c h -> p (c h)"), start=True, stop=True)
                mm(bank(0)[:, 24:48], tri_b, lf[:, 1].rearrange("p c h -> p (c h)"), start=True, stop=True)
                mm(bank(0)[:, 48:96], ones[:, :], lf.rearrange("p r c h -> p (r c h)"), start=True, stop=True)\
                    .then_inc(sem("gsum"), 1)
                pe.wait_ge(sem("ga"), l * PER["ga"] + 1)

                def a_rows(dst, r, c):
                    for h in range(MH):
                        i = mm(dst[:, h * P:(h + 1) * P], ga[:, r, c, h:h + 1].to_broadcast([P, P]), ident,
                               start=True, stop=True)
                    return i
                n = 0
                for r in range(2):
                    for c in range(NT):
                        if n >= 2:
                            pe.wait_ge(sem("amax"), l * PER["amax"] + n - 1)
                        a_rows(bank(1 + n % 2), r, c).then_inc(sem("arow"), 1)
                        n += 1
                for c in range(NT):
                    if c >= 2:
                        pe.wait_ge(sem("qkT"), l * PER["qkT"] + c - 1)
                    for j in range(4):
                        i = tr(bank(3 + c % 2)[:, j * P:(j + 1) * P], qk_tm[:, c, j * P:(j + 1) * P], ident)
                    i.then_inc(sem("qk_tr"), 1)
                phase_end(pe, ph + 4)

                outs = scan_outputs(l)

                def prep(u):
                    r, c = outs[u]
                    if u:
                        pe.wait_ge(sem("m_dm"), l * PER["m_dm"] + u)
                    a_rows(bank(0), r, c).then_inc(sem("m_arow"), 1)
                    if u:
                        pe.wait_ge(sem("m_sd"), l * PER["m_sd"] + u)
                    for h in range(MH):
                        q0 = 64 * (h % 2)
                        i = mm(bank(4 + h % 2)[:, (h // 2) * P:(h // 2 + 1) * P], qT[q0:q0 + 64, h // 2, c * P:(c + 1) * P],
                               kT[q0:q0 + 64, h // 2, c * P:(c + 1) * P], start=True, stop=True)
                    i.then_inc(sem("m_s"), 1)
                prep(0)
                for n in range(12):
                    st, r = n // 2, n % 2
                    c = (FW, BWD)[r][st]
                    if first:
                        if n in (4, 8):
                            pe.wait_ge(sem("ada_rows"), 3 + n // 4)
                        ada_unit(0, 1, n, 1)
                    outp = c < nt(l)
                    if outp:
                        u = outs.index((r, c))
                        if st:
                            pe.wait_ge(sem("m_C"), l * PER["m_C"] + n - 1)
                        else:
                            pe.wait_ge(sem("m_C0"), l * PER["m_C0"] + 1)
                        if u:
                            pe.wait_ge(sem("m_nd"), l * PER["m_nd"] + u)
                        for h in range(MH):
                            q0 = 64 * (h % 2)
                            i = mm(bank(2 + h % 2)[:, (h // 2) * 129:(h // 2) * 129 + 129],
                                   qT[q0:q0 + 64, h // 2, c * P:(c + 1) * P], Cst[q0:q0 + 64, r, h // 2, :],
                                   start=True, stop=True)
                        i.then_inc(sem("m_qc"), 1)
                        pe.wait_ge(sem("m_sd"), l * PER["m_sd"] + u + 1)
                        for h in range(MH):
                            i = tr(bank(7)[:, h * P:(h + 1) * P], sd[:, h * P:(h + 1) * P], ident)
                        i.then_inc(sem("m_sdt"), 1)
                        if u + 1 < len(outs):
                            prep(u + 1)
                    if st < 5:
                        pe.wait_ge(sem("m_vw"), l * PER["m_vw"] + n + 1)
                        if n:
                            pe.wait_ge(sem("m_C"), l * PER["m_C"] + n)
                        for h in range(MH):
                            q0 = 64 * (h % 2)
                            i = mm(PS[3][q0:q0 + 64, (h // 2) * 129:(h // 2) * 129 + 129],
                                   qk_tm[:, c, 256 + h * 64:256 + h * 64 + 64], vws[:, h, :], start=True, stop=True)
                        i.then_inc(sem("m_kv"), 1)
                    if outp:
                        pe.wait_ge(sem("m_sdT"), l * PER["m_sdT"] + u + 1)
                        pe.wait_ge(sem("m_qcs"), l * PER["m_qcs"] + u + 1)
                        for h in range(MH):
                            i = mm(bank(2 + h % 2)[:, (h // 2) * 129:(h // 2) * 129 + 129],
                                   sdT[:, h * P:(h + 1) * P], v_ext[:, c, h, :], start=True, stop=True)
                        i.then_inc(sem("m_num"), 1)
                if first:
                    ada_columns(1, (1, 7, 0))
                phase_end(pe, ph + 5)
                def head_cols(t):
                    pe.wait_ge(sem("hfin"), l * PER["hfin"] + t + 1)
                    if t >= 2:
                        pe.wait_ge(sem("mT"), l * PER["mT"] + t - 1)
                    for j in range(KB):
                        i = tr(bank(6 + t % 2)[:, j * P:(j + 1) * P], hfin[t % 2][:, j * P:(j + 1) * P], ident)
                    i.then_inc(sem("mtr"), 1)
                for half in range(2):
                    w = split_unit(l, "o", half)
                    for t in range(nt(l)):
                        for k in range(4):
                            i = rows3(bank(t), 4 * half + k, k, t, w, half == 0 and k == 0, half == 1 and k == 3)
                        if half:
                            i.then_inc(sem("oproj"), 1)
                            if t:
                                head_cols(t - 1)
                        elif t == nt(l) - 1:
                            i.then_inc(sem("half"), 1)
                head_cols(nt(l) - 1)
                released[l, "o", 0] = ("half", l * PER["half"] + 3)
                released[l, "o", 1] = ("oproj", l * PER["oproj"] + nt(l))
                phase_end(pe, ph + 6)

                def features(name, tag, g0, sts, free, order=range(KB)):
                    for half in range(2):
                        w = split_unit(l, name, half)
                        for f in order:
                            if half == 0 and free:
                                pe.wait_ge(sem(free), l * PER[free] + g0 + f - 3)
                            for _, t0, tw in sts:
                                for k in range(4):
                                    i = cols3(PS[f], 4 * half + k, k, f, t0, tw, w, half == 0 and k == 0, half == 1 and k == 3)
                            if half:
                                i.then_inc(sem(tag), 1)
                            elif f == order[-1]:
                                i.then_inc(sem("half"), 1)
                        released[l, name, half] = (tag, l * PER[tag] + g0 + KB) if half else \
                            ("half", l * PER["half"] + SPLITS.index((name, 0)) // 2 + 1)
                features("kn", "np", 0, both(), None)
                features("qn", "np", KB, streams(l), "np_out")
                for half in range(2):
                    w = split_unit(l, "vn", half)
                    for t in range(NT):
                        if half == 0 and t % 2 == 0:
                            pe.wait_ge(sem("np_out"), l * PER["np_out"] + KB + t // 2 + 1)
                        for k in range(4):
                            i = rows3(bank(t), 4 * half + k, k, t, w, half == 0 and k == 0, half == 1 and k == 3)
                        if half:
                            i.then_inc(sem("np"), 1)
                        elif t == NT - 1:
                            i.then_inc(sem("half"), 1)
                released[l, "vn", 0] = ("half", l * PER["half"] + 6)
                released[l, "vn", 1] = ("np", l * PER["np"] + 2 * KB + NT)
                phase_end(pe, ph + 7)

                steps = att_steps(l)

                def lo_cols(n):
                    return (0, 1, 2, 3) if steps[n][0] == "L" else (2, 3)

                def scores(n):
                    kind, hg, b, f = steps[n]
                    if n >= 2:
                        pe.wait_ge(sem("a_exp"), l * PER["a_exp"] + 2 * (n - 1))
                    for part in ((0, 1) if kind == "L" else (1,)):
                        for q in range(2):
                            q0 = 64 * q
                            sp_ = bank(2 * (n % 2) + q)
                            if part == 0:
                                mm(sp_[:, 0:256], qnL[q0:q0 + 64, f, b, :],
                                   knT[q0:q0 + 64, f, 0:S].rearrange("p (j c) -> p j c", c=GW)[:, :, KSTART[b]:KSTART[b] + KC],
                                   start=True, stop=True)
                            else:
                                qs = qnL[q0:q0 + 64, f, b, :] if kind == "L" else qnC[q0:q0 + 64, f, b * P:(b + 1) * P]
                                mm(sp_[:, 256:512], qs, knT[q0:q0 + 64, f, S:TOK], start=True, stop=True)\
                                    .then_inc(sem("a_s"), 1)

                def turn(n):
                    pe.wait_ge(sem("a_dg"), l * PER["a_dg"] + n + 1)
                    for q in range(2):
                        if n:
                            pe.wait_ge(sem(f"a_pT{q}"), l * PER[f"a_pT{q}"] + n)
                        for j in lo_cols(n):
                            i = mm(bank(4 + q)[:, j * P:(j + 1) * P], pr[n % 2][q][:, j * P:(j + 1) * P], dg[n % 2][q],
                                   start=True, stop=True)
                        i.then_inc(sem("a_tr"), 1)

                def values(n):
                    kind, hg, b, f = steps[n]
                    grp = n // 2
                    if kind == "L" and n % 2 == 0:
                        pe.wait_ge(sem(f"vw_in{grp % 2}_{l}"), 128 * (grp // 2 + 1))
                    if n % 2 == 0 and grp >= 2:
                        pe.wait_ge(sem("a_fin"), l * PER["a_fin"] + grp - 1)
                    for q in range(2):
                        pe.wait_ge(sem(f"a_pT{q}"), l * PER[f"a_pT{q}"] + n + 1)
                    for j in lo_cols(n):
                        v = vw[grp % 2][:, j, :] if j < 2 else vctx[:, j - 2, :]
                        for q in range(2):
                            h = 2 * f + q
                            i = mm(bank(6 + grp % 2)[64 * q:64 * q + 64, (n % 2) * P:(n % 2 + 1) * P],
                                   v[:, h * 64:h * 64 + 64], prT[q][:, j * P:(j + 1) * P],
                                   start=(j == lo_cols(n)[0]), stop=(j == 3))
                    i.then_inc(sem("a_pv"), 1)
                scores(0)
                scores(1)
                for n in range(len(steps)):
                    turn(n)
                    if n + 2 < len(steps):
                        scores(n + 2)
                    values(n)
                phase_end(pe, ph + 8)

                features("pu", "pup", 0, streams(l), None, POOL_ORDER)
                pe.wait_ge(sem("pw_in"), l * PER["pw_in"] + 16)
                for n, gi in enumerate(POOL_ORDER):
                    pe.wait_ge(sem("pin"), l * PER["pin"] + n + 1)
                    for _, t0, tw in streams(l):
                        i = mm(PS[gi][:, t0:t0 + tw], pw[:, gi, :], pin[:, gi, t0:t0 + tw], start=True, stop=True)
                    i.then_inc(sem("pmap"), 1)
                phase_end(pe, ph + 9)

                with pe.Fori(0, 3) as bi:
                    for f in range(KD):
                        if f % 2 == 0:
                            j = f // 2
                            pe.wait_ge(sem("w_lo"), bi * 4 + (l * NSP + 14 + j + 1))
                            pe.sem_inc(sem("pe_turn"), 1)
                            wg = [x(2 - j % 2, ring_r).rearrange("p (k n) -> p k n", k=KD) for x in (unit_hi, unit_lo)]
                        pe.wait_ge(sem("mg_free"), l * PER["mg_free"] + bi * KD + (f + 1))
                        pe.sem_inc(sem("pe_turn"), 1)
                        pb, pg = PS[(f % 2) * 2], PS[(f % 2) * 2 + 1]
                        for _, t0, tw in streams(l):
                            for k in range(KD):
                                cols3(pg, k, k, f % 2, t0, tw, wg, k == 0, k == KD - 1)
                        if f % 4 == 0:
                            pe.wait_ge(sem(f"mg_in{f // 4}"), bi * 16 + 16 * (3 * l + 1))
                            pe.sem_inc(sem("pe_turn"), 1)
                        for _, t0, tw in streams(l):
                            for k in range(KB):
                                i = mm(pb[:, t0:t0 + tw], mg_wb[f // 4][:, k, (f % 4) * P:(f % 4 + 1) * P],
                                       brT[:, bass.ds(bi, 1), k, t0:t0 + tw], start=(k == 0), stop=(k == KB - 1))
                        i.then_inc(sem("mg_mm"), 1)
                phase_end(pe, ph + 10)

                def gain_rows(which, b):
                    for s in range(2):
                        for k in range(KD):
                            i = mm(PS[b + s][:, k * P:(k + 1) * P], cG[which][:, k, s:s + 1].to_broadcast([P, P]), ident,
                                   start=True, stop=True)
                        i.then_inc(sem(f"grow{which}"), 1)
                gain_rows(0, 0)
                w0, w1 = k8(unit((l, "wout", 0))), k8(unit((l, "wout", 1)))
                for t in range(nt(l)):
                    pe.wait_ge(sem("y_free"), l * PER["y_free"] + t + 1)
                    for j, w in enumerate((w0, w1)):
                        for k in range(KD):
                            i = mm(PS[2 + t % 2][:, j * 512:(j + 1) * 512], acc[:, k, t * P:(t + 1) * P], w[:, k, :],
                                   start=(k == 0), stop=(k == KD - 1))
                    i.then_inc(sem("y"), 1)
                for j in range(2):
                    released[l, "wout", j] = ("y", l * PER["y"] + nt(l))
                phase_end(pe, ph + 11)

                to_columns("n2", nt(l))
                pe.wait_ge(sem("n2_colL"), l * KD + KD)
                if first:
                    pe.wait_ge(sem(f"n2_colC{l}"), KD)
                for k in range(KD):
                    q = k % 4
                    for _, t0, tw in streams(l):
                        i = mm(PS[1][32 * q:32 * q + 32, t0:t0 + tw], rw[:, k, :], h2T[:, k, t0:t0 + tw],
                               start=(k < 4), stop=(k >= 4), skip_group_check=True)
                i.then_inc(sem("narrow"), 1)
                pe.wait_ge(sem("part"), 2 * l + 2)
                for t in range(nt(l)):
                    i = mm(bank(0)[:, t * NE:(t + 1) * NE], part[:, t * P:(t + 1) * P], cst[:, CSEL:CSEL + NE],
                           start=True, stop=True)
                i.then_inc(sem("logit"), 1)
                pe.wait_ge(sem("aff"), l * PER["aff"] + 1)
                for t in range(nt(l)):
                    i = tr(PS[1][0:NE, t * P:(t + 1) * P], affn[:, t, :], ident)
                i.then_inc(sem("afftr"), 1)
                gain_rows(1, 2)
                ns = nslot[l]
                pe.wait_ge(sem("top"), l * PER["top"] + 1)
                tr(bank(1)[0:ns, 0:NE], tif[:, 0:ns], ident[0:NE, 0:NE])
                for x in range(2):
                    for g in range(len(SETS[l])):
                        c = 16 + (2 * x + g) * NE
                        i = tr(bank(1)[:, c:c + NE], twide[:, x, g, :], ident[0:NE, 0:NE])
                i.then_inc(sem("toptr"), 1)
                phase_end(pe, ph + 12)

                def gather_T(e, add_):
                    pe.wait_ge(sem("xe_in"), l * PER["xe_in"] + 16 * e + 16 * (1 + add_))
                    pe.sem_inc(sem("pe_turn"), 1)
                    for k in range(KD):
                        i = tr(PS[0][:, k * 128:k * 128 + ns], xe[0:ns, k * P:(k + 1) * P], ident[0:ns, 0:ns])
                    i.then_inc(sem("xe_T"), 1)
                gather_T(0, 0)

                def products(src, s, lhs, banks):
                    w = slot_ap(s).rearrange("p (k n) -> p k n", k=4)
                    hk = s % 2
                    for gi, (_, c0, M, G, _) in enumerate(SETS[l]):
                        W = D // G
                        for k in range(4 * hk, 4 * hk + 4):
                            for j in range(G):
                                i = mm(bank(banks[gi])[j * M:(j + 1) * M, 0:W], lhs(gi, k), w[:, k % 4, j * W:(j + 1) * W],
                                       start=(k == 0), stop=(k == KD - 1))
                    i.then_inc(sem("unit_done"), 1)

                with pe.Fori(0, NE) as e:
                    pe.wait_ge(sem("xeT"), l * PER["xeT"] + e + 1)
                    for s in range(4):
                        if s == 2:
                            pe.wait_ge(sem("ytm"), l * PER["ytm"] + e + 1)
                            pe.sem_inc(sem("pe_turn"), 1)
                        pe.wait_ge(w_ready(s), e * 16 + 16 * (moe_base[l][s] + 1))
                        products(e, s, lambda gi, k: xeT[:, k, SETS[l][gi][1]:SETS[l][gi][1] + SETS[l][gi][2]],
                                 ((2, 4), (3, 5))[s // 2])
                    gather_T(e, 1)
                    pe.wait_ge(sem("hid"), l * PER["hid"] + e + 2)
                    for b in range(4):
                        i = tr(bank(6)[:, b * P:(b + 1) * P], hidm[:, b * P:(b + 1) * P], ident)
                    if first:
                        for b in range(2):
                            i = tr(bank(7)[:, b * P:(b + 1) * P], hidm[:, 512 + b * P:512 + (b + 1) * P], ident)
                    i.then_inc(sem("hid_T"), 1)
                    pe.wait_ge(sem("hidL"), l * PER["hidL"] + e + 1)
                    if first:
                        pe.wait_ge(sem("hidC"), e + 1)
                    for s in range(4, 6):
                        pe.wait_ge(w_ready(s), e * 16 + 16 * (moe_base[l][s] + 1))
                        products(e, s, lambda gi, k: hidL[:, k % 4, k // 4, :] if gi == 0 else hidC[:, k % 2, k // 2, :],
                                 (3, 5))
                phase_end(pe, ph + 13)

        @block.scalar
        def _(act):
            A_ = nc.scalar.activation
            n_link = [0]

            def link(ins):
                n_link[0] += 1
                ins.then_inc(sem("act_link"), 1)
                act.wait_ge(sem("act_link"), n_link[0])

            def split(l, h):
                _, slot, count, _, _ = units[(l,) + SPLITS[h]]
                act.wait_ge(w_ready(slot), 16 * count)
                A_(unit_hi(slot, ring_r), unit_lo(slot), ACT.Copy).then_inc(sem("w_hi"), 1)

            def ada_rows(la, j, b):
                act.wait_ge(sem("ada_done"), 12 * la + 4 * j + 4)
                A_(modr[:, 4 * j:4 * j + 4, :], bank(b).rearrange("p (u n) -> p u n", u=4), ACT.Copy)\
                    .then_inc(sem("ada_rows"), 1)

            for l in range(DEPTH):
                ph = NPH * l
                first = l == 0

                def root(tag, tiles):
                    A_(ssx[:, 0:tiles], ssx[:, 0:tiles], ACT.Sqrt, bias=epsc, scale=1.0 / D).then_inc(sem(f"{tag}_ss"), 1)

                if first:
                    act.wait_ge(sem("pcol"), 1)
                    A_(csil[:, :, 0:2], pcol[0][:, 0:16].rearrange("p (s k) -> p k s", s=2), ACT.Silu)\
                        .then_inc(sem("csil"), 1)
                    act.wait_ge(sem("x_in"), 32)
                    for t in range(NT):
                        link(A_(junk, x_sb[:, t, :], ACT.Square, accum_out=ssx[:, t:t + 1]))
                    root("n1", NT)
                    for j in range(3):
                        ada_rows(0, j, 1 + j)
                phase_end(act, ph + 1)

                def norm_cols(tag, tiles, dst, which):
                    act.wait_ge(sem(f"{tag}_rstd"), l + 1)
                    for t in range(0, tiles, 2):
                        A_(xn[:, t, :], x_sb[:, t, :], ACT.Copy, scale=rstd[:, t:t + 1]).then_inc(sem(f"{tag}_xn{l}"), 1)
                    for k in range(KD):
                        act.wait_ge(sem(f"{tag}_T"), l * KD + k + 1)
                        A_(dst[:, k, 0:S], PS[k % 4][:, 0:S], ACT.Identity, bias=cS[which][:, k, 0:1],
                           scale=cA[which][:, k, 0:1]).then_inc(sem(f"{tag}_colL"), 1)
                        if tag == "n1":
                            act.wait_ge(sem("n1_colL"), l * KD + k + 1)
                            act.wait_ge(sem(f"n1_colC{l}"), k + 1)
                            A_(hi_r[:, k, :], hF[:, k, :], ACT.Copy).then_inc(sem("h_hi"), 1)
                norm_cols("n1", NT, hF, 0)
                split(l, 2)
                phase_end(act, ph + 2)

                g = 0
                for name in ("qk", "v"):
                    for t in range(NT):
                        act.wait_ge(sem("proj"), l * PER["proj"] + g + 1)
                        if name == "qk":
                            A_(qk_tm[:, t, 0:256], bank(g % 8)[:, 0:256], ACT.Copy, scale=DK ** -0.5)
                            A_(qk_tm[:, t, 256:512], bank(g % 8)[:, 256:512], ACT.Copy).then_inc(sem("proj_out"), 1)
                        else:
                            A_(v_ext[:, t, :, 0:DV], bank(g % 8).rearrange("p (h n) -> p h n", h=MH), ACT.Copy)\
                                .then_inc(sem("proj_out"), 1)
                        if g == 1:
                            split(l, 3)
                        g += 1
                act.wait_ge(sem("narrow"), 2 * l + 1)
                A_(part, PS[2][:, 0:TOK], ACT.Copy).then_inc(sem("part"), 1)
                if not first:
                    split(l, 4)
                    split(l, 5)
                phase_end(act, ph + 3)

                act.wait_ge(sem("fabs"), l * PER["fabs"] + 1)
                link(A_(gt1, gt1, ACT.Exp, scale=-1.0))
                A_(gt1, gt1, ACT.Ln, bias=1.0).then_inc(sem("softp"), 1)
                for c in range(NT):
                    act.wait_ge(sem("qk_tr"), l * PER["qk_tr"] + c + 1)
                    b4 = bank(3 + c % 2).rearrange("p (j t) -> p j t", j=4)
                    A_(qT[:, :, c * P:(c + 1) * P], b4[:, 0:2, :], ACT.Copy)
                    A_(kT[:, :, c * P:(c + 1) * P], b4[:, 2:4, :], ACT.Copy).then_inc(sem("qkT"), 1)
                act.wait_ge(sem("gexp"), l * PER["gexp"] + 1)
                for t_ in (xp0, xp1, xp2, xp3):
                    A_(t_, t_, ACT.Exp)
                phase_end(act, ph + 4)

                outs = scan_outputs(l)

                def decays(u):
                    act.wait_ge(sem("m_dm"), l * PER["m_dm"] + u + 1)
                    A_(dmat, dmat, ACT.Exp).then_inc(sem("m_D"), 1)
                decays(0)
                for n in range(12):
                    r, c = n % 2, (FW, BWD)[n % 2][n // 2]
                    if c < nt(l):
                        u = outs.index((r, c))
                        act.wait_ge(sem("m_sdt"), l * PER["m_sdt"] + u + 1)
                        A_(sdT, bank(7), ACT.Copy).then_inc(sem("m_sdT"), 1)
                        if u + 1 < len(outs):
                            decays(u + 1)
                    if first and n % 4 == 3:
                        ada_rows(1, n // 4, 1)
                if first:
                    split(l, 4)
                    split(l, 5)
                phase_end(act, ph + 5)
                split(l, 6)

                def gate(t):
                    act.wait_ge(sem("oproj"), l * PER["oproj"] + t + 1)
                    if t >= 2:
                        act.wait_ge(sem("hfin"), l * PER["hfin"] + t - 1)
                    A_(osig[t % 2], bank(t), ACT.Sigmoid).then_inc(sem("osig"), 1)
                act.wait_ge(sem("hss"), l * PER["hss"] + 1)
                A_(hss[:, 0:4 * nt(l)], hss[:, 0:4 * nt(l)], ACT.Sqrt, bias=epsc, scale=1.0 / DV).then_inc(sem("hroot"), 1)
                gate(0)
                for t in range(nt(l)):
                    if t + 1 < nt(l):
                        gate(t + 1)
                    if t == 1:
                        split(l, 7)
                    act.wait_ge(sem("mtr"), l * PER["mtr"] + t + 1)
                    A_(brT[:, 0, :, t * P:(t + 1) * P], bank(6 + t % 2).rearrange("p (j t) -> p j t", j=KB), ACT.Copy)\
                        .then_inc(sem("mT"), 1)
                phase_end(act, ph + 6)

                g = 0
                split(l, 8)
                for f in range(KB):
                    act.wait_ge(sem("np"), l * PER["np"] + g + 1)
                    A_(knT[:, f, :], PS[g % 4][:, 0:TOK], ACT.Copy).then_inc(sem("np_out"), 1)
                    if f == 0:
                        split(l, 9)
                    g += 1
                split(l, 10)
                for f in range(KB):
                    act.wait_ge(sem("np"), l * PER["np"] + g + 1)
                    if first:
                        A_(qnC[:, f, :], PS[g % 4][:, S:TOK], ACT.Copy, scale=DH ** -0.5)
                    A_(qnL[:, f].rearrange("p b (r q) -> p b r q", r=ROWS),
                       PS[g % 4][:, 0:S].rearrange("p (r b q) -> p b r q", r=ROWS, b=NB)[:, :, :, ::-1], ACT.Copy, scale=DH ** -0.5)\
                        .then_inc(sem("np_out"), 1)
                    if f == 0:
                        split(l, 11)
                    g += 1
                split(l, 12)
                for t in range(NT):
                    act.wait_ge(sem("np"), l * PER["np"] + g + 1)
                    if t == 1:
                        split(l, 13)
                    if t < LT:
                        if t >= 2:
                            act.wait_ge(sem(f"v_out{t % 2}_{l}"), 16)
                        A_(vstage[t % 2], bank(t), ACT.Copy).then_inc(sem("np_out"), 1)
                    else:
                        A_(vctx[:, t - LT, :], bank(t), ACT.Copy).then_inc(sem("np_out"), 1)
                    g += 1
                phase_end(act, ph + 7)

                steps = att_steps(l)

                def probs(n):
                    lo = 0 if steps[n][0] == "L" else 256
                    if n >= 2:
                        act.wait_ge(sem("a_tr"), l * PER["a_tr"] + 2 * (n - 1))
                    for q in range(2):
                        x = 2 * (n % 2) + q
                        act.wait_ge(sem("a_max"), l * PER["a_max"] + 2 * n + q + 1)
                        A_(pr[n % 2][q][:, lo:512], bank(x)[:, lo:512], ACT.Exp, bias=nmx[:, x:x + 1],
                           accum_out=rsum[:, x:x + 1]).then_inc(sem("a_exp"), 1)
                probs(0)
                probs(1)
                for n in range(len(steps)):
                    lo = 0 if steps[n][0] == "L" else 256
                    act.wait_ge(sem("a_tr"), l * PER["a_tr"] + 2 * n + 1)
                    if n:
                        act.wait_ge(sem("a_pv"), l * PER["a_pv"] + n)
                    A_(prT[0][:, lo:512], bank(4)[:, lo:512], ACT.Copy).then_inc(sem("a_pT0"), 1)
                    if n + 2 < len(steps):
                        probs(n + 2)
                phase_end(act, ph + 8)

                for n, f in enumerate(POOL_ORDER):
                    act.wait_ge(sem("pup"), l * PER["pup"] + n + 1)
                    A_(pu[:, f, LCOL:LCOL + S], PS[f][:, 0:S], ACT.Copy)
                    if first:
                        A_(pu[:, f, CCOL:CCOL + CTX], PS[f][:, S:TOK], ACT.Copy)
                    act.drain().then_inc(sem("pu"), 1)
                for n, gi in enumerate(POOL_ORDER):
                    act.wait_ge(sem("pmap"), l * PER["pmap"] + n + 1)
                    A_(brT[:, 1, gi, 0:TW(l)], PS[gi][:, 0:TW(l)], ACT.Copy, scale=pcol[l][:, 96 + gi:97 + gi])
                split(l, 14)
                phase_end(act, ph + 9)

                for bi in range(3):
                    for f in range(KD):
                        if f % 2 == 0 and bi * 4 + f // 2 < 11:
                            split(l, 15 + bi * 4 + f // 2)
                        act.wait_ge(sem("mg_mm"), l * PER["mg_mm"] + bi * KD + (f + 1))
                        act.wait_ge(sem("mg_free"), l * PER["mg_free"] + bi * KD + (f + 1))
                        A_(sg[f % 2][:, 0:TW(l)], PS[(f % 2) * 2 + 1][:, 0:TW(l)], ACT.Sigmoid).then_inc(sem("mg_sg"), 1)
                phase_end(act, ph + 10)

                def put_rows(which, b):
                    for s in range(2):
                        act.wait_ge(sem(f"grow{which}"), 2 * l + s + 1)
                        i = A_(grow[:, s, :], PS[b + s][:, :], ACT.Copy)
                    i.then_inc(sem(f"growS{which}"), 1)
                put_rows(0, 0)
                for t in range(nt(l) + 1):
                    if t < nt(l):
                        act.wait_ge(sem("y"), l * PER["y"] + t + 1)
                        link(A_(yjunk, PS[2 + t % 2][:, :], ACT.Square, accum_out=ss[:, t:t + 1]))
                        A_(ss[:, t:t + 1], ss[:, t:t + 1], ACT.Sqrt, bias=epsc, scale=1.0 / D).then_inc(sem("yss"), 1)
                    if t:
                        act.wait_ge(sem("y_free"), l * PER["y_free"] + 2 + t)
                        link(A_(yjunk, x_sb[:, t - 1, :], ACT.Square, accum_out=ssx[:, t - 1:t]))
                root("n2", nt(l))
                phase_end(act, ph + 11)

                norm_cols("n2", nt(l), h2T, 1)
                act.wait_ge(sem("narrow"), 2 * l + 2)
                A_(part[:, 0:TW(l)], PS[1][:, 0:TW(l)], ACT.Copy).then_inc(sem("part"), 1)
                act.wait_ge(sem("asub"), l * PER["asub"] + 1)
                A_(aexp[:, 0:nt(l)], aexp[:, 0:nt(l)], ACT.Exp).then_inc(sem("aexp"), 1)
                put_rows(1, 2)
                phase_end(act, ph + 12)

                ns = nslot[l]
                act.drain().then_inc(sem("ytm"), 1)
                with act.Fori(0, NE) as e:
                    act.wait_ge(sem("unit_done"), l * PER["unit_done"] + 6 * e + 2)
                    act.wait_ge(sem("hid"), l * PER["hid"] + e + 1)
                    i = A_(gsil[:, 0:512], bank(2), ACT.Silu)
                    if first:
                        i = A_(gsil[:, 512:768], bank(4)[:, 0:256], ACT.Silu)
                    i.then_inc(sem("gsil"), 1)
                    act.wait_ge(sem("hid_T"), l * PER["hid_T"] + e + 1)
                    A_(hidL.rearrange("p b g m -> p (b g m)"), bank(6), ACT.Copy).then_inc(sem("hidL"), 1)
                    act.wait_ge(sem("iprev"), l * PER["iprev"] + e + 1)
                    act.wait_ge(sem("ig_free"), l * PER["ig_free"] + e + 1)
                    act.wait_ge(sem("unit_done"), l * PER["unit_done"] + 6 * e + 6)
                    i = A_(ytm[:, 0:512], bank(3), ACT.Copy, scale=gcur[:, 0:1])
                    if first:
                        i = A_(ytm[:, 512:768], bank(5)[:, 0:256], ACT.Copy, scale=gcur[:, 1:2])
                    i.then_inc(sem("ytm"), 1)
                phase_end(act, ph + 13)
                for t in range(nt(l) + 1):
                    if t < nt(l):
                        act.wait_ge(sem(f"moe_in{t}"), 16 * l + 16)
                        link(A_(junk, xn[:, t, :], ACT.Square, accum_out=ss[:, t:t + 1]))
                        A_(ss[:, t:t + 1], ss[:, t:t + 1], ACT.Sqrt, bias=epsc, scale=1.0 / D).then_inc(sem("n3_ss"), 1)
                    if t and l + 1 < DEPTH:
                        act.wait_ge(sem("x_tile"), l * PER["x_tile"] + t)
                        link(A_(junk, x_sb[:, t - 1, :], ACT.Square, accum_out=ssx[:, t - 1:t]))
                if l + 1 < DEPTH:
                    root("n1", NT)

        @block.vector
        def _(dve):
            V = nc.vector
            n_link = [0]

            def link(ins):
                n_link[0] += 1
                ins.then_inc(sem("dve_link"), 1)
                dve.wait_ge(sem("dve_link"), n_link[0])

            def ada_cols(la, banks):
                dve.wait_ge(sem("ada_T"), la + 1)
                for j, b in enumerate(banks):
                    src = bank(b).rearrange("p (u q m) -> p u q m", u=4, q=4)[:, :, :, 0:2]
                    i = V.tensor_tensor(modc[la][:, 16 * j:16 * j + 16, :].rearrange("p (u q) s -> p u q s", u=4), src,
                                        pcol[la][:, 48 + 16 * j:64 + 16 * j].rearrange("p (u q) -> p u q", u=4)
                                        .unsqueeze(3).to_broadcast([P, 4, 4, 2]), ALU.add)
                link(i)

            link(V.memset(csil, 0.0))
            V.memset(gw, 0.0)
            V.memset(rw, 0.0).then_inc(sem("pads_set"), 1)
            V.memset(epsc, EPS)
            V.memset(ones[:, :], 1.0).then_inc(sem("ones_set"), 1)
            dve.wait_ge(sem("const_in"), 16)
            for l in range(DEPTH):
                ph = NPH * l
                first = l == 0
                if first:
                    dve.wait_ge(sem("stage_T"), 1)
                    for j in range(DEPTH):
                        link(V.tensor_copy(pcol[j], bank(0)[:, j * P:j * P + NP_ROWS]))
                    dve.sem_inc(sem("pcol"), 1)
                    ada_cols(0, (4, 5, 6))
                for i, (sh, sc, gt, g_in, g_out) in enumerate(((0, 1, 2, 0, 1), (3, 4, 5, 2, 3))):
                    gcol = pcol[l][:, 16:48].rearrange("p (g k) -> p g k", g=4)
                    V.tensor_copy(cS[i], modc[l][:, sh * 8:sh * 8 + 8, :])
                    link(V.tensor_scalar(cA[i], modc[l][:, sc * 8:sc * 8 + 8, :], 1.0, None, ALU.add))
                    link(V.tensor_tensor(cA[i], cA[i], gcol[:, g_in, :].unsqueeze(2).to_broadcast([P, 8, 2]), ALU.mult))
                    V.tensor_tensor(cG[i], modc[l][:, gt * 8:gt * 8 + 8, :],
                                    gcol[:, g_out, :].unsqueeze(2).to_broadcast([P, 8, 2]), ALU.mult)
                phase_end(dve, ph + 1)

                def norm_cols(tag, tiles, dst, which):
                    dve.wait_ge(sem(f"{tag}_ss"), l + 1)
                    link(V.reciprocal(rstd[:, 0:tiles], ssx[:, 0:tiles]))
                    dve.sem_inc(sem(f"{tag}_rstd"), 1)
                    for t in range(1, tiles, 2):
                        V.tensor_scalar(xn[:, t, :], x_sb[:, t, :], rstd[:, t:t + 1], None, ALU.mult)\
                            .then_inc(sem(f"{tag}_xn{l}"), 1)
                    if tiles > LT:
                        for k in range(KD):
                            dve.wait_ge(sem(f"{tag}_T"), l * KD + k + 1)
                            V.tensor_scalar(dst[:, k, S:TOK], PS[k % 4][:, S:TOK], cA[which][:, k, 1:2],
                                            cS[which][:, k, 1:2], ALU.mult, ALU.add).then_inc(sem(f"{tag}_colC{l}"), 1)
                            if tag == "n1" and k:
                                low_parts(k - 1)

                def low_parts(k):
                    dve.wait_ge(sem("h_hi"), l * PER["h_hi"] + k + 1)
                    if k == 0 and not first:
                        dve.wait_ge(sem("x_out"), 16)
                    V.tensor_tensor(lo_r[:, k, :], hF[:, k, :], hi_r[:, k, :].bitcast(F32), ALU.subtract)
                norm_cols("n1", NT, hF, 0)
                low_parts(KD - 1)
                phase_end(dve, ph + 2)

                V.memset(v_ext[:, :, :, DV:DV + 1], 1.0)
                for t in range(LT):
                    dve.wait_ge(sem("proj_out"), l * PER["proj_out"] + t + 1)
                    qk = qk_tm[:, t, :].rearrange("p (h d) -> p h d", d=DK)
                    cos = cst[:, CCOS + t * DK:CCOS + (t + 1) * DK]
                    sin = cst[:, CSIN + t * DK:CSIN + (t + 1) * DK]
                    V.tensor_tensor(t_rope[0].rearrange("p (h d) -> p h d", d=DK), qk,
                                    cos.unsqueeze(1).to_broadcast([P, 8, DK]), ALU.mult)
                    x4 = qk_tm[:, t, :].rearrange("p (h r s d) -> p h r s d", h=8, r=2, s=2)
                    t4 = t_rope[1].rearrange("p (h r s d) -> p h r s d", h=8, r=2, s=2)
                    s4 = sin.rearrange("p (r s d) -> p r s d", r=2, s=2)
                    for s in range(2):
                        i = V.tensor_tensor(t4[:, :, :, s, :], x4[:, :, :, 1 - s, :],
                                            s4[:, :, s, :].unsqueeze(1).to_broadcast([P, 8, 2, 16]), ALU.mult)
                    link(i)
                    link(V.tensor_tensor(qk_tm[:, t, :], t_rope[0], t_rope[1], ALU.add))
                dve.wait_ge(sem("proj"), l * PER["proj"] + 13)
                dve.wait_ge(sem(f"gw_in"), 48 * (l + 1))
                link(V.tensor_tensor(gates, bank(6)[:, 0:96].rearrange("p (c g) -> p c g", c=NT),
                                     gbias.unsqueeze(1).to_broadcast([P, NT, 16]), ALU.add))
                phase_end(dve, ph + 3)

                g5 = gates.rearrange("p c (r i h) -> p r i c h", r=2, i=2)
                for r in range(2):
                    i = V.scalar_tensor_tensor(gt1[:, r], g5[:, r, 1], -1.0, g5[:, r, 1], ALU.mult, ALU.max)
                i.then_inc(sem("fabs"), 1)
                for r in range(2):
                    V.tensor_scalar(lf[:, r], g5[:, r, 1], 0.0, None, ALU.min)
                dve.wait_ge(sem("softp"), l * PER["softp"] + 1)
                dve.drain()
                V.tensor_tensor(lf, lf, gt1, ALU.subtract).then_inc(sem("lf"), 1)
                dve.wait_ge(sem("gsum"), l * PER["gsum"] + 1)
                V.tensor_copy(gbl.rearrange("p r c h -> p (r c h)"), bank(0)[:, 48:96])
                link(V.tensor_copy(gb.rearrange("p r c h -> p (r c h)"), bank(0)[:, 0:48]))
                for r in range(2):
                    i = V.tensor_tensor(ga[:, r], g5[:, r, 0], gb[:, r], ALU.subtract)
                i.then_inc(sem("ga"), 1)
                n = 0
                for r in range(2):
                    for c in range(NT):
                        dve.wait_ge(sem("arow"), l * PER["arow"] + n + 1)
                        b4 = bank(1 + n % 2).rearrange("p (h s) -> p h s", h=MH)
                        V.tensor_reduce(amax[:, r, c, :], b4, AX.X, ALU.max)
                        if n:
                            dve.wait_ge(sem("amax"), l * PER["amax"] + n)
                        d4 = dmat.rearrange("p (h s) -> p h s", h=MH)
                        link(V.tensor_tensor(d4, b4, mask_d[r].unsqueeze(1).to_broadcast([P, MH, P]), ALU.add))
                        V.tensor_reduce(cmax[:, r, c, :], d4, AX.X, ALU.max).then_inc(sem("amax"), 1)
                        n += 1
                for r in range(2):
                    order = (FW, BWD)[r]
                    link(V.memset(mprev[:, r, order[0], :], NEG))
                    for st in range(6):
                        c = order[st]
                        link(V.tensor_tensor(mlast[:, r, c, :], mprev[:, r, c, :], amax[:, r, c, :], ALU.max))
                        if st < 5:
                            link(V.tensor_tensor(mprev[:, r, order[st + 1], :], gbl[:, r, c, :], mlast[:, r, c, :], ALU.add))
                link(V.tensor_tensor(mt, mprev, cmax, ALU.max))
                V.tensor_tensor(xp0, mprev, mt, ALU.subtract)
                V.tensor_tensor(xp1, ga, mlast, ALU.subtract)
                V.tensor_tensor(xp2, mprev, mlast, ALU.subtract)
                link(V.tensor_tensor(xp3, gb, mt, ALU.add))
                link(V.tensor_scalar(xp3, xp3, -1.0, None, ALU.mult))
                dve.sem_inc(sem("gexp"), 1)
                V.memset(hsum[:, 0:nt(l), :], 0.0)
                link(V.memset(Cst, 0.0))
                dve.sem_inc(sem("m_C0"), 1)
                phase_end(dve, ph + 4)

                def two(ps, n):
                    return ps[:, :].rearrange("p (q x) -> p q x", q=2)[:, :, 0:2 * n].rearrange("p q (g n) -> p q g n", g=2)

                def by_parity(row):
                    return row.rearrange("p (g q n) -> p q g n", g=2, q=2)

                def cols(v):
                    return v.rearrange("p (g q) -> p q g", g=2)
                outs = scan_outputs(l)

                def exponents(u):
                    r, c = outs[u]
                    d4 = dmat.rearrange("p (h s) -> p h s", h=MH)
                    dve.wait_ge(sem("m_arow"), l * PER["m_arow"] + u + 1)
                    link(V.tensor_tensor(d4, bank(0).rearrange("p (h s) -> p h s", h=MH),
                                         mask_d[r].unsqueeze(1).to_broadcast([P, MH, P]), ALU.add))
                    V.tensor_tensor(d4, d4, mt[:, r, c, :].unsqueeze(2).to_broadcast([P, MH, P]), ALU.subtract)\
                        .then_inc(sem("m_dm"), 1)
                exponents(0)
                for n in range(12):
                    st, r = n // 2, n % 2
                    c = (FW, BWD)[r][st]
                    outp = c < nt(l)
                    if outp:
                        u = outs.index((r, c))
                        dve.wait_ge(sem("m_s"), l * PER["m_s"] + u + 1)
                        dve.wait_ge(sem("m_D"), l * PER["m_D"] + u + 1)
                        V.tensor_tensor(by_parity(sd), two(PS[2], P), by_parity(dmat), ALU.mult).then_inc(sem("m_sd"), 1)
                        dve.wait_ge(sem("m_qc"), l * PER["m_qc"] + u + 1)
                        V.tensor_tensor(qcs, two(PS[1], 129), cols(xp0[:, r, c, :]).unsqueeze(3).to_broadcast([P, 2, 2, 129]),
                                        ALU.mult).then_inc(sem("m_qcs"), 1)
                        if u + 1 < len(outs):
                            exponents(u + 1)
                    if st < 5:
                        dve.wait_ge(sem("m_kv"), l * PER["m_kv"] + n + 1)
                        for q in range(2):
                            V.tensor_tensor(Cdec[64 * q:64 * q + 64], Cst[64 * q:64 * q + 64, r],
                                            xp2[64 * q:64 * q + 64, r, c, q::2].unsqueeze(2).to_broadcast([64, 2, 129]),
                                            ALU.mult)
                        dve.drain()
                        V.tensor_tensor(Cst[:, r], Cdec, PS[3][:, 0:258].rearrange("p (g n) -> p g n", g=2), ALU.add)\
                            .then_inc(sem("m_C"), 1)
                    if outp:
                        dve.wait_ge(sem("m_num"), l * PER["m_num"] + u + 1)
                        V.tensor_tensor(nd, qcs, two(PS[1], 129), ALU.add).then_inc(sem("m_nd"), 1)
                        dve.wait_ge(sem("m_nd"), l * PER["m_nd"] + u + 1)
                        dn2 = dn.rearrange("p (q g) -> p q g", q=2)
                        link(V.scalar_tensor_tensor(dn2, nd[:, :, :, 128], -1.0,
                                                    nd[:, :, :, 128], ALU.mult, ALU.max))
                        link(V.tensor_tensor(dn2, dn2, cols(xp3[:, r, c, :]), ALU.max))
                        link(V.reciprocal(rden, dn))
                        link(V.tensor_tensor(by_parity(htmp), nd[:, :, :, 0:128], rden.rearrange("p (q g) -> p q g", q=2)
                                             .unsqueeze(3).to_broadcast([P, 2, 2, 128]), ALU.mult))
                        link(V.tensor_tensor(hsum[:, c, :], hsum[:, c, :], htmp, ALU.add))
                if first:
                    ada_cols(1, (1, 7, 0))
                phase_end(dve, ph + 5)
                for t in range(nt(l)):
                    link(V.tensor_tensor(dmat, hsum[:, t, :], hsum[:, t, :], ALU.mult))
                    link(V.tensor_reduce(hss[:, 4 * t:4 * t + 4], dmat.rearrange("p (h n) -> p h n", h=MH), AX.X, ALU.add))
                dve.sem_inc(sem("hss"), 1)
                dve.wait_ge(sem("hroot"), l * PER["hroot"] + 1)
                link(V.reciprocal(hrr[:, 0:4 * nt(l)], hss[:, 0:4 * nt(l)]))
                for t in range(nt(l)):
                    hs = hsum[:, t, :].rearrange("p (h n) -> p h n", h=MH)
                    link(V.tensor_tensor(hs, hs, hrr[:, 4 * t:4 * t + 4].unsqueeze(2).to_broadcast([P, MH, DV]), ALU.mult))
                    if t >= 2:
                        dve.wait_ge(sem("mtr"), l * PER["mtr"] + t - 1)
                    dve.wait_ge(sem("osig"), l * PER["osig"] + t + 1)
                    V.tensor_tensor(hfin[t % 2], hsum[:, t, :], osig[t % 2], ALU.mult).then_inc(sem("hfin"), 1)
                phase_end(dve, ph + 6)
                phase_end(dve, ph + 7)

                steps = att_steps(l)

                def fin(grp):
                    kind, hg, b, _ = steps[grp * 2]
                    dve.wait_ge(sem("a_pv"), l * PER["a_pv"] + 2 * grp + 2)
                    src = bank(6 + grp % 2)[:, 0:256]
                    if kind == "L":
                        dst = brT[:, 2, 2 * hg:2 * hg + 2, 0:S].rearrange("p f (r b q) -> p f r b q", r=ROWS, b=NB)[:, :, :, b, ::-1]
                        src = src.rearrange("p (f r q) -> p f r q", f=2, r=ROWS)
                    else:
                        dst = brT[:, 2, 2 * hg:2 * hg + 2, S + b * P:S + (b + 1) * P]
                        src = src.rearrange("p (f q) -> p f q", f=2)
                    V.tensor_copy(dst, src).then_inc(sem("a_fin"), 1)

                def maxima(n):
                    for q in range(2):
                        x = 2 * (n % 2) + q
                        sp_ = bank(x)
                        dve.wait_ge(sem("a_s"), l * PER["a_s"] + 2 * n + q + 1)
                        if steps[n][0] == "L":
                            if q == 0:
                                dve.wait_ge(sem("a_bm"), l * PER["a_bm"] + n + 1)
                            s3 = sp_[:, 0:256].rearrange("p (j k) -> p j k", j=ROWS)
                            link(V.tensor_tensor(s3, s3, bm[n % 2][:, q], ALU.add))
                            V.tensor_reduce(nmx[:, x:x + 1], sp_, AX.X, ALU.max, negate=True).then_inc(sem("a_max"), 1)
                        else:
                            V.tensor_reduce(nmx[:, x:x + 1], sp_[:, 256:512], AX.X, ALU.max, negate=True)\
                                .then_inc(sem("a_max"), 1)

                def scales(n):
                    x = 2 * (n % 2)
                    dve.wait_ge(sem("a_exp"), l * PER["a_exp"] + 2 * n + 2)
                    link(V.reciprocal(rrec[:, x:x + 2], rsum[:, x:x + 2]))
                    for q in range(2):
                        i = V.tensor_scalar(dg[n % 2][q], ident, rrec[:, x + q:x + q + 1], None, ALU.mult)
                    i.then_inc(sem("a_dg"), 1)
                maxima(0)
                maxima(1)
                scales(0)
                for n in range(len(steps)):
                    if n + 1 < len(steps):
                        scales(n + 1)
                    lo = 0 if steps[n][0] == "L" else 256
                    dve.wait_ge(sem("a_tr"), l * PER["a_tr"] + 2 * n + 2)
                    if n:
                        dve.wait_ge(sem("a_pv"), l * PER["a_pv"] + n)
                    V.tensor_copy(prT[1][:, lo:512], bank(5)[:, lo:512]).then_inc(sem("a_pT1"), 1)
                    if n % 2 == 0 and n:
                        fin(n // 2 - 1)
                    if n + 2 < len(steps):
                        maxima(n + 2)
                fin(len(steps) // 2 - 1)
                phase_end(dve, ph + 8)

                V.memset(pu[:, :, 0:LCOL], 0.0)
                V.memset(pu[:, :, LCOL + S:CCOL], 0.0)
                if first:
                    V.memset(pu[:, :, CCOL + CTX:PADW], 0.0)
                else:
                    V.memset(pu[:, :, CCOL:PADW], 0.0)
                dve.drain()
                for n, gi in enumerate(POOL_ORDER):
                    w = WINDOWS[gi]
                    dve.wait_ge(sem("pu"), l * PER["pu"] + n + 1)
                    src, dst, step = pu, pA, 1
                    while step < w:
                        link(V.tensor_tensor(dst[:, gi, 0:PADW + 1 - 2 * step], src[:, gi, 0:PADW + 1 - 2 * step],
                                             src[:, gi, step:PADW + 1 - step], ALU.add))
                        src, dst, step = dst, (pB, pA)[dst is pB], 2 * step
                    for _, base, cnt in [(0, LCOL, S)] + ([(1, CCOL, CTX)] if first else []):
                        for side, p0 in enumerate((base, base + cnt - 8)):
                            e0 = CED + gi * 16 + side * 8
                            lo = p0 - w // 2
                            V.tensor_tensor(src[:, gi, lo:lo + 8], src[:, gi, lo:lo + 8], cst[:, e0:e0 + 8], ALU.mult)
                    dve.drain()
                    for _, base, t0, cnt in [(0, LCOL, 0, S)] + ([(1, CCOL, S, CTX)] if first else []):
                        lo = base - w // 2
                        i = V.scalar_tensor_tensor(pin[:, gi, t0:t0 + cnt], src[:, gi, lo:lo + cnt], 1.0 / w,
                                                   pu[:, gi, base:base + cnt], ALU.mult, ALU.subtract)
                    i.then_inc(sem("pin"), 1)
                phase_end(dve, ph + 9)

                dve.drain().then_inc(sem("mg_free"), 2)
                with dve.Fori(0, 3) as bi:
                    for f in range(KD):
                        dve.wait_ge(sem("mg_sg"), l * PER["mg_sg"] + bi * KD + (f + 1))
                        dve.wait_ge(sem("mg_tfree"), l * PER["mg_tfree"] + bi * KD + (f + 1))
                        V.tensor_tensor(mtmp[f % 2][:, 0:TW(l)], sg[f % 2][:, 0:TW(l)], PS[(f % 2) * 2][:, 0:TW(l)],
                                        ALU.mult).then_inc(sem("mg_free"), 1)
                phase_end(dve, ph + 10)

                dve.drain().then_inc(sem("y_free"), 2)
                dve.wait_ge(sem("growS0"), l + 1)
                dve.wait_ge(sem("x_back"), l * PER["x_back"] + 16 * len(streams(l)))
                for t in range(nt(l)):
                    dve.wait_ge(sem("yss"), l * PER["yss"] + t + 1)
                    link(V.reciprocal(rstd[:, t:t + 1], ss[:, t:t + 1]))
                    link(V.scalar_tensor_tensor(ytmp[t % 2], PS[2 + t % 2][:, :], rstd[:, t:t + 1], grow[:, t // LT, :],
                                                ALU.mult, ALU.mult))
                    V.tensor_tensor(x_sb[:, t, :], x_sb[:, t, :], ytmp[t % 2], ALU.add).then_inc(sem("y_free"), 1)
                phase_end(dve, ph + 11)

                norm_cols("n2", nt(l), h2T, 1)
                n_t = nt(l)
                dve.wait_ge(sem("logit"), l * PER["logit"] + 1)
                lg = bank(0)[:, 0:n_t * NE].rearrange("p (t e) -> p t e", t=n_t)
                link(V.tensor_reduce(asum[:, 0:n_t], lg, AX.X, ALU.max))
                V.tensor_tensor(aexp[:, 0:n_t], lg, asum[:, 0:n_t].unsqueeze(2).to_broadcast([P, n_t, NE]), ALU.subtract)\
                    .then_inc(sem("asub"), 1)
                dve.wait_ge(sem("aexp"), l * PER["aexp"] + 1)
                link(V.tensor_reduce(asum[:, 0:n_t], aexp[:, 0:n_t], AX.X, ALU.add))
                link(V.reciprocal(arec[:, 0:n_t], asum[:, 0:n_t]))
                V.tensor_tensor(affn[:, 0:n_t], aexp[:, 0:n_t], arec[:, 0:n_t].unsqueeze(2).to_broadcast([P, n_t, NE]),
                                ALU.mult).then_inc(sem("aff"), 1)
                dve.wait_ge(sem("afftr"), l * PER["afftr"] + 1)
                link(V.tensor_copy(affT[:, 0:TW(l)], PS[1][0:NE, 0:TW(l)]))
                for s, t0, cnt in streams(l):
                    rows = affT[:, t0:t0 + cnt]
                    for j in range(cnt // 64):
                        o8 = s * 64 + 8 * j
                        link(V.max(tv[:, o8:o8 + 8], rows))
                        V.max_index(ti[:, o8:o8 + 8], tv[:, o8:o8 + 8], rows)
                        dve.drain()
                        if j < cnt // 64 - 1:
                            link(V.match_replace(rows, tv[:, o8:o8 + 8], rows, -1.0))
                link(V.tensor_copy(tif[:, 0:nslot[l]], ti[:, 0:nslot[l]]))
                if first:
                    link(V.tensor_scalar(tif[:, 64:96], tif[:, 64:96], float(S), None, ALU.add))
                for g, (s, c0, M, G, _) in enumerate(SETS[l]):
                    wv = twide.rearrange("p x g (j m) -> p x g j m", m=M)
                    V.tensor_copy(wv[:, 0, g], tv[:, c0:c0 + M].unsqueeze(1).to_broadcast([NE, G, M]))
                    for j in range(G):
                        i = V.tensor_scalar(wv[:, 1, g, j], tif[:, c0:c0 + M], float(G), float(j), ALU.mult, ALU.add)
                link(i)
                dve.sem_inc(sem("top"), 1)
                dve.wait_ge(sem("toptr"), l * PER["toptr"] + 1)
                ns = nslot[l]
                V.tensor_copy(gidx[0:ns, 0:NE], bank(1)[0:ns, 0:NE])
                V.tensor_copy(gidx[0:ns, NE:NE + 2], bank(1)[0:ns, 0:2])
                for g in range(len(SETS[l])):
                    V.tensor_copy(gval[:, g, :], bank(1)[:, 16 + g * NE:16 + (g + 1) * NE])
                    i = V.tensor_copy(sidx[:, g, :], bank(1)[:, 48 + g * NE:48 + (g + 1) * NE])
                link(i)
                link(V.tensor_copy(icur[0:ns, :], gidx[0:ns, 0:1]))
                phase_end(dve, ph + 12)

                def modulate(tag_e):
                    ps = PS[0][:, :].rearrange("p (k c) -> p k c", k=KD)
                    for s, c0, cw in [(0, 0, 64)] + ([(1, 64, 32)] if first else []):
                        V.tensor_tensor(xeT[:, :, c0:c0 + cw], ps[:, :, c0:c0 + cw],
                                        cA[1][:, :, s:s + 1].to_broadcast([P, KD, cw]), ALU.mult)
                    dve.drain()
                    for s, c0, cw in [(0, 0, 64)] + ([(1, 64, 32)] if first else []):
                        i = V.tensor_tensor(xeT[:, :, c0:c0 + cw], xeT[:, :, c0:c0 + cw],
                                            cS[1][:, :, s:s + 1].to_broadcast([P, KD, cw]), ALU.add)
                    i.then_inc(sem("xeT"), 1)
                dve.drain().then_inc(sem("hid"), 1)
                dve.wait_ge(sem("xe_T"), l * PER["xe_T"] + 1)
                V.tensor_copy(icur[0:ns, :], gidx[0:ns, 1:2]).then_inc(sem("icur"), 1)
                modulate(0)
                with dve.Fori(0, NE) as e:
                    dve.wait_ge(sem("ig_free"), l * PER["ig_free"] + e + 1)
                    ng = len(SETS[l])
                    V.tensor_copy(gcur[:, 0:ng], gval[:, 0:ng, bass.ds(e, 1)].rearrange("p g o -> p (g o)"))
                    V.tensor_copy(iprev[:, 0:ng], sidx[:, 0:ng, bass.ds(e, 1)].rearrange("p g o -> p (g o)"))\
                        .then_inc(sem("iprev"), 1)
                    dve.wait_ge(sem("unit_done"), l * PER["unit_done"] + 6 * e + 4)
                    dve.wait_ge(sem("gsil"), l * PER["gsil"] + e + 1)
                    i = V.tensor_tensor(hidm[:, 0:512], gsil[:, 0:512], bank(3), ALU.mult)
                    if first:
                        i = V.tensor_tensor(hidm[:, 512:768], gsil[:, 512:768], bank(5)[:, 0:256], ALU.mult)
                    i.then_inc(sem("hid"), 1)
                    if first:
                        dve.wait_ge(sem("hid_T"), e + 1)
                        V.tensor_copy(hidC.rearrange("p b g m -> p (b g m)"), bank(7)[:, 0:256]).then_inc(sem("hidC"), 1)
                    dve.wait_ge(sem("xe_T"), l * PER["xe_T"] + e + 2)
                    V.tensor_copy(icur[0:ns, :], gidx[0:ns, bass.ds(e + 2, 1)]).then_inc(sem("icur"), 1)
                    modulate(e)
                phase_end(dve, ph + 13)

                dve.wait_ge(sem("growS1"), l + 1)
                for t in range(n_t):
                    dve.wait_ge(sem("n3_ss"), l * PER["n3_ss"] + t + 1)
                    link(V.reciprocal(rstd[:, t:t + 1], ss[:, t:t + 1]))
                    link(V.scalar_tensor_tensor(xn[:, t, :], xn[:, t, :], rstd[:, t:t + 1], grow[:, t // LT, :],
                                                ALU.mult, ALU.mult))
                    V.tensor_tensor(x_sb[:, t, :], x_sb[:, t, :], xn[:, t, :], ALU.add).then_inc(sem("x_tile"), 1)

        @block.gpsimd
        def _(pool):
            G = nc.gpsimd

            def split(l, h):
                slot = units[(l,) + SPLITS[h]][1]
                if h < 2:
                    pool.wait_ge(w_ready(slot), 16 * units[(l,) + SPLITS[h]][2])
                    G.tensor_copy(unit_hi(slot, ring_r), unit_lo(slot)).then_inc(sem("p_hi"), 1)
                    pool.wait_ge(sem("p_hi"), 2 * l + h + 1)
                else:
                    pool.wait_ge(sem("w_hi"), l * (NSP - 2) + h - 1)
                G.tensor_tensor(unit_lo(slot, ring_r), unit_lo(slot), unit_hi(slot, ring_r).bitcast(F32), ALU.subtract)\
                    .then_inc(sem("w_lo"), 1)
            pool.wait_ge(sem("const_in"), 16)
            for l in range(DEPTH):
                ph = NPH * l
                first = l == 0
                if not first:
                    pool.wait_ge(sem("x_tile"), NT)
                phase_end(pool, ph + 1)
                split(l, 0)
                phase_end(pool, ph + 2)
                for h in range(1, 4):
                    split(l, h)
                phase_end(pool, ph + 3)
                if not first:
                    split(l, 4)
                    split(l, 5)
                phase_end(pool, ph + 4)
                for st in range(5):
                    for r in range(2):
                        c = (FW, BWD)[r][st]
                        if 2 * st + r:
                            pool.wait_ge(sem("m_kv"), l * PER["m_kv"] + 2 * st + r)
                        G.tensor_tensor(vws, v_ext[:, c], xp1[:, r, c, :].unsqueeze(2).to_broadcast([P, MH, 129]), ALU.mult)\
                            .then_inc(sem("m_vw"), 1)
                if first:
                    split(l, 4)
                    split(l, 5)
                phase_end(pool, ph + 5)
                split(l, 6)
                split(l, 7)
                phase_end(pool, ph + 6)
                for h in range(8, 13):
                    split(l, h)
                for t in range(LT):
                    pool.wait_ge(sem("np_out"), l * PER["np_out"] + 2 * KB + t + 1)
                    pool.dma_start(v_dram[l][t * P:(t + 1) * P, :], vstage[t % 2]).then_inc(sem(f"v_out{t % 2}_{l}"), 16)
                split(l, 13)
                phase_end(pool, ph + 7)

                for n, (kind, hg, b, f) in enumerate(att_steps(l)):
                    if kind != "L":
                        continue
                    if n % 8 == 0:
                        pool.wait_ge(sem("tab_in"), l * PER["tab_in"] + 128 * (hg + 1))
                    if n >= 2:
                        pool.wait_ge(sem("a_max"), l * PER["a_max"] + 2 * (n - 1))
                    off = KSTART[b] - QC * b + 16
                    h4 = 2 * (n % 2)
                    for q in range(2):
                        t3 = tab[:, h4 + q, :].rearrange("p (j w) -> p j w", j=ROWS)[:, :, off:off + KC]
                        i = G.tensor_tensor(bm[n % 2][:, q], t3, cst[:, CNM + b * KC:CNM + (b + 1) * KC].unsqueeze(1)
                                            .to_broadcast([P, ROWS, KC]), ALU.add)
                    i.then_inc(sem("a_bm"), 1)
                phase_end(pool, ph + 8)
                pool.dma_start(pw, A["pool_w"][l].rearrange("g p n -> p g n")).then_inc(sem("pw_in"), 16)
                split(l, 14)
                phase_end(pool, ph + 9)
                G.memset(acc[:, :, 0:TW(l)], 0.0)
                pool.drain().then_inc(sem("mg_tfree"), 2)
                for bi in range(3):
                    for f in range(KD):
                        if f % 2 == 0 and bi * 4 + f // 2 < 11:
                            split(l, 15 + bi * 4 + f // 2)
                        pool.wait_ge(sem("mg_free"), l * PER["mg_free"] + bi * KD + (f + 3))
                        G.tensor_tensor(acc[:, f, 0:TW(l)], acc[:, f, 0:TW(l)], mtmp[f % 2][:, 0:TW(l)], ALU.add)\
                            .then_inc(sem("mg_tfree"), 1)
                for n in range(10, 12):
                    phase_end(pool, ph + n)
                pool.wait_ge(sem(f"n2_xn{l}"), nt(l))
                pool.dma_start(xn_dram[l][0:TW(l), :].rearrange("(t p) d -> p t d", p=P), xn[:, 0:nt(l), :])\
                    .then_inc(sem("xn_out"), 16)
                phase_end(pool, ph + 12)
                ns = nslot[l]
                pool.wait_ge(sem("xn_out"), l * PER["xn_out"] + 16)
                pool.wait_ge(sem("zero_out"), 16 * NT * (l + 1))

                def gather():
                    G.indirect_dma_start(xe[0:ns, :], None, xn_dram[l][0:TW(l), :],
                                         bass.IndirectOffsetOnAxis(ap=icur[0:ns, 0:1], axis=0)).then_inc(sem("xe_in"), 16)
                gather()
                pool.drain().then_inc(sem("ig_free"), 1)
                pool.wait_ge(sem("icur"), l * PER["icur"] + 1)
                gather()
                with pool.Fori(0, NE) as e:
                    pool.wait_ge(sem("icur"), l * PER["icur"] + e + 2)
                    pool.sem_inc(sem("pool_turn"), 1)
                    gather()
                    pool.wait_ge(sem("iprev"), l * PER["iprev"] + e + 1)
                    pool.wait_ge(sem("ytm"), l * PER["ytm"] + e + 2)
                    pool.sem_inc(sem("pool_turn"), 1)
                    nset = len(SETS[l])
                    for g, (_, _, M, parts, c) in enumerate(SETS[l]):
                        W = D // parts
                        G.indirect_dma_start(moe_dram[l][0:TW(l), :].rearrange("t (j n) -> (t j) n", n=W),
                                             bass.IndirectOffsetOnAxis(ap=iprev[:, g:g + 1], axis=0),
                                             ytm[:, c:c + W], None, compute_op=ALU.add).then_inc(sem("y_added"), 16)
                    pool.wait_ge(sem("y_added"), l * PER["y_added"] + 16 * nset * e + 16 * nset)
                    pool.sem_inc(sem("ig_free"), 1)
                pool.wait_ge(sem("xe_in"), (l + 1) * PER["xe_in"])
                phase_end(pool, ph + 13)

        @block.sync
        def _(sp):
            last = [None] * 6

            def load(key):
                src, slot, count, _, _ = units[key]
                if last[slot]:
                    sp.wait_ge(sem(last[slot][0]), last[slot][1])
                nk = src.shape[1]
                dst = slot_ap(slot)[:, 0:nk * src.shape[2]]
                sp.dma_start(dst.rearrange("p (k n) -> p k n", k=nk), src).then_inc(w_ready(slot), 16)
                last[slot] = released[key]

            sp.dma_start(cst[:, :], A["tables"]).then_inc(sem("const_in"), 16)
            for l in range(DEPTH):
                rows = ((0, 8, A["c"][0].rearrange("(k p) -> k p", p=P)),
                        (8, 16, A["c_ctx"].rearrange("(k p) -> k p", p=P)),
                        (16, 48, A["norm_gain"][l].rearrange("g (k p) -> (g k) p", p=P)),
                        (48, 96, A["ada_b"][l].rearrange("(k p) -> k p", p=P)),
                        (96, 100, A["pool_scale"][l].rearrange("(k p) -> k p", p=P)))
                for r0, r1, src in rows:
                    sp.dma_start(stage[l][r0:r1, :], src).then_inc(sem("stage_in"), 16)
            for l in range(DEPTH):
                def load_tables(hg):
                    for r in range(ROWS):
                        src = A["rpb"]
                        src = bass.AP(src.tensor, src.offset + (l * NH + hg * 4) * 15 * RPW + (7 - r) * RPW,
                                      [[1, QC], [15 * RPW, 4], [1, 496]])
                        sp.dma_start(tab[r * QC:(r + 1) * QC, :, 0:496], src).then_inc(sem("tab_in"), 16)

                def load_values(grp):
                    b = grp % NB
                    if grp >= 2:
                        sp.wait_ge(sem("a_pv"), l * PER["a_pv"] + 2 * (grp - 1))
                    rows = v_dram[l].rearrange("(j c) n -> j c n", c=GW)
                    for j in range(ROWS):
                        sp.dma_start(vw[grp % 2][(j % 4) * KC:(j % 4 + 1) * KC, j // 4, :],
                                     rows[j, KSTART[b]:KSTART[b] + KC, :]).then_inc(sem(f"vw_in{grp % 2}_{l}"), 16)
                def load_branch(b, half):
                    sp.dma_start(mg_wb[half], wbr[l, b, :, 512 * half:512 * half + 512].rearrange("(k p) n -> p k n", p=P))\
                        .then_inc(sem(f"mg_in{half}"), 16)

                def load_vectors():
                    sp.wait_ge(sem("pads_set"), 1)
                    sp.dma_start(gw[:, :, 0:16], w_in[l][:, C_G:C_G + 16].rearrange("(k p) n -> p k n", p=P)).then_inc(sem("gw_in"), 16)
                    sp.dma_start(rw[:, :, 0:NE], A["router_w"][l].rearrange("(k p) n -> p k n", p=P)).then_inc(sem("gw_in"), 16)
                    sp.dma_start(gbias, A["mlstm_gate_bias"][l].rearrange("(o g) h -> o (g h)", o=1).to_broadcast([P, 16]))\
                        .then_inc(sem("gw_in"), 16)

                for key in [k_ for k_ in units if k_[0] == l and k_[1] not in ("bg", "wout")]:
                    load(key)
                    if key[1:] == ("ada", 0, 2):
                        sp.dma_start(x_sb[:, 0:LT, :], A["x"][0].rearrange("(t p) d -> p t d", p=P)).then_inc(sem("x_in"), 16)
                        sp.dma_start(x_sb[:, LT:NT, :], A["ctx"][0].rearrange("(t p) d -> p t d", p=P)).then_inc(sem("x_in"), 16)
                    if key[1:] == ("qk", 0):
                        load_vectors()
                    if key[1:] == ("vn", 0):
                        for t in range(NT):
                            sp.dma_start(moe_dram[l][t * P:(t + 1) * P, :], A["zeros"]).then_inc(sem("zero_out"), 16)
                        sp.wait_ge(sem("phase"), 4 * (NPH * l + 6))
                        load_tables(0)
                for q in range(12):
                    released[l, "bg", q] = ("mg_mm", l * PER["mg_mm"] + 2 * q + 2)
                load((l, "bg", 0))
                for i in range(2):
                    sp.wait_ge(sem(f"v_out{i}_{l}"), 32)
                for grp in range(2 * NB):
                    if grp == NB:
                        sp.wait_ge(sem("a_bm"), l * PER["a_bm"] + 2 * NB)
                        load_tables(1)
                    load_values(grp)
                sp.wait_ge(sem(last[0][0]), last[0][1])
                load_branch(0, 0)
                load_branch(0, 1)
                for q in range(1, 12):
                    load((l, "bg", q))
                    if q % 2 == 1 and 3 <= q < 11:
                        b, half = (q - 3) // 4, (q - 3) // 2 % 2
                        sp.wait_ge(sem("mg_mm"), l * PER["mg_mm"] + b * KD + 4 * half + 4)
                        load_branch(b + 1, half)
                load((l, "wout", 0))
                last[0] = last[1]
                load((l, "wout", 1))
                sp.wait_ge(sem("phase"), 4 * (NPH * l + 10))
                for s, t0, t1 in [(0, 0, LT), (1, LT, NT)][:len(streams(l))]:
                    src = (A["x"][0], A["ctx"][0])[s] if l == 0 else x_dram[l]
                    sp.dma_start(x_sb[:, t0:t1, :], src.rearrange("(t p) d -> p t d", p=P)).then_inc(sem("x_back"), 16)

                exp_src = [(A["w_gate"], 0), (A["w_gate"], 512), (A["w_up"], 0), (A["w_up"], 512),
                           (A["w_down"], 0), (A["w_down"], 512)]

                def expert_unit(e, s):
                    w, c = exp_src[s]
                    sp.dma_start(slot_ap(s).rearrange("p (k n) -> p k n", k=4),
                                 w[l][bass.ds(e, 1), c:c + 512, :].rearrange("o (k p) n -> p (o k) n", p=P))\
                        .then_inc(w_ready(s), 16)
                for s in range(6):
                    if s < 3:
                        sp.wait_ge(sem(last[s][0]), last[s][1])
                    elif s == 3:
                        sp.wait_ge(sem("phase"), 4 * (NPH * l + 10))
                    expert_unit(0, s)
                with sp.Fori(1, NE) as e:
                    for s in range(6):
                        sp.wait_ge(sem("unit_done"), l * PER["unit_done"] + 6 * e + (s - 5))
                        sp.sem_inc(sem("sp_turn"), 1)
                        s2, back = (s - 2) % 6, 1 if s < 2 else 0
                        sp.wait_ge(w_ready(s2), 16 * e + 16 * (moe_base[l][s2] + 1 - back))
                        sp.sem_inc(sem("sp_turn"), 1)
                        expert_unit(e, s)
                sp.wait_ge(sem("y_added"), l * PER["y_added"] + 16 * len(SETS[l]) * NE)
                for t in range(nt(l)):
                    sp.dma_start(xn[:, t, :], moe_dram[l][t * P:(t + 1) * P, :]).then_inc(sem(f"moe_in{t}"), 16)
                if l + 1 < DEPTH:
                    sp.wait_ge(sem("x_tile"), l * PER["x_tile"] + NT)
                    sp.dma_start(x_dram[l + 1].rearrange("(t p) d -> p t d", p=P), x_sb[:, 0:LT, :]).then_inc(sem("x_out"), 16)
                for s in range(6):
                    last[s] = ("unit_done", l * PER["unit_done"] + 6 * NE - 5 + s)
            for t in range(LT):
                sp.wait_ge(sem("x_tile"), (DEPTH - 1) * PER["x_tile"] + t + 1)
                sp.dma_start(out[0, t * P:(t + 1) * P, :], x_sb[:, t, :]).then_inc(sem("out"), 16)
            sp.wait_ge(sem("out"), 16 * LT)


_INS = ["x", "c", "ctx", "c_ctx", "norm_gain", "ada_w", "ada_b", "w_in", "mlstm_gate_bias", "pool_w", "pool_scale",
        "w_branch", "w_out", "router_w", "w_gate", "w_up", "w_down"]


def kernel(**inputs):
    import numpy as np
    import concourse.bacc as bacc
    from concourse.bass_utils import run_bass_kernel_spmd

    nc = bacc.Bacc("TRN2", target_bir_lowering=False, num_devices=1)
    arrays = {n: np.ascontiguousarray(inputs[n]) for n in _INS}
    rpb = np.asarray(inputs["na_rpb"])
    wide = np.zeros(rpb.shape[:3] + (RPW,), rpb.dtype)
    wide[..., 16:16 + rpb.shape[3]] = rpb
    arrays["rpb"] = wide
    arrays["tables"] = constants()
    arrays["zeros"] = np.zeros((P, D), np.float32)
    args = {n: nc.dram_tensor(f"in_{n}", a.shape, F32, kind="ExternalInput").ap() for n, a in arrays.items()}
    out = nc.dram_tensor("out_0_dram", (1, S, D), F32, kind="ExternalOutput").ap()
    build(nc, args, out)
    r = run_bass_kernel_spmd(nc, [{f"in_{n}": a for n, a in arrays.items()}], core_ids=[0])
    return r.results[0]["out_0_dram"]
```
